# Optimizing a Trainium2 kernel written in Bass

```python
import jax, jax.numpy as jnp
from jax import lax
import numpy as np
import math

D_MODEL = 2048
BATCH = 1
SEQ = 256
DEPTH = 1

CHUNK = 64
Q_BLOCK = 128
N_BRANCH = 3
D_RNN = D_MODEL // 2
N_RNN_BLOCKS = 8
RNN_BLOCK = D_RNN // N_RNN_BLOCKS
CONV_WIDTH = 4
LRU_C = 8.0
N_HEADS = 8
HEAD_DIM = 128
D_ATTN = N_HEADS * HEAD_DIM
D_POOL = D_MODEL // 2
POOL_WINDOWS = (2, 4, 8, 16)
N_POOL_GROUPS = 4
POOL_GROUP = D_POOL // N_POOL_GROUPS
D_FF = ((-(-8 * D_MODEL // 3) + 255) // 256) * 256
NORM_EPS = 1e-6
IN_SIZES = (D_RNN, D_RNN, D_ATTN, D_ATTN, D_ATTN, N_HEADS, D_POOL, N_BRANCH * D_MODEL)
D_IN = D_RNN * 2 + D_ATTN * 3 + N_HEADS + D_POOL + N_BRANCH * D_MODEL


def rms_norm(x, g):
    xf = x.astype(jnp.float32)
    y = xf * lax.rsqrt(jnp.mean(xf * xf, axis=-1, keepdims=True) + NORM_EPS)
    return (y * g.astype(jnp.float32)).astype(x.dtype)

def split_columns(p):
    offsets = []
    acc = 0
    for s in IN_SIZES[:-1]:
        acc += s
        offsets.append(acc)
    return jnp.split(p, offsets, axis=-1)

def causal_depthwise_conv(u, w, b):
    S = u.shape[1]
    up = jnp.pad(u, ((0, 0), (CONV_WIDTH - 1, 0), (0, 0)))
    out = b + up[:, 0:S] * w[0]
    for k in range(1, CONV_WIDTH):
        out = out + up[:, k:k + S] * w[k]
    return out

def rg_lru(u, w_r, b_r, w_i, b_i, lam):
    B, S, _ = u.shape
    ub = u.reshape(B, S, N_RNN_BLOCKS, RNN_BLOCK)
    r = jax.nn.sigmoid(jnp.einsum('bsnc,ncd->bsnd', ub, w_r).reshape(B, S, D_RNN) + b_r)
    i = jax.nn.sigmoid(jnp.einsum('bsnc,ncd->bsnd', ub, w_i).reshape(B, S, D_RNN) + b_i)
    log_a = (LRU_C * r.astype(jnp.float32)) * jax.nn.log_sigmoid(lam.astype(jnp.float32))
    a = jnp.exp(log_a)
    b_in = jnp.sqrt(-jnp.expm1(2.0 * log_a)) * (i * u).astype(jnp.float32)

    def combine(left, right):
        a1, b1 = left
        a2, b2 = right
        return a1 * a2, a2 * b1 + b2

    _, h = lax.associative_scan(combine, (a, b_in), axis=1)
    return h.astype(u.dtype)

def forgetting_attention(q, k, v, f_logit):
    B, S, H, Dh = q.shape
    nb = S // Q_BLOCK
    scale = Dh ** -0.5
    F = jnp.cumsum(jax.nn.log_sigmoid(f_logit.astype(jnp.float32)), axis=1).transpose(0, 2, 1)
    k_h = k.transpose(0, 2, 1, 3)
    v_h = v.transpose(0, 2, 1, 3)
    q_blocks = q.reshape(B, nb, Q_BLOCK, H, Dh).transpose(1, 0, 3, 2, 4)
    F_blocks = F.reshape(B, H, nb, Q_BLOCK).transpose(2, 0, 1, 3)
    k_pos = jnp.arange(S)

    def one_block(args):
        qb, Fq, blk = args
        s = jnp.einsum('bhqd,bhkd->bhqk', qb, k_h, preferred_element_type=jnp.float32) * scale
        s = s + Fq[..., None] - F[:, :, None, :]
        q_pos = blk * Q_BLOCK + jnp.arange(Q_BLOCK)
        s = jnp.where(q_pos[:, None] >= k_pos[None, :], s, -jnp.inf)
        p = jax.nn.softmax(s, axis=-1)
        return jnp.einsum('bhqk,bhkd->bhqd', p.astype(v_h.dtype), v_h)

    o = lax.map(one_block, (q_blocks, F_blocks, jnp.arange(nb)))
    return o.transpose(1, 0, 3, 2, 4).reshape(B, S, H * Dh)

def multiscale_pool(u, w_pool, scale):
    B, S, _ = u.shape
    uf = u.astype(jnp.float32).reshape(B, S, N_POOL_GROUPS, POOL_GROUP)
    cs = jnp.cumsum(uf, axis=1)
    t = jnp.arange(1, S + 1, dtype=jnp.float32)
    outs = []
    for g, w in enumerate(POOL_WINDOWS):
        c = cs[:, :, g]
        lagged = jnp.pad(c, ((0, 0), (w, 0), (0, 0)))[:, :S]
        cnt = jnp.minimum(t, w)[None, :, None]
        outs.append((c - lagged) / cnt - uf[:, :, g])
    pooled = jnp.stack(outs, axis=2).astype(u.dtype)
    y = jnp.einsum('bsgc,gcd->bsgd', pooled, w_pool).reshape(B, S, D_POOL)
    return y * scale

def hybrid_layer(x, g_mix, w_in, b_forget, conv_w, conv_b, w_rg, b_rg, w_ig, b_ig, lru_lambda,
                 w_pool, pool_scale, w_branch_rnn, w_branch_attn, w_branch_pool, w_out,
                 g_ffn, w_ffn_in, w_ffn_out):
    B, S, _ = x.shape
    h = rms_norm(x, g_mix)
    rnn_x, rnn_y, q, k, v, f_logit, pool_in, gate_logits = split_columns(h @ w_in)
    u = causal_depthwise_conv(rnn_x, conv_w, conv_b)
    y_a = jax.nn.gelu(rnn_y) * rg_lru(u, w_rg, b_rg, w_ig, b_ig, lru_lambda)
    y_b = forgetting_attention(q.reshape(B, S, N_HEADS, HEAD_DIM),
                               k.reshape(B, S, N_HEADS, HEAD_DIM),
                               v.reshape(B, S, N_HEADS, HEAD_DIM),
                               f_logit + b_forget)
    y_c = multiscale_pool(pool_in, w_pool, pool_scale)
    gates = jax.nn.sigmoid(gate_logits.astype(jnp.float32)).astype(x.dtype).reshape(B, S, N_BRANCH, D_MODEL)
    merged = (gates[:, :, 0] * (y_a @ w_branch_rnn)
              + gates[:, :, 1] * (y_b @ w_branch_attn)
              + gates[:, :, 2] * (y_c @ w_branch_pool))
    x = x + merged @ w_out
    h2 = rms_norm(x, g_ffn)
    gate, up = jnp.split(h2 @ w_ffn_in, 2, axis=-1)
    return x + (jax.nn.silu(gate) * up) @ w_ffn_out

def first_inputs(seed: int = 0) -> dict:
    key = jax.random.key(seed)
    ks = jax.random.split(key, 24)
    f32 = jnp.float32
    nrm = lambda k, shape, s: jax.random.normal(k, shape, f32) * s
    a8 = jax.random.uniform(ks[10], (DEPTH, D_RNN), f32, 0.9, 0.999)
    a = a8 ** (1.0 / LRU_C)
    lru_lambda = jnp.log(a) - jnp.log1p(-a)
    return {
        "x": jax.random.normal(ks[0], (BATCH, SEQ, D_MODEL), f32),
        "g_mix": 1.0 + nrm(ks[1], (DEPTH, D_MODEL), 0.05),
        "w_in": nrm(ks[2], (DEPTH, D_MODEL, D_IN), D_MODEL ** -0.5),
        "b_forget": jax.random.uniform(ks[3], (DEPTH, N_HEADS), f32, 1.0, 4.0),
        "conv_w": nrm(ks[4], (DEPTH, CONV_WIDTH, D_RNN), CONV_WIDTH ** -0.5),
        "conv_b": nrm(ks[5], (DEPTH, D_RNN), 0.02),
        "w_rg": nrm(ks[6], (DEPTH, N_RNN_BLOCKS, RNN_BLOCK, RNN_BLOCK), RNN_BLOCK ** -0.5),
        "b_rg": nrm(ks[7], (DEPTH, D_RNN), 0.02),
        "w_ig": nrm(ks[8], (DEPTH, N_RNN_BLOCKS, RNN_BLOCK, RNN_BLOCK), RNN_BLOCK ** -0.5),
        "b_ig": nrm(ks[9], (DEPTH, D_RNN), 0.02),
        "lru_lambda": lru_lambda,
        "w_pool": nrm(ks[11], (DEPTH, N_POOL_GROUPS, POOL_GROUP, POOL_GROUP), POOL_GROUP ** -0.5),
        "pool_scale": 1.0 + nrm(ks[12], (DEPTH, D_POOL), 0.1),
        "w_branch_rnn": nrm(ks[13], (DEPTH, D_RNN, D_MODEL), D_RNN ** -0.5),
        "w_branch_attn": nrm(ks[14], (DEPTH, D_ATTN, D_MODEL), D_ATTN ** -0.5),
        "w_branch_pool": nrm(ks[15], (DEPTH, D_POOL, D_MODEL), D_POOL ** -0.5),
        "w_out": nrm(ks[16], (DEPTH, D_MODEL, D_MODEL), D_MODEL ** -0.5),
        "g_ffn": 1.0 + nrm(ks[17], (DEPTH, D_MODEL), 0.05),
        "w_ffn_in": nrm(ks[18], (DEPTH, D_MODEL, 2 * D_FF), D_MODEL ** -0.5),
        "w_ffn_out": nrm(ks[19], (DEPTH, D_FF, D_MODEL), D_FF ** -0.5),
        "g_final": 1.0 + nrm(ks[20], (D_MODEL,), 0.05),
    }

def first_block(x, g_mix, w_in, b_forget, conv_w, conv_b, w_rg, b_rg, w_ig, b_ig, lru_lambda,
              w_pool, pool_scale, w_branch_rnn, w_branch_attn, w_branch_pool, w_out,
              g_ffn, w_ffn_in, w_ffn_out, g_final):
    for l in range(DEPTH):
        x = hybrid_layer(x, g_mix[l], w_in[l], b_forget[l], conv_w[l], conv_b[l], w_rg[l], b_rg[l],
                         w_ig[l], b_ig[l], lru_lambda[l], w_pool[l], pool_scale[l],
                         w_branch_rnn[l], w_branch_attn[l], w_branch_pool[l], w_out[l],
                         g_ffn[l], w_ffn_in[l], w_ffn_out[l])
    return rms_norm(x, g_final)


MIX_DIM = D_MODEL
RWKV_HEAD = 64
RWKV_DIM = MIX_DIM // 2
RWKV_HEADS = RWKV_DIM // RWKV_HEAD
RWKV_DECAY_LORA = max(32, int(round(1.8 * RWKV_DIM ** 0.5 / 32)) * 32)
RWKV_AAA_LORA = max(32, int(round(1.8 * RWKV_DIM ** 0.5 / 32)) * 32)
RWKV_MV_LORA = max(32, int(round(0.6 * RWKV_DIM ** 0.5 / 32)) * 32)
RWKV_GATE_LORA = max(32, int(round(0.6 * RWKV_DIM ** 0.8 / 32)) * 32)
RWKV_GN_EPS = RWKV_HEAD * 1e-5
RWKV_L2_EPS = 1e-12

GDN_HEAD = 128
GDN_V_DIM = MIX_DIM - RWKV_DIM
GDN_V_HEADS = GDN_V_DIM // GDN_HEAD
GDN_QK_HEADS = GDN_V_HEADS // 2
GDN_QK_DIM = GDN_QK_HEADS * GDN_HEAD
GDN_CONV = 4
GDN_CHUNK = 64
GDN_L2_EPS = 1e-6
GDN_NORM_EPS = 1e-6

D_FF_2 = -(-8 * D_MODEL // (3 * 256)) * 256
NORM_EPS_2 = 1e-5

N_RWKV_IN = 3 * RWKV_DIM + RWKV_DECAY_LORA + RWKV_AAA_LORA + RWKV_GATE_LORA
N_GDN_IN = 2 * GDN_QK_DIM + 2 * GDN_V_DIM + 2 * GDN_V_HEADS
N_IN = N_RWKV_IN + N_GDN_IN


def split_cols(p, sizes):
    offsets = np.cumsum(np.array(sizes))[:-1].tolist()
    return jnp.split(p, offsets, axis=-1)

def rms_norm_2(x, w, eps=NORM_EPS_2):
    x32 = x.astype(jnp.float32)
    y = x32 * lax.rsqrt(jnp.mean(x32 * x32, axis=-1, keepdims=True) + eps)
    return (y * w.astype(jnp.float32)).astype(x.dtype)

def l2_normalize(x, eps):
    x32 = x.astype(jnp.float32)
    return x32 * lax.rsqrt(jnp.sum(x32 * x32, axis=-1, keepdims=True) + eps)

def token_shift_lerp(p, mu):
    prev = jnp.pad(p, ((0, 0), (1, 0), (0, 0)))[:, :-1]
    return p + (prev - p) * mu

def causal_depthwise_conv_2(x, w):
    K, C = w.shape
    return lax.conv_general_dilated(
        x, w[:, None, :].astype(x.dtype), window_strides=(1,), padding=((K - 1, 0),),
        dimension_numbers=('NWC', 'WIO', 'NWC'), feature_group_count=C)

def rwkv7_recurrence(r, w, k, v, a, b):
    B, T, H, N = r.shape

    def step(S, inp):
        r_t, w_t, k_t, v_t, a_t, b_t = inp
        Sa = jnp.einsum('bhvk,bhk->bhv', S, a_t)
        S = S * w_t[:, :, None, :] + Sa[..., None] * b_t[:, :, None, :] + v_t[..., None] * k_t[:, :, None, :]
        return S, jnp.einsum('bhvk,bhk->bhv', S, r_t)

    xs = tuple(jnp.moveaxis(t, 1, 0) for t in (r, w, k, v, a, b))
    S0 = jnp.zeros((B, H, N, N), jnp.float32)
    _, y = lax.scan(step, S0, xs)
    return jnp.moveaxis(y, 0, 1)

def rwkv7_mixer(p, vres, v_first, mu, w0, w_up, a0, a_up, g_up, k_k, k_a, r_k, ln_w, ln_b):
    B, T, _ = p.shape
    H, N = RWKV_HEADS, RWKV_HEAD
    p = token_shift_lerp(p.astype(jnp.float32), mu)
    r, k, v, wd, ad, gd = split_cols(
        p, (RWKV_DIM, RWKV_DIM, RWKV_DIM, RWKV_DECAY_LORA, RWKV_AAA_LORA, RWKV_GATE_LORA))
    w = -jax.nn.softplus(-(w0 + jnp.tanh(wd) @ w_up)) - 0.5
    decay = jnp.exp(-jnp.exp(w))
    if vres is None:
        v_first = v
    else:
        vd, v_up, v0 = vres
        v = v + (v_first - v) * jax.nn.sigmoid(v0 + vd @ v_up)
    a = jax.nn.sigmoid(a0 + ad @ a_up)
    g = jax.nn.sigmoid(gd) @ g_up
    heads = lambda t: t.reshape(B, T, H, N)
    kk = l2_normalize(heads(k * k_k), RWKV_L2_EPS)
    k = k * (1.0 + (a - 1.0) * k_a)
    r, k, v, a, decay = map(heads, (r, k, v, a, decay))
    y = rwkv7_recurrence(r, decay, k, v, -kk, kk * a)
    mean = jnp.mean(y, axis=-1, keepdims=True)
    var = jnp.mean(jnp.square(y - mean), axis=-1, keepdims=True)
    y = ((y - mean) * lax.rsqrt(var + RWKV_GN_EPS)).reshape(B, T, RWKV_DIM) * ln_w + ln_b
    bonus = (jnp.sum(r * k * r_k, axis=-1, keepdims=True) * v).reshape(B, T, RWKV_DIM)
    return (y + bonus) * g, v_first

def gated_delta_rule_chunked(q, k, v, g, beta):
    B, T, H, dk = q.shape
    dv = v.shape[-1]
    C = GDN_CHUNK
    NC = T // C
    q = l2_normalize(q, GDN_L2_EPS) * (dk ** -0.5)
    k = l2_normalize(k, GDN_L2_EPS)

    def to_chunks(t):
        t = t.reshape((B, NC, C, H) + t.shape[3:])
        return jnp.moveaxis(t, 3, 1)

    q, k, v, g, beta = map(to_chunks, (q, k, v, g, beta))
    g = jnp.cumsum(g, axis=-1)
    idx = jnp.arange(C)
    causal = idx[:, None] >= idx[None, :]
    strict = idx[:, None] > idx[None, :]
    gamma = jnp.exp(jnp.where(causal, g[..., :, None] - g[..., None, :], -jnp.inf))
    k_beta = k * beta[..., None]
    v_beta = v * beta[..., None]
    L = jnp.where(strict, jnp.einsum('bhnid,bhnjd->bhnij', k_beta, k) * gamma, 0.0)
    eye = jnp.eye(C, dtype=L.dtype)
    rhs = jnp.concatenate([v_beta, k_beta * jnp.exp(g)[..., None]], axis=-1)
    sol = lax.linalg.triangular_solve(L + eye, rhs, left_side=True, lower=True, unit_diagonal=True)
    u, w = sol[..., :dv], sol[..., dv:]
    A_qk = jnp.einsum('bhnid,bhnjd->bhnij', q, k) * gamma
    q_g = q * jnp.exp(g)[..., None]
    g_last = g[..., -1]
    k_g = k * jnp.exp(g_last[..., None] - g)[..., None]

    def step(S, inp):
        u_i, w_i, qg_i, kg_i, A_i, gl_i = inp
        v_new = u_i - jnp.einsum('bhck,bhkv->bhcv', w_i, S)
        o = jnp.einsum('bhck,bhkv->bhcv', qg_i, S) + jnp.einsum('bhij,bhjv->bhiv', A_i, v_new)
        S = S * jnp.exp(gl_i)[..., None, None] + jnp.einsum('bhck,bhcv->bhkv', kg_i, v_new)
        return S, o

    xs = tuple(jnp.moveaxis(t, 2, 0) for t in (u, w, q_g, k_g, A_qk, g_last))
    S0 = jnp.zeros((B, H, dk, dv), jnp.float32)
    _, o = lax.scan(step, S0, xs)
    return o.transpose(1, 0, 3, 2, 4).reshape(B, T, H, dv)

def gdn_mixer(p, conv_w, A_log, dt_bias, norm_w):
    B, T, _ = p.shape
    p = p.astype(jnp.float32)
    qkv, z, a, b = split_cols(p, (2 * GDN_QK_DIM + GDN_V_DIM, GDN_V_DIM, GDN_V_HEADS, GDN_V_HEADS))
    qkv = jax.nn.silu(causal_depthwise_conv_2(qkv, conv_w.astype(jnp.float32)))
    q, k, v = split_cols(qkv, (GDN_QK_DIM, GDN_QK_DIM, GDN_V_DIM))
    rep = GDN_V_HEADS // GDN_QK_HEADS
    q = jnp.repeat(q.reshape(B, T, GDN_QK_HEADS, GDN_HEAD), rep, axis=2)
    k = jnp.repeat(k.reshape(B, T, GDN_QK_HEADS, GDN_HEAD), rep, axis=2)
    v = v.reshape(B, T, GDN_V_HEADS, GDN_HEAD)
    g = -jnp.exp(A_log) * jax.nn.softplus(a + dt_bias)
    beta = jax.nn.sigmoid(b)
    o = gated_delta_rule_chunked(q, k, v, g, beta)
    o = o * lax.rsqrt(jnp.mean(o * o, axis=-1, keepdims=True) + GDN_NORM_EPS) * norm_w
    o = o * jax.nn.silu(z.reshape(B, T, GDN_V_HEADS, GDN_HEAD))
    return o.reshape(B, T, GDN_V_DIM)

def second_inputs(seed: int = 0) -> dict:
    key = jax.random.key(seed)
    ks = iter(jax.random.split(key, 40))
    L, D, Lv = DEPTH, D_MODEL, DEPTH - 1

    def nrm(shape, scale):
        return jax.random.normal(next(ks), shape, jnp.float32) * scale

    def unif(shape, lo, hi):
        return jax.random.uniform(next(ks), shape, jnp.float32, lo, hi)

    dt = jnp.exp(unif((L, GDN_V_HEADS), math.log(1e-3), math.log(1e-1)))
    return {
        'x': nrm((BATCH, SEQ, D), 1.0),
        'attn_norm_w': 1.0 + nrm((L, D), 0.05),
        'w_in': nrm((L, D, N_IN), D ** -0.5),
        'rwkv_mu': unif((L, N_RWKV_IN), 0.0, 1.0),
        'rwkv_w0': unif((L, RWKV_DIM), -6.0, -0.5),
        'rwkv_w_up': nrm((L, RWKV_DECAY_LORA, RWKV_DIM), 0.1 * RWKV_DECAY_LORA ** -0.5),
        'rwkv_a0': nrm((L, RWKV_DIM), 0.1),
        'rwkv_a_up': nrm((L, RWKV_AAA_LORA, RWKV_DIM), 0.5 * RWKV_AAA_LORA ** -0.5),
        'rwkv_g_up': nrm((L, RWKV_GATE_LORA, RWKV_DIM), RWKV_GATE_LORA ** -0.5),
        'rwkv_k_k': 0.85 + nrm((L, RWKV_DIM), 0.05),
        'rwkv_k_a': 1.0 + nrm((L, RWKV_DIM), 0.05),
        'rwkv_r_k': -0.04 + nrm((L, RWKV_HEADS, RWKV_HEAD), 0.02),
        'rwkv_ln_w': 1.0 + nrm((L, RWKV_DIM), 0.05),
        'rwkv_ln_b': nrm((L, RWKV_DIM), 0.02),
        'vres_down': nrm((Lv, D, RWKV_MV_LORA), D ** -0.5),
        'vres_mu': unif((Lv, RWKV_MV_LORA), 0.0, 1.0),
        'vres_up': nrm((Lv, RWKV_MV_LORA, RWKV_DIM), 0.5 * RWKV_MV_LORA ** -0.5),
        'vres_v0': 1.0 + nrm((Lv, RWKV_DIM), 0.1),
        'gdn_conv_w': nrm((L, GDN_CONV, 2 * GDN_QK_DIM + GDN_V_DIM), 0.5),
        'gdn_A_log': jnp.log(unif((L, GDN_V_HEADS), 1.0, 16.0)),
        'gdn_dt_bias': jnp.log(jnp.expm1(dt)),
        'gdn_norm_w': 1.0 + nrm((L, GDN_HEAD), 0.05),
        'w_out': nrm((L, MIX_DIM, D), MIX_DIM ** -0.5),
        'ffn_norm_w': 1.0 + nrm((L, D), 0.05),
        'ffn_w_gate': nrm((L, D, D_FF_2), D ** -0.5),
        'ffn_w_up': nrm((L, D, D_FF_2), D ** -0.5),
        'ffn_w_down': nrm((L, D_FF_2, D), D_FF_2 ** -0.5),
        'final_norm_w': 1.0 + nrm((D,), 0.05),
    }

def second_block(x, attn_norm_w, w_in, rwkv_mu, rwkv_w0, rwkv_w_up, rwkv_a0, rwkv_a_up, rwkv_g_up,
              rwkv_k_k, rwkv_k_a, rwkv_r_k, rwkv_ln_w, rwkv_ln_b, vres_down, vres_mu, vres_up, vres_v0,
              gdn_conv_w, gdn_A_log, gdn_dt_bias, gdn_norm_w, w_out, ffn_norm_w, ffn_w_gate, ffn_w_up,
              ffn_w_down, final_norm_w):
    v_first = None
    for l in range(DEPTH):
        h = rms_norm_2(x, attn_norm_w[l])
        if l == 0:
            w_cat = w_in[0]
        else:
            w_cat = jnp.concatenate([w_in[l], vres_down[l - 1]], axis=1)
        proj = h @ w_cat
        p_rwkv = proj[..., :N_RWKV_IN]
        p_gdn = proj[..., N_RWKV_IN:N_IN]
        if l == 0:
            vres = None
        else:
            vd = token_shift_lerp(proj[..., N_IN:].astype(jnp.float32), vres_mu[l - 1])
            vres = (vd, vres_up[l - 1], vres_v0[l - 1])
        y_a, v_first = rwkv7_mixer(p_rwkv, vres, v_first, rwkv_mu[l], rwkv_w0[l], rwkv_w_up[l],
                                   rwkv_a0[l], rwkv_a_up[l], rwkv_g_up[l], rwkv_k_k[l], rwkv_k_a[l],
                                   rwkv_r_k[l], rwkv_ln_w[l], rwkv_ln_b[l])
        y_b = gdn_mixer(p_gdn, gdn_conv_w[l], gdn_A_log[l], gdn_dt_bias[l], gdn_norm_w[l])
        y = jnp.concatenate([y_a, y_b], axis=-1).astype(x.dtype)
        x = x + y @ w_out[l]
        h = rms_norm_2(x, ffn_norm_w[l])
        x = x + (jax.nn.silu(h @ ffn_w_gate[l]) * (h @ ffn_w_up[l])) @ ffn_w_down[l]
    return rms_norm_2(x, final_norm_w)


def setup_inputs(seed=0):
    out = dict(first_inputs(seed))
    for name, value in second_inputs(seed + 1).items():
        if name != "x":
            out[name + "_2"] = value
    return out


def reference(
    x, g_mix, w_in, b_forget, conv_w, conv_b, w_rg, b_rg, w_ig, b_ig, lru_lambda, w_pool,
    pool_scale, w_branch_rnn, w_branch_attn, w_branch_pool, w_out, g_ffn, w_ffn_in, w_ffn_out,
    g_final, attn_norm_w_2, w_in_2, rwkv_mu_2, rwkv_w0_2, rwkv_w_up_2, rwkv_a0_2, rwkv_a_up_2,
    rwkv_g_up_2, rwkv_k_k_2, rwkv_k_a_2, rwkv_r_k_2, rwkv_ln_w_2, rwkv_ln_b_2, vres_down_2,
    vres_mu_2, vres_up_2, vres_v0_2, gdn_conv_w_2, gdn_A_log_2, gdn_dt_bias_2, gdn_norm_w_2,
    w_out_2, ffn_norm_w_2, ffn_w_gate_2, ffn_w_up_2, ffn_w_down_2, final_norm_w_2,
):
    x = first_block(
        x, g_mix, w_in, b_forget, conv_w, conv_b, w_rg, b_rg, w_ig, b_ig, lru_lambda, w_pool,
        pool_scale, w_branch_rnn, w_branch_attn, w_branch_pool, w_out, g_ffn, w_ffn_in,
        w_ffn_out, g_final,
    )
    return second_block(
        x, attn_norm_w_2, w_in_2, rwkv_mu_2, rwkv_w0_2, rwkv_w_up_2, rwkv_a0_2, rwkv_a_up_2,
        rwkv_g_up_2, rwkv_k_k_2, rwkv_k_a_2, rwkv_r_k_2, rwkv_ln_w_2, rwkv_ln_b_2, vres_down_2,
        vres_mu_2, vres_up_2, vres_v0_2, gdn_conv_w_2, gdn_A_log_2, gdn_dt_bias_2, gdn_norm_w_2,
        w_out_2, ffn_norm_w_2, ffn_w_gate_2, ffn_w_up_2, ffn_w_down_2, final_norm_w_2,
    )


_drawn_inputs = setup_inputs


def setup_inputs(seed=0):
    import zlib

    import numpy as np

    out = dict(_drawn_inputs(seed))
    spreads = {}
    factors = {'b_rg': 37.67,
     'b_ig': 23.467,
     'rwkv_w_up_2': 8.0,
     'rwkv_a0_2': 3.591,
     'rwkv_k_k_2': 11.164,
     'rwkv_k_a_2': 2.701,
     'rwkv_r_k_2': 3.451,
     'rwkv_ln_w_2': 2.86,
     'rwkv_ln_b_2': 8.0,
     'gdn_norm_w_2': 3.067}
    for name, (base, spread) in spreads.items():
        noise = np.random.default_rng([zlib.crc32(name.encode()), seed]).standard_normal(out[name].shape)
        drawn = base * np.exp(spread * noise) if base else spread * noise
        out[name] = __import__('jax').numpy.asarray(drawn.astype(out[name].dtype))
    for name, factor in factors.items():
        out[name] = (out[name] * factor).astype(out[name].dtype)
    return out
```

```python
from contextlib import ExitStack

import concourse.bass as bass
from concourse import mybir

F32 = mybir.dt.float32
F32R = mybir.dt.float32r
ALU = mybir.AluOpType
ACT = mybir.ActivationFunctionType
AX_X = mybir.AxisListType.X

P = 128
T = 256
D = 2048
KT = D // P
NT = 8
H = 8
FF = 5632
FT = FF // P
CK = 4
CN = 512
KB = 1024
INV_LEVELS = (5, 5, 6)
NEG = -1.0e30
EPS1, EPS2 = 1e-6, 1e-5


class Gemm:

    def __init__(self, before, ring, hi, strips, bodies, sources):
        self.ring, self.hi, self.strips, self.bodies, self.sources = ring, hi, strips, bodies, sources
        self.per = sum(n for n, _ in strips)
        self.base = before.base + before.per * before.bodies if before else 0
        self.sbase = before.sbase + before.ns * before.bodies if before else 0
        self.ns = len([r for _, r in strips if r])
        self.landed0 = list(before.landed1) if before else [0] * 4
        self.landed1 = [n + (self.per // ring * bodies if s < ring else 0) for s, n in enumerate(self.landed0)]
        self.ends = {}
        at = 0
        for s, (n, _) in enumerate(strips):
            at += n
            self.ends[at - 1] = s
        assert self.per % ring == 0 and self.per % hi == 0

    def chunk(self, i, j):
        return self.base + i * self.per + j

    def landed(self, i, j):
        return 16 * (self.landed0[j % self.ring] + 1 + j // self.ring) + i * (16 * (self.per // self.ring))

    def strip(self, i, s):
        return self.sbase + i * self.ns + s

    @property
    def end(self):
        return self.base + self.per * self.bodies


def build(nc, a, out):
    ctx = ExitStack()
    with ctx:
        base = -(-nc.sbuf_base // 64) * 64
        RING, XO, HHO, HLO, HO = base, base + 48 * KB, base + 64 * KB, base + 80 * KB, base + 96 * KB
        WO = base + 112 * KB
        CO = WO + 80 * KB
        used = {}

        def at(name, shape, off, dt=F32):
            return nc.alloc_sbuf_tensor_at(name, shape, dt, offset=off)

        const_at = [CO]

        def const(name, shape, dt=F32):
            n = 4
            for s in shape[1:]:
                n *= s
            t = at(name, shape, const_at[0], dt)
            const_at[0] += -(-n // 32) * 32
            assert const_at[0] <= nc.sbuf_usable_end, name
            return t

        psum = ctx.enter_context(nc.psum_tensor("psum", [P, 8, 512], F32))

        def pair(s):
            return psum[:, 2 * (s % 4):2 * (s % 4) + 2, :].rearrange("p b (t n) -> p (b t) n", t=2)

        def bank(b):
            return psum[:, b, :]

        def sem(name):
            return ctx.enter_context(nc.semaphore(name))

        raw = [at(f"weight_raw{s}", [P, CK, CN], RING + 8 * KB * s) for s in range(4)]
        lo = [at(f"weight_lo{s}", [P, CK, CN], RING + 8 * KB * s, F32R) for s in range(4)]
        hi = {2: [at(f"weight_hi2_{s}", [P, CK, CN], RING + 32 * KB + 8 * KB * s, F32R) for s in range(2)],
              3: [at(f"weight_hi3_{s}", [P, CK, CN], RING + 24 * KB + 8 * KB * s, F32R) for s in range(3)]}
        X = at("residual", [P, KT, T], XO)
        Hh = at("h_hi", [P, KT, T], HHO, F32R)
        Hl = at("h_lo", [P, KT, T], HLO, F32R)
        Hr = at("h_raw", [P, KT, T], HO)
        tokens = at("x_tokens", [P, 2, D], HO)
        out_tokens = at("out_tokens", [P, 2, D], WO)
        SQ = at("squares", [P, KT, T], WO)
        proj = at("proj1", [P, 6 * NT, T], WO)
        TO = WO + 48 * KB
        t1, t2, t3, t4 = (at(f"temp{n}", [P, NT, T], TO + 8 * KB * n) for n in range(4))
        rx = proj[:, 0:NT, :]
        ry = proj[:, NT:2 * NT, :]
        t1b = at("conv_u_t", [P, NT, T], HO)
        t4b = at("gelu_t", [P, NT, T], HO + 8 * KB)
        yh = [at(f"y_hi{b}", [P, NT, T], WO + 16 * KB * b, F32R) for b in range(3)]
        yl = [at(f"y_lo{b}", [P, NT, T], WO + 16 * KB * b + 8 * KB, F32R) for b in range(3)]
        merged = at("merged", [P, KT, T], TO)
        sg = at("sig_gate", [P, 4, T], TO + 16 * KB)
        gated = at("gated", [P, 4, T], TO + 20 * KB)
        Fh = at("ffn_hi", [P, FT, T], HO, F32R)
        Fl = at("ffn_lo", [P, FT, T], HO + FT * KB, F32R)
        act_gate = at("ffn_act", [P, 4, T], HO + 2 * FT * KB)
        act_up = at("ffn_act_up", [P, 4, T], HO + 2 * FT * KB + 4 * KB)

        ident = const("ident", [P, P])
        ones = const("ones", [P, P])
        causal = const("causal", [P, P])
        par1 = const("par1", [P, 316])
        rstd = const("rstd", [P, T])
        lam8 = const("lam8", [P, NT])
        spt = [const(f"sp_tmp{n}", [P, NT]) for n in range(4)]
        fT = [at(f"f_tmp{n}", [H, T], TO + KB * n) for n in range(4)]
        ones8 = const("ones_rows", [H, T])
        neg_f = const("neg_f_cumsum", [H, T])
        bfor = const("b_forget_col", [H, 1])
        wf = const("w_forget", [P, KT, H])
        neg_max = const("neg_max", [P, 4])
        rowsum = const("rowsum", [P, 4])
        rows = [at(f"param_rows{n}", [P, P], WO + 512 * n) for n in range(3)]

        w_rg = at("w_rg_s", [P, NT, P], RING)
        w_ig = at("w_ig_s", [P, NT, P], RING + 4 * KB)
        w_pl = at("w_pool_s", [P, 4, 2, 256], RING + 8 * KB)
        recip_cnt = at("recip_cnt", [P, 4, T], RING + 16 * KB)
        selrow = at("selrow", [H, H, P], RING + 20 * KB)
        fmask = at("f_masked", [H, H, T], RING + 24 * KB)
        probs = at("probs", [P, 2, 384], RING + 32 * KB)
        probsT = at("probs_t", [P, 2, 384], RING + 35 * KB)
        vtok = at("v_tokens", [P, 2, 1024], RING + 38 * KB)

        groups = [[("g_mix", 16), ("conv_w", 32), ("conv_b", 8), ("b_rg", 8), ("b_ig", 8), ("lru_lambda", 8),
                   ("pool_scale", 8), ("g_ffn", 16), ("g_final", 16)],
                  [("attn_norm_w_2", 16), ("rwkv_mu_2", 27), ("rwkv_w0_2", 8), ("rwkv_a0_2", 8), ("rwkv_k_k_2", 8),
                   ("rwkv_k_a_2", 8), ("rwkv_r_k_2", 8), ("rwkv_ln_w_2", 8), ("rwkv_ln_b_2", 8), ("ffn_norm_w_2", 16)],
                  [("gdn_conv_w_2", 64), ("gdn_norm_w_2", 1), ("final_norm_w_2", 16)]]
        col, ncols, spans = {}, 0, []
        for g in groups:
            spans.append((ncols, sum(k for _, k in g)))
            for n, k in g:
                col[n] = ncols
                ncols += k

        def pcol(name, k=0, rows=P):
            return par1[0:rows, col[name] + k:col[name] + k + 1]

        low = [const(f"low_mask{n}", [P, P]) for n in range(7)]
        low0_t = const("low_mask0_t", [P, P])
        upper_strict = const("upper_strict64", [P, P])
        upper_incl = const("upper_incl64", [P, P])
        head_ones = const("head_ones64", [P, P])
        chunk_decay = const("chunk_decay", [P, NT, 4])
        state = const("rwkv_state", [P, NT, 64])
        gb = const("gdn_b", [H, T])
        alog, dtb = const("gdn_A_log_col", [H, 1]), const("gdn_dt_col", [H, 1])
        tokp = const("gdn_token_scalars", [P, 8, H])
        CH = 64
        proj2 = at("proj2", [P, 48, T], WO)
        yfin = at("y_out", [P, KT, T], WO)
        w_lora = at("w_lora", [P, KT, 288], TO)
        w_ab = at("w_ab", [P, KT, 16], TO + 18 * KB)

        def slot(name, off, shape=(NT, T)):
            return at(name, [P, *shape], off)
        R0, R1, R2, R3, R4, R5 = (RING + 8 * KB * n for n in range(6))
        w_upa = slot("w_up_a_up", R4, (1024,))
        w_gu = slot("g_up", R4 + 4 * KB, (2, 1024))
        lp = slot("lora", TO + 24 * KB, (3, T))
        lpd = slot("lora_shift", TO + 27 * KB, (3, T))
        shift = [slot(f"shift{n}", o) for n, o in enumerate((HHO, HLO, HHO + 8 * KB))]
        Rw, Kw, Vw = proj2[:, 0:8, :], proj2[:, 8:16, :], proj2[:, 16:24, :]
        ld, reset = slot("log_decay", TO), slot("reset_mask", TO + 8 * KB)
        cum, a_lr = slot("cum_decay", HO), slot("a_rate", HO + 8 * KB)
        kk, bonus = slot("kk", HHO), slot("bonus", HHO + 8 * KB)
        at_f, bt_f = slot("a_tilde", HLO), slot("b_tilde", HLO + 8 * KB)
        gate2 = slot("rwkv_gate", R3)
        at_tok, bt_tok = slot("a_tokens", R2, (1024,)), slot("b_tokens", R2 + 4 * KB, (1024,))
        kt_tok, v_tok2 = slot("k_tokens", TO + 24 * KB, (1024,)), slot("v_tokens2", TO + 28 * KB, (1024,))
        nt_r, akt, rbt = (slot(n, TO + 8 * KB * k, (16, P)) for k, n in enumerate(("rw_nt", "rw_akt", "rw_rbt")))
        rkt, x_r = slot("rw_rkt", HO, (16, P)), slot("rw_x", HO + 8 * KB, (16, P))
        xt_r, z_r = slot("rw_xt", R0, (16, P)), slot("rw_z", R1, (16, P))
        uv, wt = slot("rw_uv", R4, (1024,)), slot("rw_wt", R4 + 4 * KB, (NT, P))
        z1, u_tok = slot("rw_z1", R5, (1024,)), slot("rw_u", R5 + 4 * KB, (1024,))
        y_rw = slot("rw_y", HHO)
        gn_sq, gn_r = slot("gn_squares", TO), slot("gn_rstd", TO + 8 * KB)
        cv, cv_s = slot("gdn_conv", TO, (16, T)), slot("gdn_conv_sig", TO + 16 * KB, (16, T))
        gn = [at(f"gdn_small{n}", [H, T], TO + 16 * KB + KB * n) for n in range(8)]
        l2s = slot("gdn_l2", HHO, (8, T))
        selrow2 = at("selrow2", [H, H, P], TO + 24 * KB)
        neg_ls, neg_ui = at("neg_lower_strict", [P, P], TO + 28 * KB), at("neg_upper_incl", [P, P], TO + 28 * KB + 512)
        gm, ngm = at("gdn_gm", [H, H, T], HLO), at("gdn_ngm", [H, H, T], HLO + 8 * KB)
        gam, gam_t = slot("gamma", R3, (16, P)), slot("gamma_t", R4, (16, P))
        nt_g, x_g, xt_g, z_g = (slot(n, o, (16, P)) for n, o in (("gd_nt", HO), ("gd_x", HO + 8 * KB), ("gd_xt", R0), ("gd_z", R1)))
        aqk = slot("gd_aqk_t", R2, (16, P))
        v_beta = slot("gd_v_beta", R5, (16, P))
        k_bg = slot("gd_k_beta_g", HHO, (16, P))
        k_g, q_g = slot("gd_k_g", HHO + 8 * KB, (NT, P)), slot("gd_q_g", HHO + 12 * KB, (NT, P))
        u_g = slot("gd_u", HLO, (16, P))
        w_g, v_new = slot("gd_w_t", HLO + 8 * KB, (NT, P)), slot("gd_v_new", HLO + 12 * KB, (NT, P))
        s_g = slot("gd_state", R3, (NT, P))
        o_g = slot("gd_o", TO + 24 * KB)
        o_sq, o_r = slot("gd_o_sq", HO), slot("gd_o_rstd", R0)
        z_sig = slot("gd_z_sig", R1)

        def hc(x):
            h = 2 * (x % 8) + x // 8
            return slice(64 * h, 64 * h + 64)

        def hr(x):
            return slice(64 * (x // 8), 64 * (x // 8) + 64)

        def bc(m, n):
            return m[:].unsqueeze(1).to_broadcast([P, n, P])

        STEPS = {
            "gpsimd": ["rows_cleared", "reset_built", "selrow2_built"],
            "tensor": ["lora_mm", "zw_mm", "za_mm", "g_mm", "kk_sum", "rk_sum", "gn_mean", "gn_var", "gd_tok",
                "gd_l2", "gd_gram", "gd_w", "gd_s", "gd_eg", "gd_ws", "gd_o", "gd_o_sum"],
            "scalar": ["lora_out", "lora_act", "ld_out", "a_out", "g_out", "kk_sq", "kk_root", "e_prev", "e_plus",
                "e_minus", "gn_sq", "gn_root", "gd_cv_sig", "gd_beta", "gd_expA", "gd_sq", "gd_l2_root",
                "gd_tok_exp", "gd_w_out", "gd_s_out", "gd_o_out", "gd_o_sq", "gd_z_sig", "gd_o_root"],
            "vector": ["ab_out", "lora_in", "kk", "l_prev", "kk_mean", "rk", "at_made", "rw_fm", "gn_c", "gn_m",
                "gn_out", "gd_cv", "gd_silu", "gd_cum", "gd_rows", "gd_tok_out", "gd_l2_mean", "gd_qk",
                "gd_n", "gd_k_bg", "gd_qg", "gd_vn", "gd_o_mean", "y2_split"],
        }
        step_sem = {e: sem(f"{e}_steps") for e in STEPS}
        step_of = {n: (e, k + 1) for e in STEPS for k, n in enumerate(STEPS[e])}
        made = {e: 0 for e in STEPS}

        def step(name):
            e, k = step_of[name]
            made[e] += 1
            assert made[e] == k, name
            return step_sem[e]

        def at_step(name):
            e, k = step_of[name]
            return step_sem[e], k

        sems = {}

        def S(name):
            if name not in sems:
                sems[name] = sem(name)
            return sems[name]

        landed = [sem(f"chunk_landed{s}") for s in range(4)]
        hi_ready, lo_ready = sem("chunk_hi_ready"), sem("chunk_lo_ready")
        chunks_used, strips_out = sem("chunks_used"), sem("strips_evacuated")
        x_landed, par_landed = sem("x_landed"), sem("params_landed")
        consts = sem("constants_built")
        x_turned, par_turned, par_ready, x_ready = sem("x_transposed"), sem("params_transposed"), sem("params_ready"), sem("x_ready")
        n_sq, n_sum, n_mean, n_root, h_ready = (sem(f"norm_{x}") for x in ("squared", "summed", "mean", "root", "split"))
        mw_landed, mix_tables = sem("mixer_weights_landed"), sem("mixer_tables_built")
        f_logits = sem("f_logits_summed")
        sp_abs, sp_exp = sem("softplus_abs"), sem("softplus_exp")
        proj_out = sem("proj_evacuated")
        pool_in, pool_mm = sem("pooled_ready"), sem("pool_product")
        conv_u, gates_mm, r_sig, i_sig = sem("conv_u"), sem("lru_gate_products"), sem("lru_r"), sem("lru_i")
        lru_a, lru_th, lru_sq, lru_var, lru_root = (sem(f"lru_{x}") for x in ("decay", "tanh", "decay_squared", "variance", "input_scale"))
        gelu_sq, gelu_arg, gelu_sig = sem("gelu_squared"), sem("gelu_argument"), sem("gelu_sigmoid")
        q_scaled, f_rows = sem("q_scaled"), sem("f_rows")
        v_turned, v_tok = sem("v_transposed"), sem("v_tokens_ready")
        sc_mm, sc_max, sc_exp, sc_p, sc_t, sc_pt, sc_o, sc_y = (
            sem(f"attn_{x}") for x in ("scores", "max", "exp", "probs", "transposed", "probs_t", "product", "out"))
        y_ready, merged_ready = sem("y_split"), sem("merged_split")
        merged_sum, gate_sig, ffn_hi = sem("merged_added"), sem("gate_sigmoid"), sem("ffn_hi")
        pool_out, lru_iu, lam_ready = sem("pool_out"), sem("lru_gated_input"), sem("lambda_ready")
        ffn_sig, ffn_split = sem("ffn_sigmoid"), sem("ffn_split")
        down_done = sem("down_product")
        out_turned, out_copied, out_stored = sem("out_transposed"), sem("out_copied"), sem("out_stored")
        chain = {k: sem(f"{k}_order") for k in ("vector", "scalar", "gpsimd", "tensor")}

        w_in = a["w_in"][0].rearrange("(k p) n -> p k n", p=P)

        def sl(w, k, c):
            return w[:, CK * k:CK * k + CK, bass.ds(c, CN)]

        def h_rhs(kt):
            return Hh[:, kt, :], Hl[:, kt, :]

        in1 = Gemm(None, 4, 2, [(4, h_rhs)] * 2, 6,
                   lambda i: [sl(w_in, k, (5128 if isinstance(i, int) and i == 5 else i * 1024) + s * CN)
                              for s in range(2) for k in range(4)])
        w_br = [a[n][0].rearrange("(k p) n -> p k n", p=P) for n in ("w_branch_rnn", "w_branch_attn", "w_branch_pool")]
        GATES = 5128 + 1024

        def y_rhs(b):
            return lambda kt: (yh[b][:, kt, :], yl[b][:, kt, :])

        mer = Gemm(in1, 3, 3, [x for b in range(3) for x in ((4, h_rhs), (2, y_rhs(b)))], 4,
                   lambda i: [x for b in range(3) for x in
                              [sl(w_in, k, GATES + b * D + i * CN) for k in range(4)] +
                              [sl(w_br[b], k, i * CN) for k in range(2)]])
        w_o = a["w_out"][0].rearrange("(k p) n -> p k n", p=P)
        wo1 = Gemm(mer, 4, 2, [(4, h_rhs)] * 2, 2,
                   lambda i: [sl(w_o, k, i * 1024 + s * CN) for s in range(2) for k in range(4)])
        w_f1 = a["w_ffn_in"][0].rearrange("(k p) n -> p k n", p=P)
        up1 = Gemm(wo1, 4, 2, [(4, h_rhs)] * 2, FF // CN,
                   lambda i: [sl(w_f1, k, i * CN + s * FF) for s in range(2) for k in range(4)])
        w_d1 = a["w_ffn_out"][0].rearrange("(k p) n -> p k n", p=P)
        dn1 = Gemm(up1, 4, 2, [(4, None)], FT // CK,
                   lambda i: [w_d1[:, bass.ds(i * CK, CK), c * CN:(c + 1) * CN] for c in range(4)])

        w_in2 = a["w_in_2"][0].rearrange("(k p) n -> p k n", p=P)
        N_RWKV = 3360
        in2 = Gemm(dn1, 4, 2, [(4, h_rhs)] * 2, 6,
                   lambda i, off=0: [sl(w_in2, k, off + i * 1024 + s * CN) for s in range(2) for k in range(4)])
        w_o2 = a["w_out_2"][0].rearrange("(k p) n -> p k n", p=P)
        wo2 = Gemm(in2, 4, 2, [(4, h_rhs)] * 2, 2,
                   lambda i: [sl(w_o2, k, i * 1024 + s * CN) for s in range(2) for k in range(4)])
        w_gu2 = [a[n][0].rearrange("(k p) n -> p k n", p=P) for n in ("ffn_w_gate_2", "ffn_w_up_2")]
        up2 = Gemm(wo2, 4, 2, [(4, h_rhs)] * 2, FF // CN,
                   lambda i: [sl(w_gu2[s], k, i * CN) for s in range(2) for k in range(4)])
        w_d2 = a["ffn_w_down_2"][0].rearrange("(k p) n -> p k n", p=P)
        dn2 = Gemm(up2, 4, 2, [(4, None)], FT // CK,
                   lambda i: [w_d2[:, bass.ds(i * CK, CK), c * CN:(c + 1) * CN] for c in range(4)])

        def wait(e, s, v):
            if isinstance(v, int) and v <= 0:
                return
            e.wait_ge(s, v)

        def settler(e, name):
            n = [0]

            def settle(ins):
                n[0] += 1
                ins.then_inc(chain[name], 1)
                e.wait_ge(chain[name], n[0])
            return settle

        def loops(e, g, body, last=None):
            last = g.bodies if last is None else last
            body(0)
            if last == 2:
                body(1)
            else:
                with e.Fori(1, last) as i:
                    body(i)

        block = ctx.enter_context(nc.Block())

        @block.sync
        def _(sp):
            sp.dma_start(tokens[:], a["x"][0].rearrange("(b p) n -> p b n", p=P)).then_inc(x_landed, 16)
            sp.wait_ge(*at_step("rows_cleared"))
            for g, tile in zip(groups, rows):
                r = 0
                for n, k in g:
                    src = a[n]
                    src = src if n in ("g_final", "final_norm_w_2") else src[0]
                    if len(src.shape) == 2 and n != "rwkv_r_k_2":
                        src = src.rearrange("k (r c) -> (k r) c", c=P)
                    elif n == "rwkv_r_k_2":
                        src = src.rearrange("(r h) c -> r (h c)", h=2)
                    elif n == "rwkv_mu_2":
                        sp.dma_start(tile[r + 26:r + 27, 0:32], src[26 * P:3360].rearrange("(r c) -> r c", r=1)).then_inc(par_landed, 16)
                        sp.dma_start(tile[r:r + 26, :], src[0:26 * P].rearrange("(r c) -> r c", c=P)).then_inc(par_landed, 16)
                        r += k
                        continue
                    else:
                        src = src.rearrange("(r c) -> r c", c=P)
                    sp.dma_start(tile[r:r + k, :], src).then_inc(par_landed, 16)
                    r += k
            with nc.allow_non_contiguous_dma(reason="8 values"):
                sp.dma_start(bfor[:], a["b_forget"].rearrange("a h -> h a")).then_inc(par_landed, 16)
                sp.dma_start(alog[:], a["gdn_A_log_2"].rearrange("a h -> h a")).then_inc(par_landed, 16)
                sp.dma_start(dtb[:], a["gdn_dt_bias_2"].rearrange("a h -> h a")).then_inc(par_landed, 16)
                sp.dma_start(wf[:], w_in[:, :, 5120:5128]).then_inc(par_landed, 16)

            def load(g, i, *more):
                for j, src in enumerate(g.sources(i, *more)):
                    wait(sp, chunks_used, g.chunk(i, j) - g.ring + 1)
                    sp.dma_start(raw[j % g.ring][:], src).then_inc(landed[j % g.ring], 16)

            def loads(g, last=None):
                wait(sp, chunks_used, g.base)
                loops(sp, g, lambda i: load(g, i), last)

            loads(in1, 5)
            load(in1, 5)
            sp.wait_ge(chunks_used, in1.end)
            sp.dma_start(w_rg[:], a["w_rg"][0].rearrange("n c d -> c n d")).then_inc(mw_landed, 16)
            sp.dma_start(w_ig[:], a["w_ig"][0].rearrange("n c d -> c n d")).then_inc(mw_landed, 16)
            sp.dma_start(w_pl[:], a["w_pool"][0].rearrange("g (t p) d -> p g t d", p=P)).then_inc(mw_landed, 16)
            sp.wait_ge(y_ready, 3)
            sp.wait_ge(chunks_used, mer.base)
            for i in range(mer.bodies):
                load(mer, i)
            loads(wo1)
            loads(up1)
            loads(dn1)
            sp.wait_ge(chunks_used, in2.base)
            sp.dma_start(w_lora[:], w_in2[:, :, 3072:N_RWKV]).then_inc(S("lora_w_landed"), 16)
            sp.dma_start(w_ab[:], w_in2[:, :, 6432:6448]).then_inc(S("lora_w_landed"), 16)
            load(in2, 0)
            with sp.Fori(1, 3) as i:
                load(in2, i)
            with sp.Fori(3, 6) as i:
                load(in2, i, N_RWKV - 3072)
            sp.wait_ge(chunks_used, in2.end)
            sp.dma_start(w_upa[0:64, :], a["rwkv_w_up_2"][0]).then_inc(S("ups_landed"), 16)
            sp.dma_start(w_upa[64:P, :], a["rwkv_a_up_2"][0]).then_inc(S("ups_landed"), 16)
            sp.dma_start(w_gu[:, 0, :], a["rwkv_g_up_2"][0, 0:P]).then_inc(S("ups_landed"), 16)
            sp.dma_start(w_gu[0:32, 1, :], a["rwkv_g_up_2"][0, P:160]).then_inc(S("ups_landed"), 16)
            sp.wait_ge(*at_step("y2_split"))
            loads(wo2)
            loads(up2)
            loads(dn2)
            sp.wait_ge(out_copied, 8)
            for b in range(2):
                sp.dma_start(out[0, b * P:(b + 1) * P, :], out_tokens[:, b, :]).then_inc(out_stored, 16)
            sp.wait_ge(out_stored, 32)

        @block.gpsimd
        def _(gp):
            settle = settler(gp, "gpsimd")
            gp.memset(rows[1][:], 0.0).then_inc(step("rows_cleared"), 1)
            gp.memset(ident[:], 0.0)
            gp.memset(causal[:], 0.0)
            settle(gp.memset(ones[:], 1.0))
            gp.affine_select(out=ident[:], in_=ident[:], compare_op=ALU.not_equal, fill=1.0, base=0,
                             pattern=[[-1, P]], channel_multiplier=1).then_inc(consts, 1)
            gp.affine_select(out=causal[:], in_=causal[:], compare_op=ALU.is_ge, fill=NEG, base=0,
                             pattern=[[-1, P]], channel_multiplier=1).then_inc(consts, 1)
            gp.wait_ge(chunks_used, in1.end)
            for g, w in enumerate((2, 4, 8, 16)):
                gp.memset(recip_cnt[:, g, :], 1.0 / w)
            settle(gp.memset(selrow[:], 0.0))
            for g, w in enumerate((2, 4, 8, 16)):
                for t in range(w - 1):
                    gp.memset(recip_cnt[:, g, t:t + 1], 1.0 / (t + 1))
            gp.affine_select(out=selrow[:], in_=selrow[:], compare_op=ALU.not_equal, fill=1.0, base=0,
                             pattern=[[-1, H], [0, P]], channel_multiplier=1).then_inc(mix_tables, 1)

            def keep(m, base, pattern, cm):
                settle(gp.affine_select(out=m[:], in_=m[:], compare_op=ALU.is_ge, fill=0.0, base=base,
                                        pattern=pattern, channel_multiplier=cm))

            for m in (*low, low0_t, upper_strict, upper_incl, head_ones):
                settle(gp.memset(m[:], 1.0))
            for n in range(7):
                s = 2 ** n
                keep(low[n], -s, [[-s, P // s], [0, s]], 1)
                keep(low[n], 2 * s - 1, [[2 * s, P // (2 * s)], [0, 2 * s]], -1)
            keep(low0_t, -1, [[1, P]], -1)
            keep(low0_t, 0, [[-2, P // 2], [0, 2]], 1)
            for m in (upper_strict, upper_incl, head_ones):
                keep(m, 0, [[-CH, P // CH], [0, CH]], 1)
            keep(upper_strict, -1, [[1, P]], -1)
            keep(upper_incl, 0, [[1, P]], -1)
            keep(head_ones, CH - 1, [[CH, P // CH], [0, CH]], -1)
            gp.memset(state[:], 0.0).then_inc(S("rw_state"), 1)
            gp.wait_ge(*at_step("lora_mm"))
            settle(gp.memset(reset[:], 1.0))
            gp.memset(reset[:].rearrange("p k (c t) -> p (k c) t", t=CH)[:, :, 0:1], 0.0).then_inc(step("reset_built"), 1)
            gp.wait_ge(*at_step("gd_silu"))
            gp.memset(neg_ls[:], 0.0)
            gp.memset(neg_ui[:], 0.0)
            settle(gp.memset(selrow2[:], 0.0))
            gp.affine_select(out=neg_ls[:], in_=neg_ls[:], compare_op=ALU.is_ge, fill=NEG, base=-1,
                             pattern=[[-1, P]], channel_multiplier=1)
            gp.affine_select(out=neg_ui[:], in_=neg_ui[:], compare_op=ALU.is_ge, fill=NEG, base=0,
                             pattern=[[1, P]], channel_multiplier=-1)
            gp.affine_select(out=selrow2[:], in_=selrow2[:], compare_op=ALU.not_equal, fill=1.0, base=0,
                             pattern=[[-1, H], [0, P]], channel_multiplier=1).then_inc(step("selrow2_built"), 1)

        @block.tensor
        def _(pe):
            mm, tr = nc.tensor.matmul, nc.tensor.transpose
            pe.wait_ge(consts, 2)
            pe.wait_ge(par_landed, 16 * (sum(len(g) for g in groups) + 5))
            for (c, k), tile in zip(spans, rows):
                last = tr(bank(0)[:, c:c + k], tile[0:k, :], ident[0:k, 0:k])
            last.then_inc(par_turned, 1)
            pe.wait_ge(x_landed, 16)
            pe.wait_ge(par_ready, 1)
            for b in range(8):
                for k in range(2):
                    for t in range(2):
                        last = tr(bank(b)[:, (2 * k + t) * P:(2 * k + t + 1) * P],
                                  tokens[:, t, (2 * b + k) * P:(2 * b + k + 1) * P], ident[:])
                last.then_inc(x_turned, 1)

            def norm_sums(n):
                pe.wait_ge(n_sq, n + 1)
                for k in range(KT):
                    last = mm(bank(7)[:, 0:T], ones[:], SQ[:, k, :], start=(k == 0), stop=(k == KT - 1))
                last.then_inc(n_sum, 1)

            def product(g, i, j, acc, rhs, start, stop):
                pe.wait_ge(lo_ready, g.chunk(i, j) + 1)
                wh, wl = hi[g.hi][j % g.hi], lo[j % g.ring]
                for f in range(4):
                    for k in range(CK):
                        xh, xl = rhs(k)
                        c = slice(f * P, (f + 1) * P)
                        mm(acc[:, f, :], wh[:, k, c], xh, start=(start and k == 0 and f % 2 == 0),
                           stop=False, skip_group_check=True)
                        mm(acc[:, f, :], wl[:, k, c], xh, start=False, stop=False, skip_group_check=True)
                        last = mm(acc[:, f, :], wh[:, k, c], xl, start=False,
                                  stop=(stop and k == CK - 1), skip_group_check=True)
                last.then_inc(chunks_used, 1)

            def body(g, i):
                j = 0
                for s, (n, rhs) in enumerate(g.strips):
                    wait(pe, strips_out, g.strip(i, s) - 1)
                    for c in range(n):
                        product(g, i, j, pair(s % 2), lambda k: rhs(CK * c + k), c == 0, c == n - 1)
                        j += 1

            def down(g, i):
                for j in range(4):
                    def rhs(k):
                        if isinstance(i, int):
                            return Fh[:, CK * i + k, :], Fl[:, CK * i + k, :]
                        return (Fh[:, bass.ds(CK * i + k, 1), :].rearrange("p a n -> p (a n)"),
                                Fl[:, bass.ds(CK * i + k, 1), :].rearrange("p a n -> p (a n)"))
                    product(g, i, j, pair(j), rhs, isinstance(i, int) and i == 0, isinstance(i, int) and i == g.bodies - 1)

            def downs(g, n):
                pe.wait_ge(ffn_split, n * (FF // CN))
                pe.wait_ge(strips_out, g.sbase)
                down(g, 0)
                with pe.Fori(1, g.bodies - 1) as i:
                    down(g, i)
                down(g, g.bodies - 1)

            norm_sums(0)
            pe.wait_ge(h_ready, 1)
            loops(pe, in1, lambda i: body(in1, i))

            pe.wait_ge(strips_out, in1.sbase + in1.ns * in1.bodies)
            for k in range(KT):
                last = mm(bank(7)[0:H, 0:T], wf[:, k, :], Hr[:, k, :], start=(k == 0), stop=(k == KT - 1))
            last.then_inc(f_logits, 1)
            v = proj[:, 4 * NT:5 * NT, :]
            for h in range(H):
                for t in range(2):
                    last = tr(bank(h // 2)[:, (2 * (h % 2) + t) * P:(2 * (h % 2) + t + 1) * P],
                              v[:, h, t * P:(t + 1) * P], ident[:])
                if h % 2:
                    last.then_inc(v_turned, 1)
            pe.wait_ge(mw_landed, 48)
            pe.wait_ge(pool_in, 1)
            pe.wait_ge(f_rows, 1)
            for g in range(4):
                for d in range(2):
                    for c in range(2):
                        last = mm(bank(4 + g)[:, d * T:(d + 1) * T], w_pl[:, g, c, d * P:(d + 1) * P],
                                  t1[:, 2 * g + c, :], start=(d == 0 and c == 0), stop=(c == 1), skip_group_check=True)
                last.then_inc(pool_mm, 1)
            pe.wait_ge(v_tok, 4)
            pe.wait_ge(conv_u, 1)
            for w, b0 in ((w_rg, 0), (w_ig, 4)):
                if b0:
                    pe.wait_ge(pool_out, 4)
                for n in range(NT):
                    last = mm(bank(b0 + n // 2)[:, (n % 2) * T:(n % 2 + 1) * T], w[:, n, :], t1b[:, n, :],
                              start=(n % 2 == 0), stop=True, skip_group_check=True)
                    if n % 2:
                        last.then_inc(gates_mm, 1)
            q, kk = proj[:, 2 * NT:3 * NT, :], proj[:, 3 * NT:4 * NT, :]

            def scores(h):
                if h == 0:
                    pe.wait_ge(q_scaled, 1)
                    pe.wait_ge(f_rows, 3)
                    pe.wait_ge(i_sig, NT)
                if h >= 2:
                    pe.wait_ge(sc_exp, h - 1)
                s = bank(4 + h % 2)
                for t in range(2):
                    n, o = (t + 1) * P, t * P
                    dst = s[:, t * P:t * P + n]
                    mm(dst, q[:, h, o:o + P], kk[:, h, 0:n], start=(t == 0), stop=False, skip_group_check=True)
                    mm(dst, fmask[:, h, o:o + P], ones8[:, 0:n], start=False, stop=False, skip_group_check=True)
                    mm(dst, selrow[:, h, :], neg_f[:, 0:n], start=False, stop=False, skip_group_check=True)
                    last = mm(s[:, t * P + o:t * P + n], ident[:], causal[:], start=False, stop=True, skip_group_check=True)
                last.then_inc(sc_mm, 1)

            def turn(h):
                pe.wait_ge(sc_p, h + 1)
                if h >= 2:
                    pe.wait_ge(sc_pt, h - 1)
                for b in range(3):
                    last = tr(bank(6 + h % 2)[:, b * P:(b + 1) * P], probs[:, h % 2, b * P:(b + 1) * P], ident[:])
                last.then_inc(sc_t, 1)

            def mix(h):
                if h == 0:
                    pe.wait_ge(r_sig, NT)
                pe.wait_ge(sc_pt, h + 1)
                if h >= 2:
                    pe.wait_ge(sc_y, h - 1)
                o, c = bank(2 + h % 2), slice(h * P, (h + 1) * P)
                mm(o[:, 0:P], vtok[:, 0, c], probsT[:, h % 2, 0:P], start=True, stop=True, skip_group_check=True)
                mm(o[:, P:T], vtok[:, 0, c], probsT[:, h % 2, P:2 * P], start=False, stop=False, skip_group_check=True)
                mm(o[:, P:T], vtok[:, 1, c], probsT[:, h % 2, 2 * P:3 * P], start=False, stop=True,
                   skip_group_check=True).then_inc(sc_o, 1)

            for h in range(H + 2):
                if h < H:
                    scores(h)
                if 1 <= h <= H:
                    turn(h - 1)
                if h >= 2:
                    mix(h - 2)
            pe.wait_ge(y_ready, 3)
            loops(pe, mer, lambda i: body(mer, i))
            pe.wait_ge(merged_ready, 1)
            loops(pe, wo1, lambda i: body(wo1, i))
            norm_sums(1)
            pe.wait_ge(h_ready, 2)
            loops(pe, up1, lambda i: body(up1, i))
            downs(dn1, 1)
            norm_sums(2)
            norm_sums(3)
            pe.wait_ge(h_ready, 4)
            loops(pe, in2, lambda i: body(in2, i))
            pe.wait_ge(strips_out, in2.sbase + in2.ns * in2.bodies)
            pe.wait_ge(S("lora_w_landed"), 32)
            for b, o, m, c in ((0, 0, P, 0), (0, T, P, P), (1, 0, 32, 2 * P)):
                for k in range(KT):
                    mm(bank(b)[0:m, o:o + T], w_lora[:, k, c:c + m], Hr[:, k, :], start=(k == 0 and o == 0),
                       stop=(k == KT - 1), skip_group_check=True)
            for o, c in ((0, 0), (T, H)):
                for k in range(KT):
                    last = mm(bank(2)[0:H, o:o + T], w_ab[:, k, c:c + H], Hr[:, k, :], start=(k == 0 and o == 0),
                              stop=(k == KT - 1), skip_group_check=True)
            last.then_inc(step("lora_mm"), 1)
            pe.wait_ge(S("ups_landed"), 64)
            pe.wait_ge(*at_step("lora_act"))
            pe.wait_ge(*at_step("ab_out"))
            for b0, r, name in ((0, 0, "zw_mm"), (4, 64, "za_mm")):
                for n in range(NT):
                    last = mm(bank(b0 + n // 2)[:, (n % 2) * T:(n % 2 + 1) * T], w_upa[r:r + 64, n * P:(n + 1) * P],
                              lp[r:r + 64, 0, :], start=(n % 2 == 0), stop=True, skip_group_check=True)
                last.then_inc(step(name), 1)
            pe.wait_ge(*at_step("ld_out"))
            for n in range(NT):
                o = bank(n // 2)[:, (n % 2) * T:(n % 2 + 1) * T]
                mm(o, w_gu[:, 0, n * P:(n + 1) * P], lp[:, 1, :], start=(n % 2 == 0), stop=False, skip_group_check=True)
                last = mm(o, w_gu[0:32, 1, n * P:(n + 1) * P], lp[0:32, 2, :], start=False, stop=True, skip_group_check=True)
            last.then_inc(step("g_mm"), 1)

            def head_sums(src, b0, m):
                for n in range(NT):
                    last = mm(bank(b0 + n // 2)[:, (n % 2) * T:(n % 2 + 1) * T], m[:], src[:, n, :], start=(n % 2 == 0),
                              stop=True, skip_group_check=True)
                return last

            pe.wait_ge(*at_step("reset_built"))
            pe.wait_ge(*at_step("kk_sq"))
            pe.wait_ge(*at_step("a_out"))
            head_sums(bonus, 4, head_ones).then_inc(step("kk_sum"), 1)
            pe.wait_ge(*at_step("rk"))
            pe.wait_ge(*at_step("g_out"))
            head_sums(bt_f, 0, head_ones).then_inc(step("rk_sum"), 1)

            def inverse(call, lv, nt, x, xt, z):
                base = sum(4 * n for n in INV_LEVELS[:call])
                xb = base + 4 * call
                for k, n in enumerate(lv):
                    for b in range(4):
                        pe.wait_ge(S("inv_x_out"), xb + 4 * k + b + 1)
                        for u in range(4):
                            last = mm(bank(b)[:, u * P:(u + 1) * P], nt[:, 4 * b + u, :], x[:, 4 * b + u, :],
                                      start=(u == 0), stop=True, skip_group_check=True)
                        last.then_inc(S("inv_z"), 1)
                    for b in range(4):
                        pe.wait_ge(S("inv_z_out"), base + 4 * k + b + 1)
                        if b >= 2:
                            pe.wait_ge(S("inv_x_out"), xb + 4 * (k + 1) + b - 1)
                        for o in range(2):
                            for u in range(4):
                                i = 4 * b + u
                                last = mm(bank(4 + 2 * (b % 2) + o)[:, u * P:(u + 1) * P], z[:, i, :] if o else xt[:, i, :],
                                          xt[:, i, :] if o else z[:, i, :], start=(u == 0), stop=True, skip_group_check=True)
                        last.then_inc(S("inv_x"), 1)
                pe.wait_ge(S("inv_x_out"), xb + 4 * (len(lv) + 1))

            pe.wait_ge(*at_step("rw_fm"))
            for cp in range(2):
                tk = slice(cp * P, (cp + 1) * P)
                if cp:
                    pe.wait_ge(S("rw_state"), 3)
                    pe.wait_ge(S("rw_y_out"), 2)
                for m, src in enumerate((at_f, bt_f, Kw, Vw)):
                    for n in range(NT):
                        last = tr(bank(2 * m + n // 4)[:, (n % 4) * P:(n % 4 + 1) * P], src[:, n, tk], ident[:])
                    last.then_inc(S("rw_tok"), 1)
                pe.wait_ge(S("rw_tok_out"), 4 * cp + 4)
                q = 0
                for b in range(4):
                    for m, (l, r) in enumerate(((at_f, bt_f), (bt_f, at_f), (Kw, at_f), (bt_f, Rw), (Kw, Rw))):
                        wait(pe, S("rw_gram_out"), 20 * cp + q - 7)
                        for u in range(4):
                            n, h = (4 * b + u) % 8, 64 * (b // 2)
                            last = mm(bank(q % 8)[:, u * P:(u + 1) * P], l[h:h + 64, n, tk], r[h:h + 64, n, tk],
                                      start=(u == 0), stop=True, skip_group_check=True)
                        last.then_inc(S("rw_gram"), 1)
                        q += 1
                pe.wait_ge(S("rw_gram_out"), 20 * (cp + 1))
                inverse(cp, range(1, 6), nt_r, x_r, xt_r, z_r)
                for x in range(16):
                    last = mm(bank(x // 8)[:, (x % 8) * 64:(x % 8 + 1) * 64], akt[:, x, :], v_tok2[:, hc(x)],
                              start=(x % 8 == 0), stop=True, skip_group_check=True)
                last.then_inc(S("rw_z1"), 1)
                for x in range(16):
                    n = x % 8
                    last = mm(bank(2 + n // 4)[hr(x), (n % 4) * P:(n % 4 + 1) * P], at_tok[:, hc(x)],
                              xt_r[:, x, :], start=(n % 4 == 0), stop=True, skip_group_check=True)
                last.then_inc(S("rw_wt"), 1)
                pe.wait_ge(S("rw_z1_out"), cp + 1)
                for x in range(16):
                    last = mm(bank(4 + x // 8)[:, (x % 8) * 64:(x % 8 + 1) * 64], xt_r[:, x, :], z1[:, x * 64:(x + 1) * 64],
                              start=(x % 8 == 0), stop=True, skip_group_check=True)
                last.then_inc(S("rw_uv"), 1)
                pe.wait_ge(S("rw_wt_out"), cp + 1)
                pe.wait_ge(S("rw_uv_out"), cp + 1)
                for c in range(2):
                    g = 2 * cp + c
                    tp, tc = slice(64 * c, 64 * c + 64), slice(g * CH, (g + 1) * CH)
                    pe.wait_ge(S("rw_state"), g + 1)
                    for x in range(16):
                        last = mm(bank(6 + x // 8)[tp, (x % 8) * 64:(x % 8 + 1) * 64], wt[hr(x), x % 8, tp],
                                  state[hr(x), x % 8, :], start=(x % 8 == 0), stop=True, skip_group_check=True)
                    last.then_inc(S("rw_u_mm"), 1)
                    for x in range(16):
                        n = x % 8
                        last = mm(bank(c)[hr(x), n * 64:(n + 1) * 64], state[hr(x), n, :], Rw[hr(x), n, tc],
                                  start=(n == 0), stop=False, skip_group_check=True)
                    last.then_inc(S("rw_y0_mm"), 1)
                    pe.wait_ge(S("rw_u"), g + 1)
                    for x in range(16):
                        o = bank(2 + c)[hr(x), (x % 8) * 64:(x % 8 + 1) * 64]
                        mm(o, bt_tok[tp, hc(x)], u_tok[tp, x * 64:(x + 1) * 64], start=(x % 8 == 0), stop=False,
                           skip_group_check=True)
                        last = mm(o, kt_tok[tp, hc(x)], v_tok2[tp, hc(x)], start=False, stop=True, skip_group_check=True)
                    last.then_inc(S("rw_s_mm"), 1)
                    pe.wait_ge(S("rw_y0_mm"), g + 1)
                    for x in range(16):
                        o = bank(c)[hr(x), (x % 8) * 64:(x % 8 + 1) * 64]
                        mm(o, u_tok[tp, x * 64:(x + 1) * 64], rbt[tp, x, tp], start=False, stop=False,
                           skip_group_check=True)
                        last = mm(o, v_tok2[tp, hc(x)], rkt[tp, x, tp], start=False, stop=True, skip_group_check=True)
                    last.then_inc(S("rw_y_mm"), 1)
            pe.wait_ge(S("rw_y_out"), 4)
            pe.wait_ge(S("rw_state"), 5)
            head_sums(y_rw, 0, head_ones).then_inc(step("gn_mean"), 1)
            pe.wait_ge(*at_step("gn_sq"))
            head_sums(gn_sq, 4, head_ones).then_inc(step("gn_var"), 1)

            pe.wait_ge(*at_step("gn_out"))
            pe.wait_ge(*at_step("gd_cum"))
            for c in range(2):
                tk = slice(c * P, (c + 1) * P)
                mm(bank(0)[:, c * H:(c + 1) * H], gn[4][:, tk], ident[0:H, 0:H], start=(c == 0), stop=True,
                   skip_group_check=True)
                mm(bank(0)[:, (2 + c) * H:(3 + c) * H], gb[:, tk], ident[0:H, 0:H], start=False, stop=True,
                   skip_group_check=True)
            mm(bank(0)[:, 4 * H:5 * H], gn[7][:, 0:P], ident[0:H, 0:H], start=False, stop=False, skip_group_check=True)
            mm(bank(0)[:, 4 * H:5 * H], gn[5][:, 0:P], ident[0:H, 0:H], start=False, stop=True,
               skip_group_check=True).then_inc(step("gd_tok"), 1)
            pe.wait_ge(*at_step("gd_sq"))
            head_sums(l2s, 4, ones).then_inc(step("gd_l2"), 1)
            pe.wait_ge(*at_step("gd_qk"))
            pe.wait_ge(*at_step("gd_tok_out"))
            for c in range(2):
                tk = slice(c * P, (c + 1) * P)
                for b, src in ((0, cv[:, 4:8]), (2, cv[:, 0:4])):
                    for h in range(4):
                        last = mm(bank(b + c)[:, h * P:(h + 1) * P], cv[:, 4 + h, tk], src[:, h, tk], start=(h == 0),
                                  stop=True, skip_group_check=True)
            last.then_inc(step("gd_gram"), 1)
            pe.wait_ge(*at_step("gd_rows"))
            pe.wait_ge(*at_step("selrow2_built"))
            for o in range(2):
                for c in range(2):
                    tk = slice(c * P, (c + 1) * P)
                    for b in range(2):
                        B = 4 + 2 * c + b
                        if o:
                            pe.wait_ge(S("gd_gam"), 2 * c + b + 1)
                        for u in range(4):
                            h, dst = 4 * b + u, bank(B)[:, u * P:(u + 1) * P]
                            mm(dst, (ngm if o else gm)[:, h, tk], ones8[:, 0:P], start=(u == 0), stop=False, skip_group_check=True)
                            mm(dst, selrow2[:, h, :], gn[4 if o else 5][:, tk], start=False, stop=False, skip_group_check=True)
                            last = mm(dst, ident[:], neg_ui[:] if o else neg_ls[:], start=False, stop=True,
                                      skip_group_check=True)
                        last.then_inc(S("gd_diff"), 1)
            pe.wait_ge(*at_step("gd_n"))
            pe.wait_ge(S("gd_gam"), 8)
            for b in range(4):
                for u in range(4):
                    last = tr(bank(4 + b)[:, u * P:(u + 1) * P], x_g[:, 4 * b + u, :], ident[:])
                last.then_inc(S("gd_nt"), 1)
            pe.wait_ge(S("inv_x_out"), 4 * (5 + 5) + 4 * 2 + 4)
            inverse(2, range(1, 7), nt_g, x_g, xt_g, z_g)
            for m in range(4):
                for u in range(4):
                    last = tr(bank(m)[:, u * P:(u + 1) * P], cv[:, 8 + 4 * (m % 2) + u, (m // 2) * P:(m // 2 + 1) * P], ident[:])
                last.then_inc(S("gd_v_t"), 1)
            for c in range(2):
                for u in range(4):
                    last = tr(bank(4 + c)[:, u * P:(u + 1) * P], cv[:, 4 + u, c * P:(c + 1) * P], ident[:])
                last.then_inc(S("gd_k_t"), 1)
            for b in range(4):
                pe.wait_ge(S("gd_v_beta"), 4)
                for u in range(4):
                    last = mm(bank(b)[:, u * P:(u + 1) * P], xt_g[:, 4 * b + u, :], v_beta[:, 4 * b + u, :], start=(u == 0),
                              stop=True, skip_group_check=True)
                last.then_inc(S("gd_u"), 1)
            pe.wait_ge(*at_step("gd_k_bg"))
            for h in range(H):
                last = mm(bank(4 + h // 4)[:, (h % 4) * P:(h % 4 + 1) * P], k_bg[:, 8 + h, :], xt_g[:, 8 + h, :],
                          start=(h % 4 == 0), stop=True, skip_group_check=True)
            last.then_inc(step("gd_w"), 1)
            pe.wait_ge(S("gd_u_out"), 4)
            for h in range(H):
                last = mm(bank(6 + h // 4)[:, (h % 4) * P:(h % 4 + 1) * P], k_g[:, h, :], u_g[:, h, :],
                          start=(h % 4 == 0), stop=True, skip_group_check=True)
            last.then_inc(step("gd_s"), 1)
            for h in range(H):
                last = mm(bank(h // 4)[:, (h % 4) * P:(h % 4 + 1) * P], selrow2[:, h, :], gn[6][:, P:T],
                          start=(h % 4 == 0), stop=True, skip_group_check=True)
            last.then_inc(step("gd_eg"), 1)
            pe.wait_ge(*at_step("gd_w_out"))
            pe.wait_ge(*at_step("gd_s_out"))
            for h in range(H):
                last = mm(bank(4 + h // 4)[:, (h % 4) * P:(h % 4 + 1) * P], w_g[:, h, :], s_g[:, h, :],
                          start=(h % 4 == 0), stop=True, skip_group_check=True)
            last.then_inc(step("gd_ws"), 1)
            pe.wait_ge(*at_step("gd_qg"))
            pe.wait_ge(*at_step("gd_vn"))
            for h in range(H):
                b = bank(h // 2)
                o = (h % 2) * T
                mm(b[:, o:o + P], u_g[:, h, :], aqk[:, h, :], start=(h % 2 == 0), stop=True, skip_group_check=True)
                mm(b[:, o + P:o + T], s_g[:, h, :], q_g[:, h, :], start=False, stop=False, skip_group_check=True)
                last = mm(b[:, o + P:o + T], v_new[:, h, :], aqk[:, 8 + h, :], start=False, stop=True, skip_group_check=True)
            last.then_inc(step("gd_o"), 1)
            pe.wait_ge(*at_step("gd_o_sq"))
            head_sums(o_sq, 4, ones).then_inc(step("gd_o_sum"), 1)
            pe.wait_ge(*at_step("y2_split"))
            loops(pe, wo2, lambda i: body(wo2, i))
            norm_sums(4)
            pe.wait_ge(h_ready, 5)
            loops(pe, up2, lambda i: body(up2, i))
            downs(dn2, 2)
            norm_sums(5)
            pe.wait_ge(h_ready, 6)
            for n in range(8):
                t, b = n % 2, n // 2
                for k in range(4):
                    last = tr(bank(n)[:, k * P:(k + 1) * P], Hr[:, 4 * b + k, t * P:(t + 1) * P], ident[:])
                last.then_inc(out_turned, 1)

        @block.scalar
        def _(act):
            settle = settler(act, "scalar")
            A = nc.scalar.activation
            for b in range(0, 8, 2):
                act.wait_ge(x_turned, b + 1)
                A(X[:, 2 * b:2 * b + 2, :].rearrange("p k n -> p (k n)"), bank(b), ACT.Copy).then_inc(x_ready, 1)

            def squares(n, s, ready):
                act.wait_ge(s, ready)
                A(SQ[:], X[:], ACT.Square).then_inc(n_sq, 1)
                act.wait_ge(n_mean, n + 1)
                A(rstd[:], rstd[:], ACT.Sqrt).then_inc(n_root, 1)

            def split(g, i, out_of):
                for j in range(g.per):
                    act.wait_ge(landed[j % g.ring], g.landed(i, j))
                    wait(act, chunks_used, g.chunk(i, j) - g.hi + 1)
                    A(hi[g.hi][j % g.hi][:], raw[j % g.ring][:], ACT.Copy).then_inc(hi_ready, 1)
                    if j == 0 and not (isinstance(i, int) and i == 0):
                        out_of(i - 1, g.ns - 1)
                    elif j - 1 in g.ends and j:
                        out_of(i, g.ends[j - 1])

            def splits(g, out_of, last=None):
                loops(act, g, lambda i: split(g, i, out_of), last)
                if last is None:
                    out_of(g.bodies - 1, g.ns - 1)

            def strip_done(e, g, i, s):
                end = [j for j in g.ends if g.ends[j] == s][0]
                e.wait_ge(chunks_used, g.chunk(i, end) + 1)

            def to_proj(i, s):
                strip_done(act, in1, i, s)
                A(proj[:, bass.ds(i * 8 + s * 4, 4), :], pair(s % 2), ACT.Copy).then_inc(strips_out, 1)

            def nothing(i, s):
                pass

            squares(0, x_ready, 8)
            splits(in1, to_proj)

            def sp_e(n, x):
                act.wait_ge(sp_abs, n + 1)
                A(x, x, ACT.Exp, scale=-1.0).then_inc(sp_exp, 1)

            sp_e(0, spt[1][:])
            sp_e(1, fT[1][:])
            for b in range(4):
                act.wait_ge(v_turned, b + 1)
                A(vtok[:, :, 2 * b * P:2 * (b + 1) * P].rearrange("p t (h c) -> p h t c", h=2),
                  bank(b).rearrange("p (h t c) -> p h t c", h=2, t=2), ACT.Copy).then_inc(v_tok, 1)
            for b0, name, dst, done in ((0, "b_rg", rx, r_sig), (4, "b_ig", t2, i_sig)):
                for n in range(NT):
                    act.wait_ge(gates_mm, b0 + n // 2 + 1)
                    A(dst[:, n, :], bank(b0 + n // 2)[:, (n % 2) * T:(n % 2 + 1) * T], ACT.Sigmoid,
                      bias=pcol(name, n)).then_inc(done, 1)
            A(t4b[:], ry, ACT.Square).then_inc(gelu_sq, 1)
            act.wait_ge(gelu_arg, 1)
            A(t4b[:], t4b[:], ACT.Sigmoid, scale=1.5957691216057308).then_inc(gelu_sig, 1)
            act.wait_ge(lam_ready, 1)
            act.wait_ge(r_sig, NT)
            for n in range(NT):
                A(t3[:, n, :], rx[:, n, :], ACT.Exp, scale=lam8[:, n:n + 1]).then_inc(lru_a, 1)
            for n in range(NT):
                last = A(rx[:, n, :], rx[:, n, :], ACT.Tanh, scale=lam8[:, n:n + 1])
            last.then_inc(lru_th, 1)
            act.wait_ge(lru_a, NT)
            act.wait_ge(lru_iu, 1)
            A(t2[:], t3[:], ACT.Square).then_inc(lru_sq, 1)
            act.wait_ge(lru_var, 1)
            A(rx, rx, ACT.Sqrt).then_inc(lru_root, 1)

            def soft(h):
                act.wait_ge(sc_max, h + 1)
                if h >= 2:
                    act.wait_ge(sc_t, h - 1)
                b = bank(4 + h % 2)
                z = 2 * (h % 2)
                A(probs[:, h % 2, 0:P], b[:, 0:P], ACT.Exp, bias=neg_max[:, z:z + 1], accum_out=rowsum[:, z:z + 1])
                A(probs[:, h % 2, P:3 * P], b[:, P:3 * P], ACT.Exp, bias=neg_max[:, z + 1:z + 2],
                  accum_out=rowsum[:, z + 1:z + 2]).then_inc(sc_exp, 1)

            def turned(h):
                act.wait_ge(sc_t, h + 1)
                if h >= 2:
                    act.wait_ge(sc_o, h - 1)
                A(probsT[:, h % 2, :], bank(6 + h % 2)[:, 0:3 * P], ACT.Copy).then_inc(sc_pt, 1)

            for h in range(H + 1):
                if h < H:
                    soft(h)
                if h >= 1:
                    turned(h - 1)

            def gate(i, s):
                if s % 2 == 0:
                    strip_done(act, mer, i, s)
                    wait(act, strips_out, mer.strip(i, s))
                    A(sg[:], pair(0), ACT.Sigmoid).then_inc(gate_sig, 1)
            splits(mer, gate)
            splits(wo1, nothing)
            squares(1, strips_out, wo1.sbase + wo1.ns * wo1.bodies)

            def ffn_gate(i, s):
                if s == 0:
                    strip_done(act, up1, i, s)
                    wait(act, strips_out, up1.strip(i, 0))
                    A(act_gate[:], pair(0), ACT.Sigmoid).then_inc(ffn_sig, 1)
            splits(up1, ffn_gate)
            splits(dn1, nothing)
            squares(2, x_ready, 9)
            squares(3, h_ready, 3)

            def to_proj2(i, s):
                strip_done(act, in2, i, s)
                A(proj2[:, bass.ds(i * 8 + s * 4, 4), :], pair(s % 2), ACT.Copy).then_inc(strips_out, 1)

            splits(in2, to_proj2)
            act.wait_ge(*at_step("lora_mm"))
            A(lp[:, 0:2, :].rearrange("p k n -> p (k n)"), bank(0), ACT.Copy)
            A(lp[0:32, 2, :], bank(1)[0:32, 0:T], ACT.Copy).then_inc(step("lora_out"), 1)
            act.wait_ge(*at_step("lora_in"))
            A(lp[0:64, 0, :], lp[0:64, 0, :], ACT.Tanh)
            A(lp[:, 1, :], lp[:, 1, :], ACT.Sigmoid)
            A(lp[0:32, 2, :], lp[0:32, 2, :], ACT.Sigmoid).then_inc(step("lora_act"), 1)
            for b0, dst, bias, got, done in ((0, ld, "rwkv_w0_2", "zw_mm", "ld_out"), (4, a_lr, "rwkv_a0_2", "za_mm", "a_out")):
                act.wait_ge(*at_step(got))
                for n in range(NT):
                    last = A(dst[:, n, :], bank(b0 + n // 2)[:, (n % 2) * T:(n % 2 + 1) * T], ACT.Sigmoid, bias=pcol(bias, n))
                last.then_inc(step(done), 1)
            act.wait_ge(*at_step("g_mm"))
            for b in range(4):
                last = A(gate2[:, 2 * b:2 * b + 2, :].rearrange("p k n -> p (k n)"), bank(b), ACT.Copy)
            last.then_inc(step("g_out"), 1)
            act.wait_ge(*at_step("kk"))
            A(bonus[:], kk[:], ACT.Square).then_inc(step("kk_sq"), 1)
            act.wait_ge(*at_step("kk_mean"))
            A(at_f[:], at_f[:], ACT.Sqrt).then_inc(step("kk_root"), 1)
            act.wait_ge(*at_step("l_prev"))
            A(ld[:], ld[:], ACT.Exp).then_inc(step("e_prev"), 1)
            act.wait_ge(*at_step("at_made"))
            A(ld[:], cum[:], ACT.Exp).then_inc(step("e_plus"), 1)
            A(cum[:], cum[:], ACT.Exp, scale=-1.0).then_inc(step("e_minus"), 1)
            for cp in range(2):
                for m, dst in enumerate((at_tok, bt_tok)):
                    act.wait_ge(S("rw_tok"), 4 * cp + m + 1)
                    A(dst[:], psum[:, 2 * m:2 * m + 2, :].rearrange("p b n -> p (b n)"), ACT.Copy).then_inc(S("rw_tok_out"), 1)
                act.wait_ge(S("rw_z1"), cp + 1)
                A(z1[:], psum[:, 0:2, :].rearrange("p b n -> p (b n)"), ACT.Copy).then_inc(S("rw_z1_out"), 1)
                act.wait_ge(S("rw_wt"), cp + 1)
                A(wt[:].rearrange("p k n -> p (k n)"), psum[:, 2:4, :].rearrange("p b n -> p (b n)"), ACT.Copy).then_inc(S("rw_wt_out"), 1)
                act.wait_ge(S("rw_uv"), cp + 1)
                A(uv[:], psum[:, 4:6, :].rearrange("p b n -> p (b n)"), ACT.Copy).then_inc(S("rw_uv_out"), 1)
                for c in range(2):
                    g = 2 * cp + c
                    act.wait_ge(S("rw_y_mm"), g + 1)
                    A(y_rw[:, :, g * CH:(g + 1) * CH], bank(c).rearrange("p (k n) -> p k n", k=NT), ACT.Copy).then_inc(S("rw_y_out"), 1)
            act.wait_ge(*at_step("gn_c"))
            A(gn_sq[:], y_rw[:], ACT.Square).then_inc(step("gn_sq"), 1)
            act.wait_ge(*at_step("gn_m"))
            A(gn_r[:], gn_r[:], ACT.Sqrt).then_inc(step("gn_root"), 1)
            act.wait_ge(*at_step("gd_cv"))
            A(cv_s[:], cv[:], ACT.Sigmoid).then_inc(step("gd_cv_sig"), 1)
            A(gb[:], gb[:], ACT.Sigmoid).then_inc(step("gd_beta"), 1)
            sp_e(2, gn[1][:])
            A(alog[:], alog[:], ACT.Exp).then_inc(step("gd_expA"), 1)
            act.wait_ge(*at_step("gd_cum"))
            A(gn[6][:], gn[4][:], ACT.Exp).then_inc(S("gd_eg_rows"), 1)
            act.wait_ge(*at_step("gd_silu"))
            A(l2s[:], cv[:, 0:8, :], ACT.Square).then_inc(step("gd_sq"), 1)
            act.wait_ge(*at_step("gd_l2_mean"))
            A(l2s[:], l2s[:], ACT.Sqrt).then_inc(step("gd_l2_root"), 1)
            act.wait_ge(*at_step("gd_tok_out"))
            A(tokp[:, 4:6, :], tokp[:, 0:2, :], ACT.Exp)
            A(tokp[:, 6, :], tokp[:, 6, :], ACT.Exp).then_inc(step("gd_tok_exp"), 1)
            for o in range(2):
                for k in range(4):
                    act.wait_ge(S("gd_diff"), 4 * o + k + 1)
                    A((gam_t if o else gam)[:, 4 * k:4 * k + 4, :].rearrange("p k n -> p (k n)"), bank(4 + k), ACT.Exp).then_inc(S("gd_gam"), 1)
            for k in range(4):
                act.wait_ge(S("gd_nt"), k + 1)
                A(nt_g[:, 4 * k:4 * k + 4, :].rearrange("p k n -> p (k n)"), bank(4 + k), ACT.Copy).then_inc(S("gd_nt_out"), 1)
            for m in range(4):
                act.wait_ge(S("gd_v_t"), m + 1)
                for u in range(4):
                    h, c = 4 * (m % 2) + u, m // 2
                    last = A(v_beta[:, 8 * c + h, :], bank(m)[:, u * P:(u + 1) * P], ACT.Copy, scale=tokp[:, 2 + c, h:h + 1])
                last.then_inc(S("gd_v_beta"), 1)
            for b in range(4):
                act.wait_ge(S("gd_u"), b + 1)
                A(u_g[:, 4 * b:4 * b + 4, :].rearrange("p k n -> p (k n)"), bank(b), ACT.Copy).then_inc(S("gd_u_out"), 1)
            act.wait_ge(*at_step("gd_w"))
            A(w_g[:].rearrange("p k n -> p (k n)"), psum[:, 4:6, :].rearrange("p b n -> p (b n)"), ACT.Copy).then_inc(step("gd_w_out"), 1)
            act.wait_ge(*at_step("gd_s"))
            A(s_g[:].rearrange("p k n -> p (k n)"), psum[:, 6:8, :].rearrange("p b n -> p (b n)"), ACT.Copy).then_inc(step("gd_s_out"), 1)
            act.wait_ge(*at_step("gd_o"))
            for b in range(4):
                last = A(o_g[:, 2 * b:2 * b + 2, :].rearrange("p k n -> p (k n)"), bank(b), ACT.Copy)
            last.then_inc(step("gd_o_out"), 1)
            act.wait_ge(*at_step("gd_o_out"))
            A(o_sq[:], o_g[:], ACT.Square).then_inc(step("gd_o_sq"), 1)
            A(z_sig[:], proj2[:, 40:48, :], ACT.Sigmoid).then_inc(step("gd_z_sig"), 1)
            act.wait_ge(*at_step("gd_o_mean"))
            A(o_r[:], o_r[:], ACT.Sqrt).then_inc(step("gd_o_root"), 1)
            splits(wo2, nothing)
            squares(4, strips_out, wo2.sbase + wo2.ns * wo2.bodies)

            def ffn_gate2(i, s):
                if s == 0:
                    strip_done(act, up2, i, s)
                    wait(act, strips_out, up2.strip(i, 0))
                    A(act_gate[:], pair(0), ACT.Sigmoid).then_inc(ffn_sig, 1)
            splits(up2, ffn_gate2)
            splits(dn2, nothing)
            squares(5, x_ready, 10)
            for n in range(0, 8, 2):
                act.wait_ge(out_turned, n + 1)
                A(out_tokens[:, n % 2, n // 2 * 512:(n // 2 + 1) * 512], bank(n), ACT.Copy).then_inc(out_copied, 1)

        @block.vector
        def _(dve):
            settle = settler(dve, "vector")
            V = nc.vector
            dve.wait_ge(par_turned, 1)
            V.tensor_copy(par1[:], bank(0)[:, 0:ncols]).then_inc(par_ready, 1)
            for b in range(1, 8, 2):
                dve.wait_ge(x_turned, b + 1)
                V.tensor_copy(X[:, 2 * b:2 * b + 2, :].rearrange("p k n -> p (k n)"), bank(b)).then_inc(x_ready, 1)
            dve.wait_ge(par_ready, 1)

            def norm(n, gain, eps, dst, split=True):
                dve.wait_ge(n_sum, n + 1)
                V.tensor_scalar(rstd[:], bank(7)[:, 0:T], 1.0 / D, eps, ALU.mult, ALU.add).then_inc(n_mean, 1)
                dve.wait_ge(n_root, n + 1)
                settle(V.reciprocal(rstd[:], rstd[:]))
                for k in range(KT):
                    last = V.scalar_tensor_tensor(dst[:, k, :], X[:, k, :], pcol(gain, k), rstd[:], ALU.mult, ALU.mult)
                if split:
                    settle(last)
                    settle(V.tensor_copy(Hh[:], dst[:]))
                    last = V.tensor_tensor(Hl[:], dst[:], Hh[:].bitcast(F32), ALU.subtract)
                last.then_inc(h_ready, 1)

            def split(g, i, out_of):
                for j in range(g.per):
                    dve.wait_ge(hi_ready, g.chunk(i, j) + 1)
                    r = j % g.ring
                    V.tensor_tensor(lo[r][:], raw[r][:], hi[g.hi][j % g.hi][:].bitcast(F32),
                                    ALU.subtract).then_inc(lo_ready, 1)
                    if j == 0 and not (isinstance(i, int) and i == 0):
                        out_of(i - 1, g.ns - 1)
                    elif j - 1 in g.ends and j:
                        out_of(i, g.ends[j - 1])

            def splits(g, out_of, last=None):
                loops(dve, g, lambda i: split(g, i, out_of), last)
                if last is None:
                    out_of(g.bodies - 1, g.ns - 1)

            def strip_done(e, g, i, s):
                end = [j for j in g.ends if g.ends[j] == s][0]
                e.wait_ge(chunks_used, g.chunk(i, end) + 1)

            def nothing(i, s):
                pass

            def softplus(n, z, e, tmp, w2, res):
                V.scalar_tensor_tensor(e, z, -1.0, z, ALU.mult, ALU.max).then_inc(sp_abs, 1)
                dve.wait_ge(sp_exp, n + 1)
                settle(V.tensor_scalar(tmp, e, 2.0, None, ALU.add))
                settle(V.reciprocal(tmp, tmp))
                settle(V.tensor_tensor(tmp, tmp, e, ALU.mult))
                settle(V.tensor_tensor(w2, tmp, tmp, ALU.mult))
                settle(V.tensor_scalar(res, w2, 1.0 / 17, None, ALU.mult))
                for m in range(15, 1, -2):
                    settle(V.scalar_tensor_tensor(res, res, 1.0 / m, w2, ALU.add, ALU.mult))
                settle(V.scalar_tensor_tensor(res, res, 1.0, tmp, ALU.add, ALU.mult))
                settle(V.tensor_scalar(tmp, z, 0.0, None, ALU.max))
                settle(V.scalar_tensor_tensor(res, res, 2.0, tmp, ALU.mult, ALU.add))

            norm(0, "g_mix", EPS1, Hr)
            splits(in1, nothing)

            c0 = col["lru_lambda"]
            settle(V.tensor_scalar(spt[0][:], par1[:, c0:c0 + NT], -1.0, None, ALU.mult))
            softplus(0, spt[0][:], spt[1][:], spt[2][:], spt[3][:], lam8[:])
            V.tensor_scalar(lam8[:], lam8[:], -8.0, None, ALU.mult).then_inc(lam_ready, 1)
            dve.wait_ge(f_logits, 1)
            settle(V.tensor_scalar(fT[0][:], bank(7)[0:H, 0:T], bfor[:], -1.0, ALU.add, ALU.mult))
            V.memset(ones8[:], 1.0).then_inc(f_rows, 1)
            softplus(1, fT[0][:], fT[1][:], fT[2][:], fT[3][:], neg_f[:])
            settle(V.tensor_tensor_scan(fT[0][:], ones8[:], neg_f[:], 0.0, ALU.mult, ALU.subtract))
            V.tensor_scalar(neg_f[:], fT[0][:], -1.0, None, ALU.mult).then_inc(f_rows, 1)
            dve.wait_ge(mix_tables, 1)
            for h in range(H):
                last = V.tensor_scalar(fmask[:, h, :], fT[0][:], ident[0:H, h:h + 1], None, ALU.mult)
            last.then_inc(f_rows, 1)
            dve.wait_ge(strips_out, in1.sbase + in1.ns * in1.bodies)
            qs = proj[:, 2 * NT:3 * NT, :]
            V.tensor_scalar(qs, qs, float(P) ** -0.5, None, ALU.mult).then_inc(q_scaled, 1)
            dve.wait_ge(f_rows, 3)
            pin = proj[:, 5 * NT:6 * NT, :]
            src, lo_t = pin, 0
            for w, dst, n0 in ((1, t1, 0), (2, t2, 2), (4, t3, 4), (8, t4, 6)):
                V.tensor_tensor(dst[:, n0:, w:], src[:, n0:, w:], src[:, n0:, 0:T - w], ALU.add)
                settle(V.tensor_copy(dst[:, n0:, 0:w], src[:, n0:, 0:w]))
                src = dst
            for g, s in enumerate((t1, t2, t3, t4)):
                for n in range(2 * g, 2 * g + 2):
                    last = V.tensor_tensor(t1[:, n, :], s[:, n, :], recip_cnt[:, g, :], ALU.mult)
            settle(last)
            V.tensor_tensor(t1[:], t1[:], pin, ALU.subtract).then_inc(pool_in, 1)
            for g in range(4):
                dve.wait_ge(pool_mm, g + 1)
                for n in range(2 * g, 2 * g + 2):
                    last = V.tensor_scalar(t4[:, n, :], bank(4 + g)[:, (n % 2) * T:(n % 2 + 1) * T],
                                           pcol("pool_scale", n), None, ALU.mult)
                last.then_inc(pool_out, 1)
            for n in range(NT):
                last = V.tensor_scalar(t1b[:, n, :], rx[:, n, :], pcol("conv_w", 3 * NT + n), pcol("conv_b", n),
                                       ALU.mult, ALU.add)
            settle(last)
            for d in range(1, 4):
                for n in range(NT):
                    last = V.scalar_tensor_tensor(t1b[:, n, d:], rx[:, n, 0:T - d], pcol("conv_w", (3 - d) * NT + n),
                                                  t1b[:, n, d:], ALU.mult, ALU.add)
                if d < 3:
                    settle(last)
            last.then_inc(conv_u, 1)
            dve.wait_ge(gelu_sq, 1)
            settle(V.tensor_scalar(t4b[:], t4b[:], 0.044715, 1.0, ALU.mult, ALU.add))
            V.tensor_tensor(t4b[:], t4b[:], ry, ALU.mult).then_inc(gelu_arg, 1)
            dve.wait_ge(i_sig, NT)
            dve.wait_ge(conv_u, 1)
            V.tensor_tensor(t1b[:], t1b[:], t2[:], ALU.mult).then_inc(lru_iu, 1)
            dve.wait_ge(gelu_sig, 1)
            V.tensor_tensor(ry, ry, t4b[:], ALU.mult)
            dve.wait_ge(lru_th, 1)
            dve.wait_ge(lru_sq, 1)
            settle(V.scalar_tensor_tensor(rx, t2[:], 1.0, rx, ALU.add, ALU.mult))
            V.tensor_scalar(rx, rx, -1.0, None, ALU.mult).then_inc(lru_var, 1)
            V.memset(t3[:, :, 0:1], 0.0)
            dve.wait_ge(lru_root, 1)
            settle(V.tensor_tensor(rx, rx, t1b[:], ALU.mult))
            flat = lambda t: t.rearrange("p k n -> p (k n)")
            settle(V.tensor_tensor_scan(flat(t1b[:]), flat(t3[:]), flat(rx), 0.0, ALU.mult, ALU.add))
            settle(V.tensor_tensor(t1b[:], t1b[:], ry, ALU.mult))
            settle(V.tensor_copy(yh[0][:], t1b[:]))
            V.tensor_tensor(yl[0][:], t1b[:], yh[0][:].bitcast(F32), ALU.subtract).then_inc(y_ready, 1)

            def row_max(h):
                dve.wait_ge(sc_mm, h + 1)
                if h >= 2:
                    dve.wait_ge(sc_exp, h - 1)
                b, z = bank(4 + h % 2), 2 * (h % 2)
                V.reduce_max(neg_max[:, z:z + 1], b[:, 0:P], AX_X)
                settle(V.reduce_max(neg_max[:, z + 1:z + 2], b[:, P:3 * P], AX_X))
                V.tensor_scalar(neg_max[:, z:z + 2], neg_max[:, z:z + 2], -1.0, None, ALU.mult).then_inc(sc_max, 1)

            def normalise(h):
                z = 2 * (h % 2)
                dve.wait_ge(sc_exp, h + 1)
                settle(V.reciprocal(rowsum[:, z:z + 2], rowsum[:, z:z + 2]))
                V.tensor_scalar(probs[:, h % 2, 0:P], probs[:, h % 2, 0:P], rowsum[:, z:z + 1], None, ALU.mult)
                V.tensor_scalar(probs[:, h % 2, P:3 * P], probs[:, h % 2, P:3 * P], rowsum[:, z + 1:z + 2], None,
                                ALU.mult).then_inc(sc_p, 1)

            def take(h):
                dve.wait_ge(sc_o, h + 1)
                V.tensor_copy(t2[:, h, :], bank(2 + h % 2)[:, 0:T]).then_inc(sc_y, 1)

            for h in range(H + 2):
                if h < H:
                    row_max(h)
                if 1 <= h <= H:
                    normalise(h - 1)
                if h >= 2:
                    take(h - 2)
            dve.wait_ge(sc_y, H)
            V.tensor_copy(yh[2][:], t4[:])
            settle(V.tensor_copy(yh[1][:], t2[:]))
            V.tensor_tensor(yl[2][:], t4[:], yh[2][:].bitcast(F32), ALU.subtract).then_inc(y_ready, 1)
            V.tensor_tensor(yl[1][:], t2[:], yh[1][:].bitcast(F32), ALU.subtract).then_inc(y_ready, 1)

            def merge(i, s):
                if s % 2 == 0:
                    return
                b = s // 2
                m = merged[:, bass.ds(i * 4, 4), :]
                dst = m if b == 0 else gated[:]
                strip_done(dve, mer, i, s)
                dve.wait_ge(gate_sig, i * 3 + b + 1)
                if b:
                    dve.wait_ge(merged_sum, i * 2 + b)
                V.tensor_tensor(dst, sg[:], pair(1), ALU.mult).then_inc(strips_out, 2)
                if b:
                    dve.wait_ge(strips_out, mer.strip(i, s) + 1)
                    V.tensor_tensor(m, m, gated[:], ALU.add).then_inc(merged_sum, 1)
            V.memset(gated[:, 0:1, 0:1], 0.0).then_inc(merged_sum, 1)
            splits(mer, merge)
            dve.wait_ge(merged_sum, 9)
            settle(V.tensor_copy(Hh[:], merged[:]))
            V.tensor_tensor(Hl[:], merged[:], Hh[:].bitcast(F32), ALU.subtract).then_inc(merged_ready, 1)

            def residual(g):
                def f(i, s):
                    strip_done(dve, g, i, s)
                    r = X[:, bass.ds(8 * i + 4 * s, 4), :]
                    V.tensor_tensor(r, r, pair(s), ALU.add).then_inc(strips_out, 1)
                return f
            splits(wo1, residual(wo1))
            norm(1, "g_ffn", EPS1, Hr)

            def ffn(g, n):
                def f(i, s):
                    strip_done(dve, g, i, s)
                    k = n * g.bodies
                    if s == 0:
                        dve.wait_ge(ffn_sig, k + i + 1)
                        V.tensor_tensor(act_gate[:], act_gate[:], pair(0), ALU.mult).then_inc(strips_out, 1)
                        return
                    dve.wait_ge(strips_out, g.strip(i, 0) + 1)
                    wait(dve, ffn_split, k + i)
                    V.tensor_tensor(act_up[:], act_gate[:], pair(1), ALU.mult).then_inc(strips_out, 1)
                    dve.wait_ge(strips_out, g.strip(i, 1) + 1)
                    fh, fl = Fh[:, bass.ds(4 * i, 4), :], Fl[:, bass.ds(4 * i, 4), :]
                    V.tensor_copy(fh, act_up[:]).then_inc(ffn_hi, 1)
                    dve.wait_ge(ffn_hi, k + i + 1)
                    V.tensor_tensor(fl, act_up[:], fh.bitcast(F32), ALU.subtract).then_inc(ffn_split, 1)
                return f
            splits(up1, ffn(up1, 0))

            def down_out(g):
                for i in range(4):
                    dve.wait_ge(chunks_used, g.end)
                    r = X[:, 4 * i:4 * i + 4, :]
                    last = V.tensor_tensor(r, r, pair(i), ALU.add)
                last.then_inc(x_ready, 1)
            splits(dn1, nothing)
            down_out(dn1)
            norm(2, "g_final", EPS1, X, split=False)
            norm(3, "attn_norm_w_2", EPS2, Hr)
            splits(in2, nothing)
            dve.wait_ge(*at_step("lora_mm"))
            V.tensor_scalar(neg_f[:], bank(2)[0:H, 0:T], dtb[:], None, ALU.add)
            V.tensor_copy(gb[:], bank(2)[0:H, T:2 * T]).then_inc(step("ab_out"), 1)
            dve.wait_ge(*at_step("lora_out"))
            V.tensor_tensor(lpd[:, 0:2, 1:], lp[:, 0:2, 0:T - 1], lp[:, 0:2, 1:], ALU.subtract)
            V.tensor_scalar(lpd[:, 0:2, 0:1], lp[:, 0:2, 0:1], -1.0, None, ALU.mult)
            V.tensor_tensor(lpd[0:32, 2, 1:], lp[0:32, 2, 0:T - 1], lp[0:32, 2, 1:], ALU.subtract)
            settle(V.tensor_scalar(lpd[0:32, 2, 0:1], lp[0:32, 2, 0:1], -1.0, None, ALU.mult))
            for k, m in ((0, P), (1, P), (2, 32)):
                last = V.scalar_tensor_tensor(lp[0:m, k, :], lpd[0:m, k, :], pcol("rwkv_mu_2", 24 + k, m), lp[0:m, k, :],
                                              ALU.mult, ALU.add)
            last.then_inc(step("lora_in"), 1)
            dve.wait_ge(strips_out, in2.sbase + in2.ns * in2.bodies)
            for x in range(3):
                p, d = proj2[:, 8 * x:8 * x + 8, :], shift[x]
                V.tensor_tensor(d[:, :, 1:], p[:, :, 0:T - 1], p[:, :, 1:], ALU.subtract)
                last = V.tensor_scalar(d[:, :, 0:1], p[:, :, 0:1], -1.0, None, ALU.mult)
            settle(last)
            for x in range(3):
                for n in range(NT):
                    p = proj2[:, 8 * x + n, :]
                    last = V.scalar_tensor_tensor(p, shift[x][:, n, :], pcol("rwkv_mu_2", 8 * x + n), p, ALU.mult, ALU.add)
            settle(last)
            for n in range(NT):
                last = V.tensor_scalar(kk[:, n, :], Kw[:, n, :], pcol("rwkv_k_k_2", n), None, ALU.mult)
            last.then_inc(step("kk"), 1)
            dve.wait_ge(*at_step("ld_out"))
            settle(V.tensor_scalar(ld[:], ld[:], -0.6065306597126334, None, ALU.mult))
            dve.wait_ge(*at_step("reset_built"))
            dve.wait_ge(*at_step("za_mm"))
            settle(V.tensor_tensor_scan(flat(cum[:]), flat(reset[:]), flat(ld[:]), 0.0, ALU.mult, ALU.add))
            V.tensor_tensor(ld[:], cum[:], ld[:], ALU.subtract).then_inc(step("l_prev"), 1)
            dve.wait_ge(*at_step("kk_sum"))
            V.tensor_scalar(at_f[:].rearrange("p (b t) n -> p b (t n)", t=2), psum[:, 4:8, :], 1e-12, None, ALU.add).then_inc(step("kk_mean"), 1)
            dve.wait_ge(*at_step("a_out"))
            dve.wait_ge(*at_step("kk_sum"))
            for n in range(NT):
                last = V.tensor_scalar(bonus[:, n, :], a_lr[:, n, :], -1.0, pcol("rwkv_k_a_2", n), ALU.add, ALU.mult)
            settle(last)
            settle(V.scalar_tensor_tensor(Kw, bonus[:], 1.0, Kw, ALU.add, ALU.mult))
            for n in range(NT):
                last = V.scalar_tensor_tensor(bt_f[:, n, :], Rw[:, n, :], pcol("rwkv_r_k_2", n), Kw[:, n, :], ALU.mult, ALU.mult)
            last.then_inc(step("rk"), 1)
            dve.wait_ge(*at_step("kk_root"))
            settle(V.reciprocal(at_f[:], at_f[:]))
            settle(V.tensor_tensor(kk[:], kk[:], at_f[:], ALU.mult))
            V.tensor_tensor(a_lr[:], kk[:], a_lr[:], ALU.mult)
            dve.wait_ge(*at_step("e_prev"))
            V.scalar_tensor_tensor(at_f[:], kk[:], -1.0, ld[:], ALU.mult, ALU.mult).then_inc(step("at_made"), 1)
            dve.wait_ge(*at_step("rk_sum"))
            V.tensor_tensor(bonus[:].rearrange("p (b t) n -> p b (t n)", t=2), psum[:, 0:4, :],
                            Vw.rearrange("p (b t) n -> p b (t n)", t=2), ALU.mult)
            dve.wait_ge(*at_step("e_plus"))
            V.tensor_tensor(Rw, Rw, ld[:], ALU.mult)
            V.tensor_copy(chunk_decay[:], ld[:].rearrange("p k (c t) -> p k c t", t=CH)[:, :, :, CH - 1])
            dve.wait_ge(*at_step("e_minus"))
            V.tensor_tensor(Kw, Kw, cum[:], ALU.mult)
            V.tensor_tensor(bt_f[:], a_lr[:], cum[:], ALU.mult).then_inc(step("rw_fm"), 1)

            def inverse(call, lv, x, xt, z):
                base = sum(4 * n for n in INV_LEVELS[:call])
                for k, n in enumerate(lv):
                    for b in range(4):
                        dve.wait_ge(S("inv_z"), base + 4 * k + b + 1)
                        V.tensor_tensor(z[:, 4 * b:4 * b + 4, :], bank(b).rearrange("p (u n) -> p u n", u=4), bc(low[n], 4),
                                        ALU.mult).then_inc(S("inv_z_out"), 1)
                    for b in range(4):
                        dve.wait_ge(S("inv_x"), base + 4 * k + b + 1)
                        for o in range(2):
                            m = (xt if o else x)[:, 4 * b:4 * b + 4, :]
                            last = V.tensor_tensor(m, m, bank(4 + 2 * (b % 2) + o).rearrange("p (u n) -> p u n", u=4), ALU.add)
                        last.then_inc(S("inv_x_out"), 1)

            for cp in range(2):
                for m, dst in ((2, kt_tok), (3, v_tok2)):
                    dve.wait_ge(S("rw_tok"), 4 * cp + m + 1)
                    V.tensor_copy(dst[:], psum[:, 2 * m:2 * m + 2, :].rearrange("p b n -> p (b n)")).then_inc(S("rw_tok_out"), 1)
                q = 0
                for b in range(4):
                    u = slice(4 * b, 4 * b + 4)

                    def masked(dst, m):
                        dve.wait_ge(S("rw_gram"), 20 * cp + q + 1)
                        return V.tensor_tensor(dst[:, u, :], bank(q % 8).rearrange("p (u n) -> p u n", u=4), bc(m, 4),
                                               ALU.mult).then_inc(S("rw_gram_out"), 1)
                    masked(x_r, low[0])
                    q += 1
                    masked(nt_r, upper_strict)
                    q += 1
                    dve.wait_ge(S("rw_gram_out"), 20 * cp + q)
                    settle(V.tensor_tensor(xt_r[:, u, :], nt_r[:, u, :], bc(low0_t, 4), ALU.mult))
                    V.tensor_tensor(x_r[:, u, :], x_r[:, u, :], bc(ident, 4), ALU.add)
                    V.tensor_tensor(xt_r[:, u, :], xt_r[:, u, :], bc(ident, 4), ALU.add).then_inc(S("inv_x_out"), 1)
                    for dst, m in ((akt, upper_strict), (rbt, upper_incl), (rkt, upper_incl)):
                        masked(dst, m)
                        q += 1
                inverse(cp, range(1, 6), x_r, xt_r, z_r)
                for c in range(2):
                    g, tp = 2 * cp + c, slice(64 * c, 64 * c + 64)
                    dve.wait_ge(S("rw_u_mm"), g + 1)
                    dve.wait_ge(S("rw_uv_out"), cp + 1)
                    V.tensor_tensor(u_tok[tp, :], psum[tp, 6:8, :].rearrange("p b n -> p (b n)"), uv[tp, :], ALU.add).then_inc(S("rw_u"), 1)
                    dve.wait_ge(S("rw_s_mm"), g + 1)
                    settle(V.tensor_tensor(state[:].rearrange("p k n -> p (k n)"), bank(2 + c), state[:].rearrange("p k n -> p (k n)"), ALU.add))
                    V.tensor_tensor(state[:], state[:], chunk_decay[:, :, g:g + 1].to_broadcast([P, NT, 64]), ALU.mult).then_inc(S("rw_state"), 1)
            v4 = lambda t: t.rearrange("p (b t) n -> p b (t n)", t=2)
            dve.wait_ge(*at_step("gn_mean"))
            V.scalar_tensor_tensor(v4(y_rw[:]), psum[:, 0:4, :], -1.0 / 64, v4(y_rw[:]), ALU.mult, ALU.add).then_inc(step("gn_c"), 1)
            dve.wait_ge(*at_step("gn_var"))
            V.tensor_scalar(v4(gn_r[:]), psum[:, 4:8, :], 1.0 / 64, 64e-5, ALU.mult, ALU.add).then_inc(step("gn_m"), 1)
            dve.wait_ge(*at_step("gn_root"))
            settle(V.reciprocal(gn_r[:], gn_r[:]))
            settle(V.tensor_tensor(y_rw[:], y_rw[:], gn_r[:], ALU.mult))
            for n in range(NT):
                last = V.tensor_scalar(y_rw[:, n, :], y_rw[:, n, :], pcol("rwkv_ln_w_2", n), pcol("rwkv_ln_b_2", n), ALU.mult, ALU.add)
            settle(last)
            settle(V.tensor_tensor(y_rw[:], y_rw[:], bonus[:], ALU.add))
            V.tensor_tensor(yfin[:, 0:8, :], y_rw[:], gate2[:], ALU.mult).then_inc(step("gn_out"), 1)
            pq = proj2[:, 24:40, :]
            for n in range(16):
                last = V.tensor_scalar(cv[:, n, :], pq[:, n, :], pcol("gdn_conv_w_2", 48 + n), None, ALU.mult)
            settle(last)
            for d in range(1, 4):
                for n in range(16):
                    last = V.scalar_tensor_tensor(cv[:, n, d:], pq[:, n, 0:T - d], pcol("gdn_conv_w_2", 16 * (3 - d) + n),
                                                  cv[:, n, d:], ALU.mult, ALU.add)
                if d < 3:
                    settle(last)
            last.then_inc(step("gd_cv"), 1)
            dve.wait_ge(*at_step("gd_cv_sig"))
            V.tensor_tensor(cv[:], cv[:], cv_s[:], ALU.mult).then_inc(step("gd_silu"), 1)
            dve.wait_ge(*at_step("gd_silu"))
            settle(V.tensor_copy(gn[0][:], neg_f[:]))
            softplus(2, gn[0][:], gn[1][:], gn[2][:], gn[3][:], gn[4][:])
            dve.wait_ge(*at_step("gd_expA"))
            settle(V.tensor_scalar(gn[5][:], gn[4][:], alog[:], -1.0, ALU.mult, ALU.mult))
            for c in range(2):
                tk = slice(c * P, (c + 1) * P)
                last = V.tensor_tensor_scan(gn[4][:, tk], ones8[:, tk], gn[5][:, tk], 0.0, ALU.mult, ALU.add)
            settle(last)
            V.tensor_scalar(gn[7][:, 0:P], ones8[:, 0:P], gn[4][:, P - 1:P], None, ALU.mult)
            dve.wait_ge(*at_step("gd_beta"))
            V.tensor_scalar(gn[5][:], gn[4][:], -1.0, None, ALU.mult).then_inc(step("gd_cum"), 1)
            dve.wait_ge(*at_step("gd_cum"))
            for h in range(H):
                V.tensor_scalar(gm[:, h, :], gn[4][:], ident[0:H, h:h + 1], None, ALU.mult)
                last = V.tensor_scalar(ngm[:, h, :], gn[5][:], ident[0:H, h:h + 1], None, ALU.mult)
            last.then_inc(step("gd_rows"), 1)
            dve.wait_ge(*at_step("gd_tok"))
            V.tensor_copy(tokp[:, 0:4, :], bank(0)[:, 0:4 * H].rearrange("p (k h) -> p k h", h=H))
            V.tensor_copy(tokp[:, 6, :], bank(0)[:, 4 * H:5 * H]).then_inc(step("gd_tok_out"), 1)
            dve.wait_ge(*at_step("gd_l2"))
            V.tensor_scalar(v4(l2s[:]), psum[:, 4:8, :], 1e-6, None, ALU.add).then_inc(step("gd_l2_mean"), 1)
            dve.wait_ge(*at_step("gd_l2_root"))
            settle(V.reciprocal(l2s[:], l2s[:]))
            V.scalar_tensor_tensor(cv[:, 0:4, :], cv[:, 0:4, :], float(P) ** -0.5, l2s[:, 0:4, :], ALU.mult, ALU.mult)
            V.tensor_tensor(cv[:, 4:8, :], cv[:, 4:8, :], l2s[:, 4:8, :], ALU.mult).then_inc(step("gd_qk"), 1)
            dve.wait_ge(*at_step("gd_tok_exp"))
            V.tensor_tensor(tokp[:, 4:6, :], tokp[:, 4:6, :], tokp[:, 2:4, :], ALU.mult)
            settle(V.tensor_scalar(tokp[:, 0:2, :], tokp[:, 2:4, :], -1.0, None, ALU.mult))
            dve.wait_ge(*at_step("gd_gram"))
            for c in range(2):
                for b in range(2):
                    dve.wait_ge(S("gd_gam"), 2 * c + b + 1)
                    for h in range(4 * b, 4 * b + 4):
                        last = V.scalar_tensor_tensor(x_g[:, 8 * c + h, :], bank(c)[:, (h // 2) * P:(h // 2 + 1) * P],
                                                      tokp[:, c, h:h + 1], gam[:, 8 * c + h, :], ALU.mult, ALU.mult)
            last.then_inc(step("gd_n"), 1)
            for c in range(2):
                for b in range(2):
                    dve.wait_ge(S("gd_gam"), 4 + 2 * c + b + 1)
                    for h in range(4 * b, 4 * b + 4):
                        V.tensor_tensor(aqk[:, 8 * c + h, :], bank(2 + c)[:, (h // 2) * P:(h // 2 + 1) * P],
                                        gam_t[:, 8 * c + h, :], ALU.mult)
            for b in range(4):
                u = slice(4 * b, 4 * b + 4)
                dve.wait_ge(S("gd_nt_out"), b + 1)
                V.tensor_tensor(x_g[:, u, :], x_g[:, u, :], bc(low[0], 4), ALU.mult)
                settle(V.tensor_tensor(xt_g[:, u, :], nt_g[:, u, :], bc(low0_t, 4), ALU.mult))
                V.tensor_tensor(x_g[:, u, :], x_g[:, u, :], bc(ident, 4), ALU.add)
                V.tensor_tensor(xt_g[:, u, :], xt_g[:, u, :], bc(ident, 4), ALU.add).then_inc(S("inv_x_out"), 1)
            inverse(2, range(1, 7), x_g, xt_g, z_g)
            for c in range(2):
                dve.wait_ge(S("gd_k_t"), c + 1)
                for h in range(H):
                    src = bank(4 + c)[:, (h // 2) * P:(h // 2 + 1) * P]
                    if c:
                        last = V.tensor_scalar(k_bg[:, 8 + h, :], src, tokp[:, 4 + c, h:h + 1], None, ALU.mult)
                    else:
                        V.tensor_scalar(k_g[:, h, :], src, tokp[:, 6, h:h + 1], None, ALU.mult)
            last.then_inc(step("gd_k_bg"), 1)
            dve.wait_ge(*at_step("gd_eg"))
            for h in range(H):
                last = V.tensor_tensor(q_g[:, h, :], cv[:, h // 2, P:T], bank(h // 4)[:, (h % 4) * P:(h % 4 + 1) * P], ALU.mult)
            last.then_inc(step("gd_qg"), 1)
            dve.wait_ge(*at_step("gd_ws"))
            V.tensor_tensor(v_new[:].rearrange("p k n -> p (k n)"), u_g[:, 8:16, :].rearrange("p k n -> p (k n)"),
                            psum[:, 4:6, :].rearrange("p b n -> p (b n)"), ALU.subtract).then_inc(step("gd_vn"), 1)
            dve.wait_ge(*at_step("gd_z_sig"))
            zz = proj2[:, 40:48, :]
            settle(V.tensor_tensor(z_sig[:], z_sig[:], zz, ALU.mult))
            dve.wait_ge(*at_step("gd_o_sum"))
            V.tensor_scalar(v4(o_r[:]), psum[:, 4:8, :], 1.0 / P, 1e-6, ALU.mult, ALU.add).then_inc(step("gd_o_mean"), 1)
            dve.wait_ge(*at_step("gd_o_root"))
            settle(V.reciprocal(o_r[:], o_r[:]))
            settle(V.scalar_tensor_tensor(o_g[:], o_g[:], pcol("gdn_norm_w_2"), o_r[:], ALU.mult, ALU.mult))
            settle(V.tensor_tensor(yfin[:, 8:16, :], o_g[:], z_sig[:], ALU.mult))
            settle(V.tensor_copy(Hh[:], yfin[:]))
            V.tensor_tensor(Hl[:], yfin[:], Hh[:].bitcast(F32), ALU.subtract).then_inc(step("y2_split"), 1)
            splits(wo2, residual(wo2))
            norm(4, "ffn_norm_w_2", EPS2, Hr)
            splits(up2, ffn(up2, 1))
            splits(dn2, nothing)
            down_out(dn2)
            norm(5, "final_norm_w_2", EPS2, Hr, split=False)
            for n in range(1, 8, 2):
                dve.wait_ge(out_turned, n + 1)
                V.tensor_copy(out_tokens[:, n % 2, n // 2 * 512:(n // 2 + 1) * 512], bank(n)).then_inc(out_copied, 1)


INPUTS = ["x", "g_mix", "w_in", "b_forget", "conv_w", "conv_b", "w_rg", "b_rg", "w_ig", "b_ig", "lru_lambda", "w_pool",
          "pool_scale", "w_branch_rnn", "w_branch_attn", "w_branch_pool", "w_out", "g_ffn", "w_ffn_in", "w_ffn_out",
          "g_final", "attn_norm_w_2", "w_in_2", "rwkv_mu_2", "rwkv_w0_2", "rwkv_w_up_2", "rwkv_a0_2", "rwkv_a_up_2",
          "rwkv_g_up_2", "rwkv_k_k_2", "rwkv_k_a_2", "rwkv_r_k_2", "rwkv_ln_w_2", "rwkv_ln_b_2", "gdn_conv_w_2",
          "gdn_A_log_2", "gdn_dt_bias_2", "gdn_norm_w_2", "w_out_2", "ffn_norm_w_2", "ffn_w_gate_2", "ffn_w_up_2",
          "ffn_w_down_2", "final_norm_w_2"]


def kernel(**inputs):
    import numpy as np
    import concourse.bacc as bacc
    from concourse.bass_utils import run_bass_kernel_spmd

    nc = bacc.Bacc("TRN2", target_bir_lowering=False, num_devices=1)
    arrays, args = {}, {}
    for name in INPUTS:
        arrays[f"in_{name}"] = np.ascontiguousarray(inputs[name])
        args[name] = nc.dram_tensor(f"in_{name}", arrays[f"in_{name}"].shape, F32, kind="ExternalInput").ap()
    out = nc.dram_tensor("out_dram", (1, T, D), F32, kind="ExternalOutput").ap()
    build(nc, args, out)
    r = run_bass_kernel_spmd(nc, [arrays], core_ids=[0])
    return r.results[0]["out_dram"]
```

```python
from contextlib import ExitStack

import concourse.bass as bass
from concourse import mybir

F32 = mybir.dt.float32
F32R = mybir.dt.float32r
ALU = mybir.AluOpType
ACT = mybir.ActivationFunctionType
AX_X = mybir.AxisListType.X

P = 128
T = 256
D = 2048
KT = D // P
NT = 8
H = 8
FF = 5632
FT = FF // P
CK = 4
CN = 512
KB = 1024
INV_LEVELS = (5, 5, 6)
NEG = -1.0e30
EPS1, EPS2 = 1e-6, 1e-5


class Gemm:

    ring, hi = 4, 2

    def __init__(self, before, strips, bodies, sources):
        self.strips, self.bodies, self.sources = strips, bodies, sources
        ring, hi = self.ring, self.hi
        self.per = sum(n for n, _ in strips)
        self.base = before.base + before.per * before.bodies if before else 0
        self.sbase = before.sbase + before.ns * before.bodies if before else 0
        self.ns = len([r for _, r in strips if r])
        self.landed0 = list(before.landed1) if before else [0] * 4
        self.landed1 = [n + (self.per // ring * bodies if s < ring else 0) for s, n in enumerate(self.landed0)]
        self.ends = {}
        at = 0
        for s, (n, _) in enumerate(strips):
            at += n
            self.ends[at - 1] = s
        assert self.per % ring == 0 and self.per % hi == 0

    def chunk(self, i, j):
        return self.base + i * self.per + j

    def landed(self, i, j):
        return 16 * (self.landed0[j % self.ring] + 1 + j // self.ring) + i * (16 * (self.per // self.ring))

    def strip(self, i, s):
        return self.sbase + i * self.ns + s

    @property
    def end(self):
        return self.base + self.per * self.bodies


def build(nc, a, out):
    ctx = ExitStack()
    with ctx:
        base = -(-nc.sbuf_base // 64) * 64
        RING, XO, HHO, HLO, HO = base, base + 48 * KB, base + 64 * KB, base + 80 * KB, base + 96 * KB
        WO = base + 112 * KB
        CO = WO + 80 * KB
        used = {}

        def at(name, shape, off, dt=F32):
            return nc.alloc_sbuf_tensor_at(name, shape, dt, offset=off)

        const_at = [CO]

        def const(name, shape, dt=F32):
            n = 4
            for s in shape[1:]:
                n *= s
            t = at(name, shape, const_at[0], dt)
            const_at[0] += -(-n // 32) * 32
            assert const_at[0] <= nc.sbuf_usable_end, name
            return t

        psum = ctx.enter_context(nc.psum_tensor("psum", [P, 8, 512], F32))

        def pair(s):
            return psum[:, 2 * (s % 4):2 * (s % 4) + 2, :].rearrange("p b (t n) -> p (b t) n", t=2)

        def bank(b):
            return psum[:, b, :]

        def sem(name):
            return ctx.enter_context(nc.semaphore(name))

        raw = [at(f"weight_raw{s}", [P, CK, CN], RING + 8 * KB * s) for s in range(4)]
        lo = [at(f"weight_lo{s}", [P, CK, CN], RING + 8 * KB * s, F32R) for s in range(4)]
        hi = [at(f"weight_hi{s}", [P, CK, CN], RING + 32 * KB + 8 * KB * s, F32R) for s in range(2)]
        X = at("residual", [P, KT, T], XO)
        Hh = at("h_hi", [P, KT, T], HHO, F32R)
        Hl = at("h_lo", [P, KT, T], HLO, F32R)
        U = {0: at("u_in", [P, KT, T], HO), 1: at("u_ffn", [P, KT, T], WO + 32 * KB)}
        SQ = {0: at("squares_in", [P, KT, T], WO), 1: at("squares_ffn", [P, KT, T], WO + 16 * KB)}
        SQ2 = at("squares_gained", [P, KT, T], WO + 32 * KB)
        Mh = at("mixed_hi", [P, KT, T], HO, F32R)
        Ml = [at("merged_lo", [P, KT, T], WO + 48 * KB, F32R), at("y_lo2", [P, KT, T], WO, F32R)]
        tokens = at("x_tokens", [P, 2, D], HO)
        out_tokens = at("out_tokens", [P, 2, D], WO)
        proj = at("proj1", [P, 6 * NT, T], WO)
        TO = WO + 48 * KB
        t1, t2, t3, t4 = (at(f"temp{n}", [P, NT, T], TO + 8 * KB * n) for n in range(4))
        rx = proj[:, 0:NT, :]
        ry = proj[:, NT:2 * NT, :]
        t1b = at("conv_u_t", [P, NT, T], HO)
        t4b = at("gelu_t", [P, NT, T], HO + 8 * KB)
        yh = [at(f"y_hi{b}", [P, NT, T], WO + 16 * KB * b, F32R) for b in range(3)]
        yl = [at(f"y_lo{b}", [P, NT, T], WO + 16 * KB * b + 8 * KB, F32R) for b in range(3)]
        merged = at("merged", [P, KT, T], TO)
        sg = at("sig_gate", [P, 4, T], TO + 16 * KB)
        gated = at("gated", [P, 4, T], TO + 20 * KB)
        Fh = at("ffn_hi", [P, FT, T], HO, F32R)
        Fl = at("ffn_lo", [P, FT, T], HO + FT * KB, F32R)
        act_gate = at("ffn_act", [P, 4, T], HO + 2 * FT * KB)
        act_up = at("ffn_act_up", [P, 4, T], HO + 2 * FT * KB + 4 * KB)

        ident = const("ident", [P, P])
        ones = const("ones", [P, P])
        causal = const("causal", [P, P])
        par1 = const("par1", [P, 316])
        rstd = const("rstd", [P, T])
        rstd_final1 = at("rstd_final1", [P, T], WO + 78 * KB)
        lam8 = const("lam8", [P, NT])
        spt = [const(f"sp_tmp{n}", [P, NT]) for n in range(4)]
        fT = [at(f"f_tmp{n}", [H, T], TO + KB * n) for n in range(4)]
        ones8 = const("ones_rows", [H, T])
        neg_f = const("neg_f_cumsum", [H, T])
        bfor = const("b_forget_col", [H, 1])
        wf = const("w_forget", [P, KT, H])
        neg_max = const("neg_max", [P, 4])
        rowsum = const("rowsum", [P, 4])
        rows = [at(f"param_rows{n}", [P, P], WO + 76 * KB + 512 * n) for n in range(3)]

        w_rg = at("w_rg_s", [P, NT, P], RING)
        w_ig = at("w_ig_s", [P, NT, P], RING + 4 * KB)
        w_pl = at("w_pool_s", [P, 4, 2, 256], RING + 8 * KB)
        recip_cnt = at("recip_cnt", [P, 4, T], RING + 16 * KB)
        selrow = at("selrow", [H, H, P], RING + 20 * KB)
        fmask = at("f_masked", [H, H, T], RING + 24 * KB)
        probs = at("probs", [P, 2, 384], RING + 32 * KB)
        probsT = at("probs_t", [P, 2, 384], RING + 35 * KB)
        vtok = at("v_tokens", [P, 2, 1024], RING + 38 * KB)

        groups = [[("g_mix", 16), ("conv_w", 32), ("conv_b", 8), ("b_rg", 8), ("b_ig", 8), ("lru_lambda", 8),
                   ("pool_scale", 8), ("g_ffn", 16), ("g_final", 16)],
                  [("attn_norm_w_2", 16), ("rwkv_mu_2", 27), ("rwkv_w0_2", 8), ("rwkv_a0_2", 8), ("rwkv_k_k_2", 8),
                   ("rwkv_k_a_2", 8), ("rwkv_r_k_2", 8), ("rwkv_ln_w_2", 8), ("rwkv_ln_b_2", 8), ("ffn_norm_w_2", 16)],
                  [("gdn_conv_w_2", 64), ("gdn_norm_w_2", 1), ("final_norm_w_2", 16)]]
        col, ncols, spans = {}, 0, []
        for g in groups:
            spans.append((ncols, sum(k for _, k in g)))
            for n, k in g:
                col[n] = ncols
                ncols += k

        def pcol(name, k=0, rows=P):
            return par1[0:rows, col[name] + k:col[name] + k + 1]

        low = [const(f"low_mask{n}", [P, P]) for n in range(7)]
        low0_t = const("low_mask0_t", [P, P])
        upper_strict = const("upper_strict64", [P, P])
        upper_incl = const("upper_incl64", [P, P])
        head_ones = const("head_ones64", [P, P])
        chunk_decay = const("chunk_decay", [P, NT, 4])
        state = const("rwkv_state", [P, NT, 64])
        gb = const("gdn_b", [H, T])
        alog, dtb = const("gdn_A_log_col", [H, 1]), const("gdn_dt_col", [H, 1])
        tokp = const("gdn_token_scalars", [P, 8, H])
        CH = 64
        proj2 = at("proj2", [P, 48, T], WO)
        yfin = at("y_out", [P, KT, T], WO)
        w_lora = at("w_lora", [P, KT, 288], TO)
        w_ab = at("w_ab", [P, KT, 16], TO + 18 * KB)

        def slot(name, off, shape=(NT, T)):
            return at(name, [P, *shape], off)
        R0, R1, R2, R3, R4, R5 = (RING + 8 * KB * n for n in range(6))
        w_upa = slot("w_up_a_up", R4, (1024,))
        w_gu = slot("g_up", R4 + 4 * KB, (2, 1024))
        lp = slot("lora", TO + 24 * KB, (3, T))
        lpd = slot("lora_shift", TO + 27 * KB, (3, T))
        spare = proj2[:, 40:48, :]
        Rw, Kw, Vw = proj2[:, 0:8, :], proj2[:, 8:16, :], proj2[:, 16:24, :]
        ld, reset = slot("log_decay", TO), slot("reset_mask", TO + 8 * KB)
        cum, a_lr = slot("cum_decay", HO), slot("a_rate", HO + 8 * KB)
        kk, bonus = slot("kk", HHO), slot("bonus", HHO + 8 * KB)
        at_f, bt_f = slot("a_tilde", HLO), slot("b_tilde", HLO + 8 * KB)
        gate2 = slot("rwkv_gate", R3)
        at_tok, bt_tok = slot("a_tokens", R2, (1024,)), slot("b_tokens", R2 + 4 * KB, (1024,))
        kt_tok, v_tok2 = slot("k_tokens", TO + 24 * KB, (1024,)), slot("v_tokens2", TO + 28 * KB, (1024,))
        nt_r, akt, rbt = (slot(n, TO + 8 * KB * k, (16, P)) for k, n in enumerate(("rw_nt", "rw_akt", "rw_rbt")))
        rkt, x_r = slot("rw_rkt", HO, (16, P)), slot("rw_x", HO + 8 * KB, (16, P))
        xt_r, z_r = slot("rw_xt", R0, (16, P)), slot("rw_z", R1, (16, P))
        uv, wt = slot("rw_uv", R4, (1024,)), slot("rw_wt", R4 + 4 * KB, (NT, P))
        z1, u_tok = slot("rw_z1", R5, (1024,)), slot("rw_u", R5 + 4 * KB, (1024,))
        y_rw = slot("rw_y", HHO)
        gn_sq, gn_r = slot("gn_squares", TO), slot("gn_rstd", TO + 8 * KB)
        cv = proj2[:, 24:40, :]
        gn = [at(f"gdn_small{n}", [H, T], TO + 16 * KB + KB * n) for n in range(8)]
        l2s = slot("gdn_l2", HHO, (8, T))
        selrow2 = at("selrow2", [H, H, P], TO + 24 * KB)
        neg_ls, neg_ui = at("neg_lower_strict", [P, P], TO + 28 * KB), at("neg_upper_incl", [P, P], TO + 28 * KB + 512)
        gm, ngm = at("gdn_gm", [H, H, T], HLO), at("gdn_ngm", [H, H, T], HLO + 8 * KB)
        gam, gam_t = slot("gamma", R3, (16, P)), slot("gamma_t", R4, (16, P))
        nt_g, x_g, xt_g, z_g = (slot(n, o, (16, P)) for n, o in (("gd_nt", HO), ("gd_x", HO + 8 * KB), ("gd_xt", R0), ("gd_z", R1)))
        aqk = slot("gd_aqk_t", R2, (16, P))
        v_beta = slot("gd_v_beta", R5, (16, P))
        k_bg = slot("gd_k_beta_g", HHO, (16, P))
        k_g, q_g = slot("gd_k_g", HHO + 8 * KB, (NT, P)), slot("gd_q_g", HHO + 12 * KB, (NT, P))
        u_g = slot("gd_u", HLO, (16, P))
        w_g, v_new = slot("gd_w_t", HLO + 8 * KB, (NT, P)), slot("gd_v_new", HLO + 12 * KB, (NT, P))
        s_g = slot("gd_state", R3, (NT, P))
        o_g = slot("gd_o", TO + 24 * KB)
        o_sq, o_r = slot("gd_o_sq", HLO), slot("gd_o_rstd", HHO)
        z_sig = slot("gd_z_sig", HLO + 8 * KB)

        def hc(x):
            h = 2 * (x % 8) + x // 8
            return slice(64 * h, 64 * h + 64)

        def hr(x):
            return slice(64 * (x // 8), 64 * (x // 8) + 64)

        def bc(m, n):
            return m[:].unsqueeze(1).to_broadcast([P, n, P])

        STEPS = {
            "gpsimd": ["rows_cleared", "reset_built", "selrow2_built"],
            "tensor": ["lora_mm", "zw_mm", "za_mm", "g_mm", "kk_sum", "rk_sum", "gn_mean", "gn_var", "gd_tok",
                "gd_l2", "gd_gram", "gd_w", "gd_s", "gd_eg", "gd_ws", "gd_o", "gd_o_sum"],
            "scalar": ["gd_sig_qk", "gd_sig_v", "lora_act", "ld_out", "a_out", "g_out", "kk_sq", "kk_root", "e_prev", "e_plus",
                "e_minus", "gn_sq", "gn_root", "gd_beta", "gd_expA", "gd_sq", "gd_l2_root",
                "gd_tok_exp", "gd_w_out", "gd_s_out", "gd_o_out", "gd_o_sq", "gd_z_sig", "gd_o_root"],
            "vector": ["gd_cv_qk", "gd_silu_qk", "gd_cv_v", "gd_silu_v", "ab_out", "lora_out", "lora_in", "kk", "l_prev", "kk_mean", "rk", "at_made", "rw_fm", "gn_c", "gn_m",
                "gn_out", "gd_cum", "gd_rows", "gd_tok_out", "gd_l2_mean", "gd_qk",
                "gd_n", "gd_k_bg", "gd_qg", "gd_vn", "gd_o_mean"],
        }
        step_sem = {e: sem(f"{e}_steps") for e in STEPS}
        step_of = {n: (e, k + 1) for e in STEPS for k, n in enumerate(STEPS[e])}
        made = {e: 0 for e in STEPS}

        def step(name):
            e, k = step_of[name]
            made[e] += 1
            assert made[e] == k, name
            return step_sem[e]

        def at_step(name):
            e, k = step_of[name]
            return step_sem[e], k

        sems = {}

        def S(name):
            if name not in sems:
                sems[name] = sem(name)
            return sems[name]

        landed = [sem(f"chunk_landed{s}") for s in range(4)]
        hi_ready, lo_ready = sem("chunk_hi_ready"), sem("chunk_lo_ready")
        chunks_used, strips_out = sem("chunks_used"), sem("strips_evacuated")
        x_landed, par_landed = sem("x_landed"), sem("params_landed")
        consts = sem("constants_built")
        x_turned, par_turned, par_ready, x_ready = sem("x_transposed"), sem("params_transposed"), sem("params_ready"), sem("x_ready")
        n_u, n_sq, n_hi, n_sum, n_mean, n_root, h_ready = (
            sem(f"norm_{x}") for x in ("gained", "squared", "hi", "summed", "mean", "root", "split"))
        rstd_ready, ffn_silu, ffn_up, par_gains = (sem(x) for x in ("rstd_ready", "ffn_silu", "ffn_up", "gains_ready"))
        y2_parts, y2_hi, y2_made = sem("y2_split"), sem("y2_hi"), sem("y2_made")
        merged_hi, y_hi = sem("merged_hi"), sem("y_hi")
        mw_landed, mix_tables = sem("mixer_weights_landed"), sem("mixer_tables_built")
        f_logits = sem("f_logits_summed")
        sp_abs, sp_exp = sem("softplus_abs"), sem("softplus_exp")
        pool_in, pool_mm = sem("pooled_ready"), sem("pool_product")
        conv_u, gates_mm, r_sig, i_sig = sem("conv_u"), sem("lru_gate_products"), sem("lru_r"), sem("lru_i")
        lru_a, lru_th, lru_sq, lru_var, lru_root = (sem(f"lru_{x}") for x in ("decay", "tanh", "decay_squared", "variance", "input_scale"))
        gelu_sq, gelu_arg, gelu_sig = sem("gelu_squared"), sem("gelu_argument"), sem("gelu_sigmoid")
        q_scaled, f_rows = sem("q_scaled"), sem("f_rows")
        v_turned, v_tok = sem("v_transposed"), sem("v_tokens_ready")
        sc_mm, sc_max, sc_exp, sc_p, sc_t, sc_pt, sc_o, sc_y = (
            sem(f"attn_{x}") for x in ("scores", "max", "exp", "probs", "transposed", "probs_t", "product", "out"))
        y_ready, merged_ready = sem("y_split"), sem("merged_split")
        merged_sum, gate_sig, ffn_hi = sem("merged_added"), sem("gate_sigmoid"), sem("ffn_hi")
        pool_out, lru_iu, lam_ready = sem("pool_out"), sem("lru_gated_input"), sem("lambda_ready")
        ffn_sig, ffn_split = sem("ffn_sigmoid"), sem("ffn_split")
        out_turned, out_copied, out_stored = sem("out_transposed"), sem("out_copied"), sem("out_stored")
        chain = {k: sem(f"{k}_order") for k in ("vector", "scalar", "gpsimd", "tensor")}

        w_in = a["w_in"][0].rearrange("(k p) n -> p k n", p=P)

        def sl(w, k, c):
            return w[:, CK * k:CK * k + CK, bass.ds(c, CN)]

        def h_rhs(kt):
            return Hh[:, kt, :], Hl[:, kt, :]

        def mixed_rhs(n):
            return lambda kt: (Mh[:, kt, :], Ml[n][:, kt, :])

        in1 = Gemm(None, [(4, h_rhs)] * 2, 6,
                   lambda i: [sl(w_in, k, (5128 if isinstance(i, int) and i == 5 else i * 1024) + s * CN)
                              for s in range(2) for k in range(4)])
        w_br = [a[n][0].rearrange("(k p) n -> p k n", p=P) for n in ("w_branch_rnn", "w_branch_attn", "w_branch_pool")]
        GATES = 5128 + 1024

        def y_rhs(b):
            return lambda kt: (yh[b][:, kt, :], yl[b][:, kt, :])

        mer = Gemm(in1, [x for half in range(2) for b in range(3) for x in ((4, h_rhs), (2, y_rhs(b)))], 2,
                   lambda i: [x for c in range(2) for b in range(3) for x in
                              [sl(w_in, k, GATES + b * D + (2 * i + c) * CN) for k in range(4)] +
                              [sl(w_br[b], k, (2 * i + c) * CN) for k in range(2)]])
        w_o = a["w_out"][0].rearrange("(k p) n -> p k n", p=P)
        wo1 = Gemm(mer, [(4, mixed_rhs(0))] * 2, 2,
                   lambda i: [sl(w_o, k, i * 1024 + s * CN) for s in range(2) for k in range(4)])
        w_f1 = a["w_ffn_in"][0].rearrange("(k p) n -> p k n", p=P)
        up1 = Gemm(wo1, [(4, h_rhs)] * 2, FF // CN,
                   lambda i: [sl(w_f1, k, i * CN + s * FF) for s in range(2) for k in range(4)])
        w_d1 = a["w_ffn_out"][0].rearrange("(k p) n -> p k n", p=P)
        dn1 = Gemm(up1, [(4, None)], FT // CK,
                   lambda i: [w_d1[:, bass.ds(i * CK, CK), c * CN:(c + 1) * CN] for c in range(4)])

        w_in2 = a["w_in_2"][0].rearrange("(k p) n -> p k n", p=P)
        N_RWKV = 3360
        in2 = Gemm(dn1, [(4, h_rhs)] * 2, 6,
                   lambda i, off=0: [sl(w_in2, k, off + i * 1024 + s * CN) for s in range(2) for k in range(4)])
        w_o2 = a["w_out_2"][0].rearrange("(k p) n -> p k n", p=P)
        wo2 = Gemm(in2, [(4, mixed_rhs(1))] * 2, 2,
                   lambda i: [sl(w_o2, k, i * 1024 + s * CN) for s in range(2) for k in range(4)])
        w_gu2 = [a[n][0].rearrange("(k p) n -> p k n", p=P) for n in ("ffn_w_gate_2", "ffn_w_up_2")]
        up2 = Gemm(wo2, [(4, h_rhs)] * 2, FF // CN,
                   lambda i: [sl(w_gu2[s], k, i * CN) for s in range(2) for k in range(4)])
        w_d2 = a["ffn_w_down_2"][0].rearrange("(k p) n -> p k n", p=P)
        dn2 = Gemm(up2, [(4, None)], FT // CK,
                   lambda i: [w_d2[:, bass.ds(i * CK, CK), c * CN:(c + 1) * CN] for c in range(4)])

        def wait(e, s, v):
            if isinstance(v, int) and v <= 0:
                return
            e.wait_ge(s, v)

        def settler(e, name):
            n = [0]

            def settle(ins):
                n[0] += 1
                ins.then_inc(chain[name], 1)
                e.wait_ge(chain[name], n[0])
            return settle

        def loops(e, g, body, last=None):
            last = g.bodies if last is None else last
            body(0)
            if last == 2:
                body(1)
            else:
                with e.Fori(1, last) as i:
                    body(i)

        block = ctx.enter_context(nc.Block())

        @block.sync
        def _(sp):
            sp.dma_start(tokens[:], a["x"][0].rearrange("(b p) n -> p b n", p=P)).then_inc(x_landed, 16)
            sp.wait_ge(*at_step("rows_cleared"))
            for g, tile in zip(groups, rows):
                r = 0
                for n, k in g:
                    src = a[n]
                    src = src if n in ("g_final", "final_norm_w_2") else src[0]
                    if len(src.shape) == 2 and n != "rwkv_r_k_2":
                        src = src.rearrange("k (r c) -> (k r) c", c=P)
                    elif n == "rwkv_r_k_2":
                        src = src.rearrange("(r h) c -> r (h c)", h=2)
                    elif n == "rwkv_mu_2":
                        sp.dma_start(tile[r + 26:r + 27, 0:32], src[26 * P:3360].rearrange("(r c) -> r c", r=1)).then_inc(par_landed, 16)
                        sp.dma_start(tile[r:r + 26, :], src[0:26 * P].rearrange("(r c) -> r c", c=P)).then_inc(par_landed, 16)
                        r += k
                        continue
                    else:
                        src = src.rearrange("(r c) -> r c", c=P)
                    sp.dma_start(tile[r:r + k, :], src).then_inc(par_landed, 16)
                    r += k
            with nc.allow_non_contiguous_dma(reason="8 values"):
                sp.dma_start(bfor[:], a["b_forget"].rearrange("a h -> h a")).then_inc(par_landed, 16)
                sp.dma_start(alog[:], a["gdn_A_log_2"].rearrange("a h -> h a")).then_inc(par_landed, 16)
                sp.dma_start(dtb[:], a["gdn_dt_bias_2"].rearrange("a h -> h a")).then_inc(par_landed, 16)
                sp.dma_start(wf[:], w_in[:, :, 5120:5128]).then_inc(par_landed, 16)

            def load(g, i, *more):
                for j, src in enumerate(g.sources(i, *more)):
                    wait(sp, chunks_used, g.chunk(i, j) - g.ring + 1)
                    sp.dma_start(raw[j % g.ring][:], src).then_inc(landed[j % g.ring], 16)

            def loads(g, last=None):
                loops(sp, g, lambda i: load(g, i), last)

            loads(in1, 5)
            load(in1, 5)
            sp.wait_ge(chunks_used, in1.end)
            sp.dma_start(w_rg[:], a["w_rg"][0].rearrange("n c d -> c n d")).then_inc(mw_landed, 16)
            sp.dma_start(w_ig[:], a["w_ig"][0].rearrange("n c d -> c n d")).then_inc(mw_landed, 16)
            sp.dma_start(w_pl[:], a["w_pool"][0].rearrange("g (t p) d -> p g t d", p=P)).then_inc(mw_landed, 16)
            sp.wait_ge(pool_mm, 4)
            sp.wait_ge(gates_mm, 8)
            for j, src in enumerate(mer.sources(0)):
                if j == 2:
                    sp.wait_ge(sc_mm, H)
                if j >= mer.ring:
                    sp.wait_ge(chunks_used, mer.chunk(0, j) - mer.ring + 1)
                sp.dma_start(raw[j % mer.ring][:], src).then_inc(landed[j % mer.ring], 16)
            load(mer, 1)
            loads(wo1)
            loads(up1)
            loads(dn1)
            sp.wait_ge(chunks_used, in2.base)
            sp.dma_start(w_lora[:], w_in2[:, :, 3072:N_RWKV]).then_inc(S("lora_w_landed"), 16)
            sp.dma_start(w_ab[:], w_in2[:, :, 6432:6448]).then_inc(S("lora_w_landed"), 16)
            load(in2, 0)
            with sp.Fori(1, 3) as i:
                load(in2, i)
            with sp.Fori(3, 6) as i:
                load(in2, i, N_RWKV - 3072)
            sp.wait_ge(chunks_used, in2.end)
            sp.dma_start(w_upa[0:64, :], a["rwkv_w_up_2"][0]).then_inc(S("ups_landed"), 16)
            sp.dma_start(w_upa[64:P, :], a["rwkv_a_up_2"][0]).then_inc(S("ups_landed"), 16)
            sp.dma_start(w_gu[:, 0, :], a["rwkv_g_up_2"][0, 0:P]).then_inc(S("ups_landed"), 16)
            sp.dma_start(w_gu[0:32, 1, :], a["rwkv_g_up_2"][0, P:160]).then_inc(S("ups_landed"), 16)
            sp.wait_ge(*at_step("gd_o"))
            loads(wo2)
            loads(up2)
            loads(dn2)
            sp.wait_ge(out_copied, 8)
            for b in range(2):
                sp.dma_start(out[0, b * P:(b + 1) * P, :], out_tokens[:, b, :]).then_inc(out_stored, 16)
            sp.wait_ge(out_stored, 32)

        @block.gpsimd
        def _(gp):
            settle = settler(gp, "gpsimd")
            gp.memset(rows[1][:], 0.0).then_inc(step("rows_cleared"), 1)
            gp.memset(ident[:], 0.0)
            gp.memset(causal[:], 0.0)
            settle(gp.memset(ones[:], 1.0))
            gp.affine_select(out=ident[:], in_=ident[:], compare_op=ALU.not_equal, fill=1.0, base=0,
                             pattern=[[-1, P]], channel_multiplier=1).then_inc(consts, 1)
            gp.affine_select(out=causal[:], in_=causal[:], compare_op=ALU.is_ge, fill=NEG, base=0,
                             pattern=[[-1, P]], channel_multiplier=1).then_inc(consts, 1)
            gp.wait_ge(chunks_used, in1.end)
            for g, w in enumerate((2, 4, 8, 16)):
                gp.memset(recip_cnt[:, g, :], 1.0 / w)
            settle(gp.memset(selrow[:], 0.0))
            for g, w in enumerate((2, 4, 8, 16)):
                for t in range(w - 1):
                    gp.memset(recip_cnt[:, g, t:t + 1], 1.0 / (t + 1))
            gp.affine_select(out=selrow[:], in_=selrow[:], compare_op=ALU.not_equal, fill=1.0, base=0,
                             pattern=[[-1, H], [0, P]], channel_multiplier=1).then_inc(mix_tables, 1)

            def keep(m, base, pattern, cm):
                settle(gp.affine_select(out=m[:], in_=m[:], compare_op=ALU.is_ge, fill=0.0, base=base,
                                        pattern=pattern, channel_multiplier=cm))

            for m in (*low, low0_t, upper_strict, upper_incl, head_ones):
                settle(gp.memset(m[:], 1.0))
            for n in range(7):
                s = 2 ** n
                keep(low[n], -s, [[-s, P // s], [0, s]], 1)
                keep(low[n], 2 * s - 1, [[2 * s, P // (2 * s)], [0, 2 * s]], -1)
            keep(low0_t, -1, [[1, P]], -1)
            keep(low0_t, 0, [[-2, P // 2], [0, 2]], 1)
            for m in (upper_strict, upper_incl, head_ones):
                keep(m, 0, [[-CH, P // CH], [0, CH]], 1)
            keep(upper_strict, -1, [[1, P]], -1)
            keep(upper_incl, 0, [[1, P]], -1)
            keep(head_ones, CH - 1, [[CH, P // CH], [0, CH]], -1)
            gp.memset(state[:], 0.0).then_inc(S("rw_state"), 1)
            gp.wait_ge(*at_step("lora_mm"))
            settle(gp.memset(reset[:], 1.0))
            gp.memset(reset[:].rearrange("p k (c t) -> p (k c) t", t=CH)[:, :, 0:1], 0.0).then_inc(step("reset_built"), 1)
            gp.wait_ge(*at_step("gn_out"))
            gp.memset(neg_ls[:], 0.0)
            gp.memset(neg_ui[:], 0.0)
            settle(gp.memset(selrow2[:], 0.0))
            gp.affine_select(out=neg_ls[:], in_=neg_ls[:], compare_op=ALU.is_ge, fill=NEG, base=-1,
                             pattern=[[-1, P]], channel_multiplier=1)
            gp.affine_select(out=neg_ui[:], in_=neg_ui[:], compare_op=ALU.is_ge, fill=NEG, base=0,
                             pattern=[[1, P]], channel_multiplier=-1)
            gp.affine_select(out=selrow2[:], in_=selrow2[:], compare_op=ALU.not_equal, fill=1.0, base=0,
                             pattern=[[-1, H], [0, P]], channel_multiplier=1).then_inc(step("selrow2_built"), 1)

        @block.tensor
        def _(pe):
            mm, tr = nc.tensor.matmul, nc.tensor.transpose
            pe.wait_ge(consts, 2)
            pe.wait_ge(x_landed, 16)
            for b in range(8):
                for k in range(2):
                    for t in range(2):
                        last = tr(bank(b)[:, (2 * k + t) * P:(2 * k + t + 1) * P],
                                  tokens[:, t, (2 * b + k) * P:(2 * b + k + 1) * P], ident[:])
                last.then_inc(x_turned, 1)
            pe.wait_ge(par_landed, 16 * (sum(len(g) for g in groups) + 5))
            pe.wait_ge(x_ready, 1)
            for (c, k), tile in zip(spans, rows):
                last = tr(bank(0)[:, c:c + k], tile[0:k, :], ident[0:k, 0:k])
            last.then_inc(par_turned, 1)

            def norm_sums(n, *squares):
                pe.wait_ge(n_sq, 4 * n + 4)
                for m, q in enumerate(squares):
                    for k in range(KT):
                        last = mm(bank(7)[:, m * T:(m + 1) * T], ones[:], q[:, k, :], start=(k == 0 and m == 0),
                                  stop=(k == KT - 1), skip_group_check=True)
                last.then_inc(n_sum, 1)

            def product(g, i, j, acc, rhs, start, stop):
                pe.wait_ge(lo_ready, g.chunk(i, j) + 1)
                wh, wl = hi[j % g.hi], lo[j % g.ring]
                for f in range(4):
                    for k in range(CK):
                        xh, xl = rhs(k)
                        c = slice(f * P, (f + 1) * P)
                        mm(acc[:, f, :], wh[:, k, c], xh, start=(start and k == 0 and f % 2 == 0),
                           stop=False, skip_group_check=True)
                        mm(acc[:, f, :], wl[:, k, c], xh, start=False, stop=False, skip_group_check=True)
                        last = mm(acc[:, f, :], wh[:, k, c], xl, start=False,
                                  stop=(stop and k == CK - 1), skip_group_check=True)
                last.then_inc(chunks_used, 1)

            def body(g, i, parts=None, n_norm=0, *squares):
                j = 0
                for s, (n, rhs) in enumerate(g.strips):
                    wait(pe, strips_out, g.strip(i, s) - 1)
                    if g is mer and s == 3:
                        pe.wait_ge(y_ready, 3)
                    for c in range(n):
                        if parts is not None and s == 0:
                            pe.wait_ge(parts, 4 * n_norm + c + 1)
                            if c == 2 and squares:
                                norm_sums(n_norm, *squares)
                        product(g, i, j, pair(s % 2), lambda k: rhs(CK * c + k), c == 0, c == n - 1)
                        j += 1

            def normed(g, n_norm, *squares):
                body(g, 0, h_ready, n_norm, *squares)
                with pe.Fori(1, g.bodies) as i:
                    body(g, i)

            def down(g, i):
                for j in range(4):
                    def rhs(k):
                        if isinstance(i, int):
                            return Fh[:, CK * i + k, :], Fl[:, CK * i + k, :]
                        return (Fh[:, bass.ds(CK * i + k, 1), :].rearrange("p a n -> p (a n)"),
                                Fl[:, bass.ds(CK * i + k, 1), :].rearrange("p a n -> p (a n)"))
                    if isinstance(i, int) and i == 0 and j < 2:
                        pe.wait_ge(strips_out, g.sbase - 1 + j)
                    product(g, i, j, pair(j), rhs, isinstance(i, int) and i == 0, isinstance(i, int) and i == g.bodies - 1)

            def downs(g, n):
                pe.wait_ge(ffn_split, n * (FF // CN) - 1)
                down(g, 0)
                with pe.Fori(1, g.bodies - 1) as i:
                    down(g, i)
                pe.wait_ge(ffn_split, n * (FF // CN))
                down(g, g.bodies - 1)

            pe.wait_ge(par_ready, 1)
            normed(in1, 0, SQ[0])

            pe.wait_ge(strips_out, in1.sbase + in1.ns * in1.bodies)
            for k in range(KT):
                last = mm(bank(7)[0:H, 0:T], wf[:, k, :], U[0][:, k, :], start=(k == 0), stop=(k == KT - 1))
            last.then_inc(f_logits, 1)
            v = proj[:, 4 * NT:5 * NT, :]
            for h in range(H):
                for t in range(2):
                    last = tr(bank(h // 2)[:, (2 * (h % 2) + t) * P:(2 * (h % 2) + t + 1) * P],
                              v[:, h, t * P:(t + 1) * P], ident[:])
                if h % 2:
                    last.then_inc(v_turned, 1)
            pe.wait_ge(mw_landed, 48)
            pe.wait_ge(pool_in, 1)
            pe.wait_ge(f_rows, 1)
            for g in range(4):
                for d in range(2):
                    for c in range(2):
                        last = mm(bank(4 + g)[:, d * T:(d + 1) * T], w_pl[:, g, c, d * P:(d + 1) * P],
                                  t1[:, 2 * g + c, :], start=(d == 0 and c == 0), stop=(c == 1), skip_group_check=True)
                last.then_inc(pool_mm, 1)
            pe.wait_ge(v_tok, 4)
            pe.wait_ge(conv_u, 1)
            for w, b0 in ((w_rg, 0), (w_ig, 4)):
                if b0:
                    pe.wait_ge(pool_out, 4)
                for n in range(NT):
                    last = mm(bank(b0 + n // 2)[:, (n % 2) * T:(n % 2 + 1) * T], w[:, n, :], t1b[:, n, :],
                              start=(n % 2 == 0), stop=True, skip_group_check=True)
                    if n % 2:
                        last.then_inc(gates_mm, 1)
            q, kk = proj[:, 2 * NT:3 * NT, :], proj[:, 3 * NT:4 * NT, :]

            def scores(h):
                if h == 0:
                    pe.wait_ge(q_scaled, 1)
                    pe.wait_ge(f_rows, 3)
                    pe.wait_ge(i_sig, NT)
                if h >= 2:
                    pe.wait_ge(sc_exp, h - 1)
                s = bank(4 + h % 2)
                for t in range(2):
                    n, o = (t + 1) * P, t * P
                    dst = s[:, t * P:t * P + n]
                    mm(dst, q[:, h, o:o + P], kk[:, h, 0:n], start=(t == 0), stop=False, skip_group_check=True)
                    mm(dst, fmask[:, h, o:o + P], ones8[:, 0:n], start=False, stop=False, skip_group_check=True)
                    mm(dst, selrow[:, h, :], neg_f[:, 0:n], start=False, stop=False, skip_group_check=True)
                    last = mm(s[:, t * P + o:t * P + n], ident[:], causal[:], start=False, stop=True, skip_group_check=True)
                last.then_inc(sc_mm, 1)

            def turn(h):
                pe.wait_ge(sc_p, h + 1)
                if h >= 2:
                    pe.wait_ge(sc_pt, h - 1)
                for b in range(3):
                    last = tr(bank(6 + h % 2)[:, b * P:(b + 1) * P], probs[:, h % 2, b * P:(b + 1) * P], ident[:])
                last.then_inc(sc_t, 1)

            def mix(h):
                if h == 0:
                    pe.wait_ge(r_sig, NT)
                pe.wait_ge(sc_pt, h + 1)
                if h >= 2:
                    pe.wait_ge(sc_y, h - 1)
                o, c = bank(2 + h % 2), slice(h * P, (h + 1) * P)
                mm(o[:, 0:P], vtok[:, 0, c], probsT[:, h % 2, 0:P], start=True, stop=True, skip_group_check=True)
                mm(o[:, P:T], vtok[:, 0, c], probsT[:, h % 2, P:2 * P], start=False, stop=False, skip_group_check=True)
                mm(o[:, P:T], vtok[:, 1, c], probsT[:, h % 2, 2 * P:3 * P], start=False, stop=True,
                   skip_group_check=True).then_inc(sc_o, 1)

            for h in range(H + 2):
                if h < H:
                    scores(h)
                if 1 <= h <= H:
                    turn(h - 1)
                if h >= 2:
                    mix(h - 2)
            pe.wait_ge(y_ready, 1)
            with pe.Fori(0, mer.bodies) as i:
                body(mer, i)
            body(wo1, 0, merged_ready, 0)
            body(wo1, 1)
            normed(up1, 1, SQ[1])
            downs(dn1, 1)
            normed(in2, 2, SQ[0], SQ2)
            pe.wait_ge(strips_out, in2.sbase + in2.ns * in2.bodies)
            pe.wait_ge(S("lora_w_landed"), 32)
            for b, o, m, c in ((0, 0, P, 0), (0, T, P, P), (1, 0, 32, 2 * P)):
                for k in range(KT):
                    mm(bank(b)[0:m, o:o + T], w_lora[:, k, c:c + m], U[0][:, k, :], start=(k == 0 and o == 0),
                       stop=(k == KT - 1), skip_group_check=True)
            for o, c in ((0, 0), (T, H)):
                for k in range(KT):
                    last = mm(bank(2)[0:H, o:o + T], w_ab[:, k, c:c + H], U[0][:, k, :], start=(k == 0 and o == 0),
                              stop=(k == KT - 1), skip_group_check=True)
            last.then_inc(step("lora_mm"), 1)
            pe.wait_ge(S("ups_landed"), 64)
            pe.wait_ge(*at_step("lora_act"))
            pe.wait_ge(*at_step("ab_out"))
            for b0, r, name in ((0, 0, "zw_mm"), (4, 64, "za_mm")):
                for n in range(NT):
                    last = mm(bank(b0 + n // 2)[:, (n % 2) * T:(n % 2 + 1) * T], w_upa[r:r + 64, n * P:(n + 1) * P],
                              lp[r:r + 64, 0, :], start=(n % 2 == 0), stop=True, skip_group_check=True)
                last.then_inc(step(name), 1)
            pe.wait_ge(*at_step("ld_out"))
            for n in range(NT):
                o = bank(n // 2)[:, (n % 2) * T:(n % 2 + 1) * T]
                mm(o, w_gu[:, 0, n * P:(n + 1) * P], lp[:, 1, :], start=(n % 2 == 0), stop=False, skip_group_check=True)
                last = mm(o, w_gu[0:32, 1, n * P:(n + 1) * P], lp[0:32, 2, :], start=False, stop=True, skip_group_check=True)
            last.then_inc(step("g_mm"), 1)

            def head_sums(src, b0, m):
                for n in range(NT):
                    last = mm(bank(b0 + n // 2)[:, (n % 2) * T:(n % 2 + 1) * T], m[:], src[:, n, :], start=(n % 2 == 0),
                              stop=True, skip_group_check=True)
                return last

            pe.wait_ge(*at_step("reset_built"))
            pe.wait_ge(*at_step("kk_sq"))
            pe.wait_ge(*at_step("a_out"))
            head_sums(bonus, 4, head_ones).then_inc(step("kk_sum"), 1)
            pe.wait_ge(*at_step("rk"))
            pe.wait_ge(*at_step("g_out"))
            head_sums(bt_f, 0, head_ones).then_inc(step("rk_sum"), 1)

            def inverse(call, lv, nt, x, xt, z):
                base = sum(4 * n for n in INV_LEVELS[:call])
                xb = base + 4 * call
                for k, n in enumerate(lv):
                    for b in range(4):
                        pe.wait_ge(S("inv_x_out"), xb + 4 * k + b + 1)
                        for u in range(4):
                            last = mm(bank(b)[:, u * P:(u + 1) * P], nt[:, 4 * b + u, :], x[:, 4 * b + u, :],
                                      start=(u == 0), stop=True, skip_group_check=True)
                        last.then_inc(S("inv_z"), 1)
                    for b in range(4):
                        pe.wait_ge(S("inv_z_out"), base + 4 * k + b + 1)
                        if b >= 2:
                            pe.wait_ge(S("inv_x_out"), xb + 4 * (k + 1) + b - 1)
                        for o in range(2):
                            for u in range(4):
                                i = 4 * b + u
                                last = mm(bank(4 + 2 * (b % 2) + o)[:, u * P:(u + 1) * P], z[:, i, :] if o else xt[:, i, :],
                                          xt[:, i, :] if o else z[:, i, :], start=(u == 0), stop=True, skip_group_check=True)
                        last.then_inc(S("inv_x"), 1)
                pe.wait_ge(S("inv_x_out"), xb + 4 * (len(lv) + 1))

            pe.wait_ge(*at_step("rw_fm"))
            for cp in range(2):
                tk = slice(cp * P, (cp + 1) * P)
                if cp:
                    pe.wait_ge(S("rw_state"), 3)
                    pe.wait_ge(S("rw_y_out"), 2)
                for m, src in enumerate((at_f, bt_f, Kw, Vw)):
                    for n in range(NT):
                        last = tr(bank(2 * m + n // 4)[:, (n % 4) * P:(n % 4 + 1) * P], src[:, n, tk], ident[:])
                    last.then_inc(S("rw_tok"), 1)
                pe.wait_ge(S("rw_tok_out"), 4 * cp + 4)
                q = 0
                for b in range(4):
                    for m, (l, r) in enumerate(((at_f, bt_f), (bt_f, at_f), (Kw, at_f), (bt_f, Rw), (Kw, Rw))):
                        wait(pe, S("rw_gram_out"), 20 * cp + q - 7)
                        for u in range(4):
                            n, h = (4 * b + u) % 8, 64 * (b // 2)
                            last = mm(bank(q % 8)[:, u * P:(u + 1) * P], l[h:h + 64, n, tk], r[h:h + 64, n, tk],
                                      start=(u == 0), stop=True, skip_group_check=True)
                        last.then_inc(S("rw_gram"), 1)
                        q += 1
                pe.wait_ge(S("rw_gram_out"), 20 * (cp + 1))
                inverse(cp, range(1, 6), nt_r, x_r, xt_r, z_r)
                for x in range(16):
                    last = mm(bank(x // 8)[:, (x % 8) * 64:(x % 8 + 1) * 64], akt[:, x, :], v_tok2[:, hc(x)],
                              start=(x % 8 == 0), stop=True, skip_group_check=True)
                last.then_inc(S("rw_z1"), 1)
                for x in range(16):
                    n = x % 8
                    last = mm(bank(2 + n // 4)[hr(x), (n % 4) * P:(n % 4 + 1) * P], at_tok[:, hc(x)],
                              xt_r[:, x, :], start=(n % 4 == 0), stop=True, skip_group_check=True)
                last.then_inc(S("rw_wt"), 1)
                pe.wait_ge(S("rw_z1_out"), cp + 1)
                for x in range(16):
                    last = mm(bank(4 + x // 8)[:, (x % 8) * 64:(x % 8 + 1) * 64], xt_r[:, x, :], z1[:, x * 64:(x + 1) * 64],
                              start=(x % 8 == 0), stop=True, skip_group_check=True)
                last.then_inc(S("rw_uv"), 1)
                pe.wait_ge(S("rw_wt_out"), cp + 1)
                pe.wait_ge(S("rw_uv_out"), cp + 1)
                for c in range(2):
                    g = 2 * cp + c
                    tp, tc = slice(64 * c, 64 * c + 64), slice(g * CH, (g + 1) * CH)
                    pe.wait_ge(S("rw_state"), g + 1)
                    for x in range(16):
                        last = mm(bank(6 + x // 8)[tp, (x % 8) * 64:(x % 8 + 1) * 64], wt[hr(x), x % 8, tp],
                                  state[hr(x), x % 8, :], start=(x % 8 == 0), stop=True, skip_group_check=True)
                    last.then_inc(S("rw_u_mm"), 1)
                    for x in range(16):
                        n = x % 8
                        last = mm(bank(c)[hr(x), n * 64:(n + 1) * 64], state[hr(x), n, :], Rw[hr(x), n, tc],
                                  start=(n == 0), stop=False, skip_group_check=True)
                    last.then_inc(S("rw_y0_mm"), 1)
                    pe.wait_ge(S("rw_u"), g + 1)
                    for x in range(16):
                        o = bank(2 + c)[hr(x), (x % 8) * 64:(x % 8 + 1) * 64]
                        mm(o, bt_tok[tp, hc(x)], u_tok[tp, x * 64:(x + 1) * 64], start=(x % 8 == 0), stop=False,
                           skip_group_check=True)
                        last = mm(o, kt_tok[tp, hc(x)], v_tok2[tp, hc(x)], start=False, stop=True, skip_group_check=True)
                    last.then_inc(S("rw_s_mm"), 1)
                    pe.wait_ge(S("rw_y0_mm"), g + 1)
                    for x in range(16):
                        o = bank(c)[hr(x), (x % 8) * 64:(x % 8 + 1) * 64]
                        mm(o, u_tok[tp, x * 64:(x + 1) * 64], rbt[tp, x, tp], start=False, stop=False,
                           skip_group_check=True)
                        last = mm(o, v_tok2[tp, hc(x)], rkt[tp, x, tp], start=False, stop=True, skip_group_check=True)
                    last.then_inc(S("rw_y_mm"), 1)
            pe.wait_ge(S("rw_y_out"), 4)
            pe.wait_ge(S("rw_state"), 5)
            head_sums(y_rw, 0, head_ones).then_inc(step("gn_mean"), 1)
            pe.wait_ge(*at_step("gn_sq"))
            head_sums(gn_sq, 4, head_ones).then_inc(step("gn_var"), 1)

            pe.wait_ge(*at_step("gn_out"))
            pe.wait_ge(*at_step("gd_cum"))
            for c in range(2):
                tk = slice(c * P, (c + 1) * P)
                mm(bank(0)[:, c * H:(c + 1) * H], gn[4][:, tk], ident[0:H, 0:H], start=(c == 0), stop=True,
                   skip_group_check=True)
                mm(bank(0)[:, (2 + c) * H:(3 + c) * H], gb[:, tk], ident[0:H, 0:H], start=False, stop=True,
                   skip_group_check=True)
            mm(bank(0)[:, 4 * H:5 * H], gn[7][:, 0:P], ident[0:H, 0:H], start=False, stop=False, skip_group_check=True)
            mm(bank(0)[:, 4 * H:5 * H], gn[5][:, 0:P], ident[0:H, 0:H], start=False, stop=True,
               skip_group_check=True).then_inc(step("gd_tok"), 1)
            pe.wait_ge(*at_step("gd_sq"))
            head_sums(l2s, 4, ones).then_inc(step("gd_l2"), 1)
            pe.wait_ge(*at_step("gd_qk"))
            pe.wait_ge(*at_step("gd_tok_out"))
            for c in range(2):
                tk = slice(c * P, (c + 1) * P)
                for b, src in ((0, cv[:, 4:8]), (2, cv[:, 0:4])):
                    for h in range(4):
                        last = mm(bank(b + c)[:, h * P:(h + 1) * P], cv[:, 4 + h, tk], src[:, h, tk], start=(h == 0),
                                  stop=True, skip_group_check=True)
            last.then_inc(step("gd_gram"), 1)
            pe.wait_ge(*at_step("gd_rows"))
            pe.wait_ge(*at_step("selrow2_built"))
            for o in range(2):
                for c in range(2):
                    tk = slice(c * P, (c + 1) * P)
                    for b in range(2):
                        B = 4 + 2 * c + b
                        if o:
                            pe.wait_ge(S("gd_gam"), 2 * c + b + 1)
                        for u in range(4):
                            h, dst = 4 * b + u, bank(B)[:, u * P:(u + 1) * P]
                            mm(dst, (ngm if o else gm)[:, h, tk], ones8[:, 0:P], start=(u == 0), stop=False, skip_group_check=True)
                            mm(dst, selrow2[:, h, :], gn[4 if o else 5][:, tk], start=False, stop=False, skip_group_check=True)
                            last = mm(dst, ident[:], neg_ui[:] if o else neg_ls[:], start=False, stop=True,
                                      skip_group_check=True)
                        last.then_inc(S("gd_diff"), 1)
            pe.wait_ge(*at_step("gd_n"))
            pe.wait_ge(S("gd_gam"), 8)
            for b in range(4):
                for u in range(4):
                    last = tr(bank(4 + b)[:, u * P:(u + 1) * P], x_g[:, 4 * b + u, :], ident[:])
                last.then_inc(S("gd_nt"), 1)
            pe.wait_ge(S("inv_x_out"), 4 * (5 + 5) + 4 * 2 + 4)
            inverse(2, range(1, 7), nt_g, x_g, xt_g, z_g)
            for m in range(4):
                for u in range(4):
                    last = tr(bank(m)[:, u * P:(u + 1) * P], cv[:, 8 + 4 * (m % 2) + u, (m // 2) * P:(m // 2 + 1) * P], ident[:])
                last.then_inc(S("gd_v_t"), 1)
            for c in range(2):
                for u in range(4):
                    last = tr(bank(4 + c)[:, u * P:(u + 1) * P], cv[:, 4 + u, c * P:(c + 1) * P], ident[:])
                last.then_inc(S("gd_k_t"), 1)
            for b in range(4):
                pe.wait_ge(S("gd_v_beta"), 4)
                for u in range(4):
                    last = mm(bank(b)[:, u * P:(u + 1) * P], xt_g[:, 4 * b + u, :], v_beta[:, 4 * b + u, :], start=(u == 0),
                              stop=True, skip_group_check=True)
                last.then_inc(S("gd_u"), 1)
            pe.wait_ge(*at_step("gd_k_bg"))
            for h in range(H):
                last = mm(bank(4 + h // 4)[:, (h % 4) * P:(h % 4 + 1) * P], k_bg[:, 8 + h, :], xt_g[:, 8 + h, :],
                          start=(h % 4 == 0), stop=True, skip_group_check=True)
            last.then_inc(step("gd_w"), 1)
            pe.wait_ge(S("gd_u_out"), 4)
            for h in range(H):
                last = mm(bank(6 + h // 4)[:, (h % 4) * P:(h % 4 + 1) * P], k_g[:, h, :], u_g[:, h, :],
                          start=(h % 4 == 0), stop=True, skip_group_check=True)
            last.then_inc(step("gd_s"), 1)
            for h in range(H):
                last = mm(bank(h // 4)[:, (h % 4) * P:(h % 4 + 1) * P], selrow2[:, h, :], gn[6][:, P:T],
                          start=(h % 4 == 0), stop=True, skip_group_check=True)
            last.then_inc(step("gd_eg"), 1)
            pe.wait_ge(*at_step("gd_w_out"))
            pe.wait_ge(*at_step("gd_s_out"))
            for h in range(H):
                last = mm(bank(4 + h // 4)[:, (h % 4) * P:(h % 4 + 1) * P], w_g[:, h, :], s_g[:, h, :],
                          start=(h % 4 == 0), stop=True, skip_group_check=True)
            last.then_inc(step("gd_ws"), 1)
            pe.wait_ge(*at_step("gd_qg"))
            pe.wait_ge(*at_step("gd_vn"))
            for h in range(H):
                b = bank(h // 2)
                o = (h % 2) * T
                mm(b[:, o:o + P], u_g[:, h, :], aqk[:, h, :], start=(h % 2 == 0), stop=True, skip_group_check=True)
                mm(b[:, o + P:o + T], s_g[:, h, :], q_g[:, h, :], start=False, stop=False, skip_group_check=True)
                last = mm(b[:, o + P:o + T], v_new[:, h, :], aqk[:, 8 + h, :], start=False, stop=True, skip_group_check=True)
            last.then_inc(step("gd_o"), 1)
            pe.wait_ge(*at_step("gd_o_sq"))
            head_sums(o_sq, 4, ones).then_inc(step("gd_o_sum"), 1)
            pe.wait_ge(*at_step("gd_o_out"))
            body(wo2, 0, y2_parts, 0)
            body(wo2, 1)
            normed(up2, 3, SQ[1])
            downs(dn2, 2)
            norm_sums(4, SQ[0])
            pe.wait_ge(h_ready, 17)
            for n in range(8):
                t, b = n % 2, n // 2
                for k in range(4):
                    last = tr(bank(n)[:, k * P:(k + 1) * P], U[0][:, 4 * b + k, t * P:(t + 1) * P], ident[:])
                last.then_inc(out_turned, 1)

        @block.scalar
        def _(act):
            settle = settler(act, "scalar")
            A = nc.scalar.activation

            def squares(n, q, sq, s, ready, sq2=None):
                act.wait_ge(s, ready)
                k = slice(4 * q, 4 * q + 4)
                last = A(sq[:, k, :], X[:, k, :], ACT.Square)
                if sq2:
                    for t in range(4 * q, 4 * q + 4):
                        last = A(sq2[:, t, :], X[:, t, :], ACT.Square, scale=pcol("g_final", t))
                last.then_inc(n_sq, 1)

            def high(n, q, u):
                act.wait_ge(n_u, 4 * n + q + 1)
                k = slice(4 * q, 4 * q + 4)
                A(Hh[:, k, :], u[:, k, :], ACT.Copy).then_inc(n_hi, 1)

            def root(k, r=rstd):
                act.wait_ge(n_mean, k)
                A(r[:], r[:], ACT.Sqrt).then_inc(n_root, 1)

            def chunks(g, i, j0, j1):
                for j in range(j0, j1):
                    act.wait_ge(landed[j % g.ring], g.landed(i, j))
                    wait(act, chunks_used, g.chunk(i, j) - g.hi + 1)
                    A(hi[j % g.hi][:], raw[j % g.ring][:], ACT.Copy).then_inc(hi_ready, 1)

            def split(g, i, out_of, j0=0):
                for j in range(j0, g.per):
                    chunks(g, i, j, j + 1)
                    if j == 1 and not (isinstance(i, int) and i == 0):
                        out_of(i - 1, g.ns - 1)
                    elif j > 1 and j - 2 in g.ends:
                        out_of(i, g.ends[j - 2])

            def strip_done(e, g, i, s):
                end = [j for j in g.ends if g.ends[j] == s][0]
                e.wait_ge(chunks_used, g.chunk(i, end) + 1)

            def nothing(i, s):
                pass

            def rest(g, out_of):
                split(g, 0, out_of, 4)
                with act.Fori(1, g.bodies) as i:
                    split(g, i, out_of)

            for q in range(4):
                squares(0, q, SQ[0], x_ready, q + 1)
            for q in range(4):
                high(0, q, U[0])
            chunks(in1, 0, 0, 4)
            root(1)
            rest(in1, nothing)

            def sp_e(n, x):
                act.wait_ge(sp_abs, n + 1)
                A(x, x, ACT.Exp, scale=-1.0).then_inc(sp_exp, 1)

            sp_e(0, spt[1][:])
            sp_e(1, fT[1][:])
            for b in range(4):
                act.wait_ge(v_turned, b + 1)
                A(vtok[:, :, 2 * b * P:2 * (b + 1) * P].rearrange("p t (h c) -> p h t c", h=2),
                  bank(b).rearrange("p (h t c) -> p h t c", h=2, t=2), ACT.Copy).then_inc(v_tok, 1)
            for b0, name, dst, done in ((0, "b_rg", rx, r_sig), (4, "b_ig", t2, i_sig)):
                for n in range(NT):
                    act.wait_ge(gates_mm, b0 + n // 2 + 1)
                    A(dst[:, n, :], bank(b0 + n // 2)[:, (n % 2) * T:(n % 2 + 1) * T], ACT.Sigmoid,
                      bias=pcol(name, n)).then_inc(done, 1)
            A(t4b[:], ry, ACT.Square).then_inc(gelu_sq, 1)
            act.wait_ge(gelu_arg, 1)
            A(t4b[:], t4b[:], ACT.Sigmoid, scale=1.5957691216057308).then_inc(gelu_sig, 1)
            act.wait_ge(lam_ready, 1)
            act.wait_ge(r_sig, NT)
            for n in range(NT):
                A(t3[:, n, :], rx[:, n, :], ACT.Exp, scale=lam8[:, n:n + 1]).then_inc(lru_a, 1)
            for n in range(NT):
                last = A(rx[:, n, :], rx[:, n, :], ACT.Tanh, scale=lam8[:, n:n + 1])
            last.then_inc(lru_th, 1)
            act.wait_ge(lru_a, NT)
            act.wait_ge(lru_iu, 1)
            A(t2[:], t3[:], ACT.Square).then_inc(lru_sq, 1)
            act.wait_ge(lru_var, 1)
            A(rx, rx, ACT.Sqrt).then_inc(lru_root, 1)

            def soft(h):
                act.wait_ge(sc_max, h + 1)
                if h >= 2:
                    act.wait_ge(sc_t, h - 1)
                b = bank(4 + h % 2)
                z = 2 * (h % 2)
                A(probs[:, h % 2, 0:P], b[:, 0:P], ACT.Exp, bias=neg_max[:, z:z + 1], accum_out=rowsum[:, z:z + 1])
                A(probs[:, h % 2, P:3 * P], b[:, P:3 * P], ACT.Exp, bias=neg_max[:, z + 1:z + 2],
                  accum_out=rowsum[:, z + 1:z + 2]).then_inc(sc_exp, 1)

            def turned(h):
                act.wait_ge(sc_t, h + 1)
                if h >= 2:
                    act.wait_ge(sc_o, h - 1)
                A(probsT[:, h % 2, :], bank(6 + h % 2)[:, 0:3 * P], ACT.Copy).then_inc(sc_pt, 1)

            for h in range(H + 1):
                if h < H:
                    soft(h)
                if h >= 1:
                    turned(h - 1)

            def gate(i, s):
                if s % 2 == 0:
                    act.wait_ge(strips_out, mer.strip(i, s) + 1)
                    A(sg[:], sg[:], ACT.Sigmoid).then_inc(gate_sig, 1)
                elif s % 6 == 5:
                    c = s // 6
                    act.wait_ge(merged_sum, i * 4 + 2 * c + 3)
                    m = slice(4 * c, 4 * c + 4) if isinstance(i, int) else bass.ds(8 * i + 4 * c, 4)
                    if isinstance(i, int):
                        m = slice(8 * i + 4 * c, 8 * i + 4 * c + 4)
                    A(Mh[:, m, :], merged[:, m, :], ACT.Copy).then_inc(merged_hi, 1)
            act.wait_ge(sc_o, H)
            chunks(mer, 0, 0, 2)
            act.wait_ge(sc_y, H)
            A(yh[1][:], t2[:], ACT.Copy).then_inc(y_hi, 1)
            A(yh[2][:], t4[:], ACT.Copy).then_inc(y_hi, 1)
            split(mer, 0, gate, 2)
            split(mer, 1, gate)
            chunks(wo1, 0, 0, 2)
            gate(1, 11)

            def residual_high(g, n):
                def f(i, s):
                    squares(n, 2 * i + s, SQ[1], strips_out, g.strip(i, s) + 1)
                    high(n, 2 * i + s, U[1])
                return f

            def ffn_gate(g, n):
                def f(i, s):
                    k = n * g.bodies
                    if s == 0:
                        act.wait_ge(strips_out, g.strip(i, 0) + 1)
                        wait(act, ffn_split, k + i)
                        A(act_up[:], act_gate[:], ACT.Sigmoid).then_inc(ffn_sig, 1)
                    else:
                        act.wait_ge(ffn_up, k + i + 1)
                        A(Fh[:, bass.ds(4 * i, 4), :], act_up[:], ACT.Copy).then_inc(ffn_hi, 1)
                return f

            def out_ffn(wo, up, dn, n_norm, n, rhs):
                f = residual_high(wo, n_norm)
                split(wo, 0, f, rhs)
                split(wo, 1, f)
                chunks(up, 0, 0, 2)
                f(1, 1)
                chunks(up, 0, 2, 4)
                root(n_root_of[n_norm])
                f = ffn_gate(up, n)
                rest(up, f)
                chunks(dn, 0, 0, 2)
                f(up.bodies - 1, 1)
                chunks(dn, 0, 2, 4)
                with act.Fori(1, dn.bodies - 1) as i:
                    chunks(dn, i, 0, 4)

            n_root_of = {1: 2, 3: 5}
            out_ffn(wo1, up1, dn1, 1, 0, 2)
            chunks(dn1, dn1.bodies - 1, 0, 4)
            for q in range(4):
                squares(2, q, SQ[0], x_ready, 5 + q, SQ2)
                high(2, q, U[0])
                if 0 < q < 3:
                    chunks(in2, 0, q - 1, q)
            chunks(in2, 0, 2, 4)
            root(3, rstd_final1)
            root(4)
            split(in2, 0, nothing, 4)
            with act.Fori(1, 4) as i:
                split(in2, i, nothing)
            for i, h, part in ((4, 0, "qk"), (5, 1, "v")):
                chunks(in2, i, 0, 6)
                act.wait_ge(*at_step(f"gd_cv_{part}"))
                A(cv[:, 8 * h:8 * h + 8, :], spare, ACT.Sigmoid).then_inc(step(f"gd_sig_{part}"), 1)
                chunks(in2, i, 6, 8)
            act.wait_ge(*at_step("lora_mm"))
            act.wait_ge(*at_step("lora_in"))
            A(lp[0:64, 0, :], lp[0:64, 0, :], ACT.Tanh)
            A(lp[:, 1, :], lp[:, 1, :], ACT.Sigmoid)
            A(lp[0:32, 2, :], lp[0:32, 2, :], ACT.Sigmoid).then_inc(step("lora_act"), 1)
            for b0, dst, bias, got, done in ((0, ld, "rwkv_w0_2", "zw_mm", "ld_out"), (4, a_lr, "rwkv_a0_2", "za_mm", "a_out")):
                act.wait_ge(*at_step(got))
                for n in range(NT):
                    last = A(dst[:, n, :], bank(b0 + n // 2)[:, (n % 2) * T:(n % 2 + 1) * T], ACT.Sigmoid, bias=pcol(bias, n))
                last.then_inc(step(done), 1)
            act.wait_ge(*at_step("g_mm"))
            for b in range(4):
                last = A(gate2[:, 2 * b:2 * b + 2, :].rearrange("p k n -> p (k n)"), bank(b), ACT.Copy)
            last.then_inc(step("g_out"), 1)
            act.wait_ge(*at_step("kk"))
            A(bonus[:], kk[:], ACT.Square).then_inc(step("kk_sq"), 1)
            act.wait_ge(*at_step("kk_mean"))
            A(at_f[:], at_f[:], ACT.Sqrt).then_inc(step("kk_root"), 1)
            act.wait_ge(*at_step("l_prev"))
            A(ld[:], ld[:], ACT.Exp).then_inc(step("e_prev"), 1)
            act.wait_ge(*at_step("at_made"))
            A(ld[:], cum[:], ACT.Exp).then_inc(step("e_plus"), 1)
            A(cum[:], cum[:], ACT.Exp, scale=-1.0).then_inc(step("e_minus"), 1)
            for cp in range(2):
                for m, dst in enumerate((at_tok, bt_tok)):
                    act.wait_ge(S("rw_tok"), 4 * cp + m + 1)
                    A(dst[:], psum[:, 2 * m:2 * m + 2, :].rearrange("p b n -> p (b n)"), ACT.Copy).then_inc(S("rw_tok_out"), 1)
                act.wait_ge(S("rw_z1"), cp + 1)
                A(z1[:], psum[:, 0:2, :].rearrange("p b n -> p (b n)"), ACT.Copy).then_inc(S("rw_z1_out"), 1)
                act.wait_ge(S("rw_wt"), cp + 1)
                A(wt[:].rearrange("p k n -> p (k n)"), psum[:, 2:4, :].rearrange("p b n -> p (b n)"), ACT.Copy).then_inc(S("rw_wt_out"), 1)
                act.wait_ge(S("rw_uv"), cp + 1)
                A(uv[:], psum[:, 4:6, :].rearrange("p b n -> p (b n)"), ACT.Copy).then_inc(S("rw_uv_out"), 1)
                for c in range(2):
                    g = 2 * cp + c
                    act.wait_ge(S("rw_y_mm"), g + 1)
                    A(y_rw[:, :, g * CH:(g + 1) * CH], bank(c).rearrange("p (k n) -> p k n", k=NT), ACT.Copy).then_inc(S("rw_y_out"), 1)
            act.wait_ge(*at_step("gn_c"))
            A(gn_sq[:], y_rw[:], ACT.Square).then_inc(step("gn_sq"), 1)
            act.wait_ge(*at_step("gn_m"))
            A(gn_r[:], gn_r[:], ACT.Sqrt).then_inc(step("gn_root"), 1)
            A(gb[:], gb[:], ACT.Sigmoid).then_inc(step("gd_beta"), 1)
            sp_e(2, gn[1][:])
            A(alog[:], alog[:], ACT.Exp).then_inc(step("gd_expA"), 1)
            act.wait_ge(*at_step("gd_cum"))
            A(gn[6][:], gn[4][:], ACT.Exp).then_inc(S("gd_eg_rows"), 1)
            act.wait_ge(*at_step("gn_out"))
            A(l2s[:], cv[:, 0:8, :], ACT.Square).then_inc(step("gd_sq"), 1)
            act.wait_ge(*at_step("gd_l2_mean"))
            A(l2s[:], l2s[:], ACT.Sqrt).then_inc(step("gd_l2_root"), 1)
            act.wait_ge(*at_step("gd_tok_out"))
            A(tokp[:, 4:6, :], tokp[:, 0:2, :], ACT.Exp)
            A(tokp[:, 6, :], tokp[:, 6, :], ACT.Exp).then_inc(step("gd_tok_exp"), 1)
            for o in range(2):
                for k in range(4):
                    act.wait_ge(S("gd_diff"), 4 * o + k + 1)
                    A((gam_t if o else gam)[:, 4 * k:4 * k + 4, :].rearrange("p k n -> p (k n)"), bank(4 + k), ACT.Exp).then_inc(S("gd_gam"), 1)
            for k in range(4):
                act.wait_ge(S("gd_nt"), k + 1)
                A(nt_g[:, 4 * k:4 * k + 4, :].rearrange("p k n -> p (k n)"), bank(4 + k), ACT.Copy).then_inc(S("gd_nt_out"), 1)
            for m in range(4):
                act.wait_ge(S("gd_v_t"), m + 1)
                for u in range(4):
                    h, c = 4 * (m % 2) + u, m // 2
                    last = A(v_beta[:, 8 * c + h, :], bank(m)[:, u * P:(u + 1) * P], ACT.Copy, scale=tokp[:, 2 + c, h:h + 1])
                last.then_inc(S("gd_v_beta"), 1)
            for b in range(4):
                act.wait_ge(S("gd_u"), b + 1)
                A(u_g[:, 4 * b:4 * b + 4, :].rearrange("p k n -> p (k n)"), bank(b), ACT.Copy).then_inc(S("gd_u_out"), 1)
            act.wait_ge(*at_step("gn_out"))
            A(Mh[:, 0:8, :], yfin[:, 0:8, :], ACT.Copy).then_inc(y2_hi, 1)
            act.wait_ge(*at_step("gd_w"))
            A(w_g[:].rearrange("p k n -> p (k n)"), psum[:, 4:6, :].rearrange("p b n -> p (b n)"), ACT.Copy).then_inc(step("gd_w_out"), 1)
            act.wait_ge(*at_step("gd_s"))
            A(s_g[:].rearrange("p k n -> p (k n)"), psum[:, 6:8, :].rearrange("p b n -> p (b n)"), ACT.Copy).then_inc(step("gd_s_out"), 1)
            act.wait_ge(*at_step("gd_o"))
            for b in range(4):
                last = A(o_g[:, 2 * b:2 * b + 2, :].rearrange("p k n -> p (k n)"), bank(b), ACT.Copy)
            last.then_inc(step("gd_o_out"), 1)
            act.wait_ge(*at_step("gd_o_out"))
            A(o_sq[:], o_g[:], ACT.Square).then_inc(step("gd_o_sq"), 1)
            A(z_sig[:], proj2[:, 40:48, :], ACT.Sigmoid).then_inc(step("gd_z_sig"), 1)
            chunks(wo2, 0, 0, 2)
            act.wait_ge(*at_step("gd_o_mean"))
            A(o_r[:], o_r[:], ACT.Sqrt).then_inc(step("gd_o_root"), 1)
            for q in range(2):
                act.wait_ge(y2_made, q + 1)
                A(Mh[:, 8 + 4 * q:12 + 4 * q, :], yfin[:, 8 + 4 * q:12 + 4 * q, :], ACT.Copy).then_inc(y2_hi, 1)
            out_ffn(wo2, up2, dn2, 3, 1, 2)
            chunks(dn2, dn2.bodies - 1, 0, 4)
            for q in range(4):
                squares(4, q, SQ[0], x_ready, 9 + q)
            root(6)
            for n in range(0, 8, 2):
                act.wait_ge(out_turned, n + 1)
                A(out_tokens[:, n % 2, n // 2 * 512:(n // 2 + 1) * 512], bank(n), ACT.Copy).then_inc(out_copied, 1)

        @block.vector
        def _(dve):
            settle = settler(dve, "vector")
            V = nc.vector
            for q in range(4):
                dve.wait_ge(x_turned, 2 * q + 2)
                V.tensor_copy(X[:, 4 * q:4 * q + 4, :], pair(q)).then_inc(x_ready, 1)
            dve.wait_ge(par_turned, 1)
            V.tensor_copy(par1[:], bank(0)[:, 0:ncols]).then_inc(par_ready, 1)
            dve.wait_ge(par_ready, 1)
            dve.wait_ge(x_ready, 4)

            def gained(n, q, u, gain):
                for k in range(4 * q, 4 * q + 4):
                    last = V.tensor_scalar(u[:, k, :], X[:, k, :], pcol(gain, k), None, ALU.mult)
                last.then_inc(n_u, 1)

            def low_part(n, q, u):
                dve.wait_ge(n_hi, 4 * n + q + 1)
                k = slice(4 * q, 4 * q + 4)
                V.tensor_tensor(Hl[:, k, :], u[:, k, :], Hh[:, k, :].bitcast(F32), ALU.subtract).then_inc(h_ready, 1)

            def inverse_root(k, n, eps, r=rstd, m=0, times=None):
                dve.wait_ge(n_sum, n)
                b = bank(7)[:, m * T:(m + 1) * T]
                if times is not None:
                    settle(V.scalar_tensor_tensor(r[:], b, 1.0 / D, times[:], ALU.mult, ALU.mult))
                    settle(V.tensor_tensor(r[:], r[:], times[:], ALU.mult))
                    V.tensor_scalar(r[:], r[:], eps, None, ALU.add).then_inc(n_mean, 1)
                else:
                    V.tensor_scalar(r[:], b, 1.0 / D, eps, ALU.mult, ALU.add).then_inc(n_mean, 1)
                dve.wait_ge(n_root, k)
                settle(V.reciprocal(r[:], r[:]))

            def chunks(g, i, j0, j1):
                for j in range(j0, j1):
                    dve.wait_ge(hi_ready, g.chunk(i, j) + 1)
                    r = j % g.ring
                    V.tensor_tensor(lo[r][:], raw[r][:], hi[j % g.hi][:].bitcast(F32), ALU.subtract).then_inc(lo_ready, 1)

            def rstds(rows=P, n=4):
                return rstd[0:rows, :].unsqueeze(1).to_broadcast([rows, n, T])

            def split(g, i, out_of, j0=0, later=None, last=None):
                for j in range(j0, g.per):
                    chunks(g, i, j, j + 1)
                    first = isinstance(i, int) and i == 0
                    for d, f in enumerate((out_of, later, last)):
                        if f is None:
                            continue
                        if j == d and not first:
                            f(i - 1, g.ns - 1)
                        elif j > d and j - 1 - d in g.ends:
                            f(i, g.ends[j - 1 - d])

            def strip_done(e, g, i, s):
                end = [j for j in g.ends if g.ends[j] == s][0]
                e.wait_ge(chunks_used, g.chunk(i, end) + 1)

            def nothing(i, s):
                pass

            def softplus(n, z, e, tmp, w2, res):
                V.scalar_tensor_tensor(e, z, -1.0, z, ALU.mult, ALU.max).then_inc(sp_abs, 1)
                dve.wait_ge(sp_exp, n + 1)
                settle(V.tensor_scalar(tmp, e, 2.0, None, ALU.add))
                settle(V.reciprocal(tmp, tmp))
                settle(V.tensor_tensor(tmp, tmp, e, ALU.mult))
                settle(V.tensor_tensor(w2, tmp, tmp, ALU.mult))
                settle(V.tensor_scalar(res, w2, 1.0 / 17, None, ALU.mult))
                for m in range(15, 1, -2):
                    settle(V.scalar_tensor_tensor(res, res, 1.0 / m, w2, ALU.add, ALU.mult))
                settle(V.scalar_tensor_tensor(res, res, 1.0, tmp, ALU.add, ALU.mult))
                settle(V.tensor_scalar(tmp, z, 0.0, None, ALU.max))
                settle(V.scalar_tensor_tensor(res, res, 2.0, tmp, ALU.mult, ALU.add))

            def to_proj(g, dst):
                def f(i, s):
                    strip_done(dve, g, i, s)
                    V.tensor_tensor(dst[:, bass.ds(i * 8 + s * 4, 4), :], pair(s % 2), rstds(), ALU.mult).then_inc(strips_out, 1)
                return f

            def rest(g, out_of):
                split(g, 0, out_of, 4)
                with dve.Fori(1, g.bodies) as i:
                    split(g, i, out_of)

            for q in range(4):
                gained(0, q, U[0], "g_mix")
            for q in range(4):
                low_part(0, q, U[0])
            c0, c1 = col["attn_norm_w_2"], col["g_final"]
            settle(V.tensor_tensor(par1[:, c0:c0 + KT], par1[:, c0:c0 + KT], par1[:, c1:c1 + KT], ALU.mult))
            chunks(in1, 0, 0, 4)
            inverse_root(1, 1, EPS1)
            f = to_proj(in1, proj)
            rest(in1, f)
            f(in1.bodies - 1, 1)

            c0 = col["lru_lambda"]
            settle(V.tensor_scalar(spt[0][:], par1[:, c0:c0 + NT], -1.0, None, ALU.mult))
            softplus(0, spt[0][:], spt[1][:], spt[2][:], spt[3][:], lam8[:])
            V.tensor_scalar(lam8[:], lam8[:], -8.0, None, ALU.mult).then_inc(lam_ready, 1)
            dve.wait_ge(f_logits, 1)
            settle(V.tensor_tensor(fT[0][:], bank(7)[0:H, 0:T], rstd[0:H, :], ALU.mult))
            settle(V.tensor_scalar(fT[0][:], fT[0][:], bfor[:], -1.0, ALU.add, ALU.mult))
            V.memset(ones8[:], 1.0).then_inc(f_rows, 1)
            softplus(1, fT[0][:], fT[1][:], fT[2][:], fT[3][:], neg_f[:])
            settle(V.tensor_tensor_scan(fT[0][:], ones8[:], neg_f[:], 0.0, ALU.mult, ALU.subtract))
            V.tensor_scalar(neg_f[:], fT[0][:], -1.0, None, ALU.mult).then_inc(f_rows, 1)
            dve.wait_ge(mix_tables, 1)
            for h in range(H):
                last = V.tensor_scalar(fmask[:, h, :], fT[0][:], ident[0:H, h:h + 1], None, ALU.mult)
            last.then_inc(f_rows, 1)
            dve.wait_ge(strips_out, in1.sbase + in1.ns * in1.bodies)
            qs = proj[:, 2 * NT:3 * NT, :]
            V.tensor_scalar(qs, qs, float(P) ** -0.5, None, ALU.mult).then_inc(q_scaled, 1)
            dve.wait_ge(f_rows, 3)
            pin = proj[:, 5 * NT:6 * NT, :]
            src, lo_t = pin, 0
            for w, dst, n0 in ((1, t1, 0), (2, t2, 2), (4, t3, 4), (8, t4, 6)):
                V.tensor_tensor(dst[:, n0:, w:], src[:, n0:, w:], src[:, n0:, 0:T - w], ALU.add)
                settle(V.tensor_copy(dst[:, n0:, 0:w], src[:, n0:, 0:w]))
                src = dst
            for g, s in enumerate((t1, t2, t3, t4)):
                for n in range(2 * g, 2 * g + 2):
                    last = V.tensor_tensor(t1[:, n, :], s[:, n, :], recip_cnt[:, g, :], ALU.mult)
            settle(last)
            V.tensor_tensor(t1[:], t1[:], pin, ALU.subtract).then_inc(pool_in, 1)
            for g in range(4):
                dve.wait_ge(pool_mm, g + 1)
                for n in range(2 * g, 2 * g + 2):
                    last = V.tensor_scalar(t4[:, n, :], bank(4 + g)[:, (n % 2) * T:(n % 2 + 1) * T],
                                           pcol("pool_scale", n), None, ALU.mult)
                last.then_inc(pool_out, 1)
            for n in range(NT):
                last = V.tensor_scalar(t1b[:, n, :], rx[:, n, :], pcol("conv_w", 3 * NT + n), pcol("conv_b", n),
                                       ALU.mult, ALU.add)
            settle(last)
            for d in range(1, 4):
                for n in range(NT):
                    last = V.scalar_tensor_tensor(t1b[:, n, d:], rx[:, n, 0:T - d], pcol("conv_w", (3 - d) * NT + n),
                                                  t1b[:, n, d:], ALU.mult, ALU.add)
                if d < 3:
                    settle(last)
            last.then_inc(conv_u, 1)
            dve.wait_ge(gelu_sq, 1)
            settle(V.tensor_scalar(t4b[:], t4b[:], 0.044715, 1.0, ALU.mult, ALU.add))
            V.tensor_tensor(t4b[:], t4b[:], ry, ALU.mult).then_inc(gelu_arg, 1)
            dve.wait_ge(i_sig, NT)
            dve.wait_ge(conv_u, 1)
            V.tensor_tensor(t1b[:], t1b[:], t2[:], ALU.mult).then_inc(lru_iu, 1)
            dve.wait_ge(gelu_sig, 1)
            V.tensor_tensor(ry, ry, t4b[:], ALU.mult)
            dve.wait_ge(lru_th, 1)
            dve.wait_ge(lru_sq, 1)
            settle(V.scalar_tensor_tensor(rx, t2[:], 1.0, rx, ALU.add, ALU.mult))
            V.tensor_scalar(rx, rx, -1.0, None, ALU.mult).then_inc(lru_var, 1)
            V.memset(t3[:, :, 0:1], 0.0)
            dve.wait_ge(lru_root, 1)
            settle(V.tensor_tensor(rx, rx, t1b[:], ALU.mult))
            flat = lambda t: t.rearrange("p k n -> p (k n)")
            settle(V.tensor_tensor_scan(flat(t1b[:]), flat(t3[:]), flat(rx), 0.0, ALU.mult, ALU.add))
            settle(V.tensor_tensor(t1b[:], t1b[:], ry, ALU.mult))
            settle(V.tensor_copy(yh[0][:], t1b[:]))
            V.tensor_tensor(yl[0][:], t1b[:], yh[0][:].bitcast(F32), ALU.subtract).then_inc(y_ready, 1)

            def row_max(h):
                dve.wait_ge(sc_mm, h + 1)
                if h >= 2:
                    dve.wait_ge(sc_exp, h - 1)
                b, z = bank(4 + h % 2), 2 * (h % 2)
                V.reduce_max(neg_max[:, z:z + 1], b[:, 0:P], AX_X)
                settle(V.reduce_max(neg_max[:, z + 1:z + 2], b[:, P:3 * P], AX_X))
                V.tensor_scalar(neg_max[:, z:z + 2], neg_max[:, z:z + 2], -1.0, None, ALU.mult).then_inc(sc_max, 1)

            def normalise(h):
                z = 2 * (h % 2)
                dve.wait_ge(sc_exp, h + 1)
                settle(V.reciprocal(rowsum[:, z:z + 2], rowsum[:, z:z + 2]))
                V.tensor_scalar(probs[:, h % 2, 0:P], probs[:, h % 2, 0:P], rowsum[:, z:z + 1], None, ALU.mult)
                V.tensor_scalar(probs[:, h % 2, P:3 * P], probs[:, h % 2, P:3 * P], rowsum[:, z + 1:z + 2], None,
                                ALU.mult).then_inc(sc_p, 1)

            def take(h):
                dve.wait_ge(sc_o, h + 1)
                V.tensor_copy(t2[:, h, :], bank(2 + h % 2)[:, 0:T]).then_inc(sc_y, 1)

            for h in range(H + 2):
                if h < H:
                    row_max(h)
                if 1 <= h <= H:
                    normalise(h - 1)
                if h >= 2:
                    take(h - 2)
            dve.wait_ge(sc_y, H)
            chunks(mer, 0, 0, 2)
            for b, y in ((1, t2), (2, t4)):
                dve.wait_ge(y_hi, b)
                V.tensor_tensor(yl[b][:], y[:], yh[b][:].bitcast(F32), ALU.subtract).then_inc(y_ready, 1)

            def merge(i, s):
                strip_done(dve, mer, i, s)
                if s % 2 == 0:
                    wait(dve, strips_out, mer.strip(i, s))
                    V.tensor_tensor(sg[:], pair(0), rstds(), ALU.mult).then_inc(strips_out, 1)
                    return
                b, c = s // 2 % 3, s // 6
                m = merged[:, bass.ds(i * 8 + 4 * c, 4), :]
                dst = m if b == 0 else gated[:]
                dve.wait_ge(gate_sig, i * 6 + s // 2 + 1)
                if b:
                    dve.wait_ge(merged_sum, i * 4 + 2 * c + b)
                V.tensor_tensor(dst, sg[:], pair(1), ALU.mult).then_inc(strips_out, 1)
                if b:
                    dve.wait_ge(strips_out, mer.strip(i, s) + 1)
                    V.tensor_tensor(m, m, gated[:], ALU.add).then_inc(merged_sum, 1)

            def merge_low(i, s):
                if s % 6 == 5:
                    c = s // 6
                    dve.wait_ge(merged_hi, i * 2 + c + 1)
                    k = bass.ds(i * 8 + 4 * c, 4)
                    V.tensor_tensor(Ml[0][:, k, :], merged[:, k, :], Mh[:, k, :].bitcast(F32), ALU.subtract).then_inc(merged_ready, 1)
            V.memset(gated[:, 0:1, 0:1], 0.0).then_inc(merged_sum, 1)
            split(mer, 0, merge, 2, None, merge_low)
            split(mer, 1, merge, 0, None, merge_low)
            chunks(wo1, 0, 0, 1)
            merge(1, 11)
            chunks(wo1, 0, 1, 3)
            merge_low(1, 11)

            def residual(g, n, gain):
                def f(i, s):
                    strip_done(dve, g, i, s)
                    r = X[:, 8 * i + 4 * s:8 * i + 4 * s + 4, :]
                    V.tensor_tensor(r, r, pair(s), ALU.add).then_inc(strips_out, 1)
                    dve.wait_ge(strips_out, g.strip(i, s) + 1)
                    gained(n, 2 * i + s, U[1], gain)
                return f

            def ffn(g, n):
                def f(i, s):
                    strip_done(dve, g, i, s)
                    k = n * g.bodies
                    if s == 0:
                        wait(dve, ffn_up, k + i)
                        V.tensor_tensor(act_gate[:], pair(0), rstds(), ALU.mult).then_inc(strips_out, 1)
                        return
                    dve.wait_ge(ffn_silu, k + i + 1)
                    V.tensor_tensor(act_up[:], pair(1), rstds(), ALU.mult).then_inc(strips_out, 1)
                    dve.wait_ge(strips_out, g.strip(i, 1) + 1)
                    V.tensor_tensor(act_up[:], act_gate[:], act_up[:], ALU.mult).then_inc(ffn_up, 1)

                def silu(i, s):
                    if s == 0:
                        dve.wait_ge(ffn_sig, n * g.bodies + i + 1)
                        V.tensor_tensor(act_gate[:], act_gate[:], act_up[:], ALU.mult).then_inc(ffn_silu, 1)

                def low(i, s):
                    if s == 1:
                        k = n * g.bodies
                        dve.wait_ge(ffn_hi, k + i + 1)
                        fh, fl = Fh[:, bass.ds(4 * i, 4), :], Fl[:, bass.ds(4 * i, 4), :]
                        V.tensor_tensor(fl, act_up[:], fh.bitcast(F32), ALU.subtract).then_inc(ffn_split, 1)
                return f, silu, low

            def out_ffn(wo, up, dn, n_norm, gain, eps, n, j0):
                f = residual(wo, n_norm, gain)
                low = lambda i, s: low_part(n_norm, 2 * i + s, U[1])
                split(wo, 0, f, j0, None, low)
                split(wo, 1, f, 0, None, low)
                chunks(up, 0, 0, 1)
                f(1, 1)
                chunks(up, 0, 1, 3)
                low(1, 1)
                chunks(up, 0, 3, 4)
                inverse_root({1: 2, 3: 5}[n_norm], n_norm + 1, eps)
                f, silu, low = ffn(up, n)
                split(up, 0, f, 4, silu, low)
                with dve.Fori(1, up.bodies) as i:
                    split(up, i, f, 0, silu, low)
                chunks(dn, 0, 0, 1)
                f(up.bodies - 1, 1)
                chunks(dn, 0, 1, 3)
                low(up.bodies - 1, 1)
                chunks(dn, 0, 3, 4)
                with dve.Fori(1, dn.bodies - 1) as i:
                    chunks(dn, i, 0, 4)

            def down_out(g, q, count):
                dve.wait_ge(chunks_used, g.end - 3 + q)
                r = X[:, 4 * q:4 * q + 4, :]
                V.tensor_tensor(r, r, pair(q), ALU.add).then_inc(x_ready, 1)
                dve.wait_ge(x_ready, count)

            out_ffn(wo1, up1, dn1, 1, "g_ffn", EPS1, 0, 3)
            chunks(dn1, dn1.bodies - 1, 0, 3)
            for q in range(4):
                down_out(dn1, q, 5 + q)
                gained(2, q, U[0], "attn_norm_w_2")
                if q == 0:
                    chunks(dn1, dn1.bodies - 1, 3, 4)
                elif q < 3:
                    low_part(2, q - 1, U[0])
                    chunks(in2, 0, q - 1, q)
            low_part(2, 2, U[0])
            chunks(in2, 0, 2, 3)
            low_part(2, 3, U[0])
            chunks(in2, 0, 3, 4)
            inverse_root(3, 3, EPS1, rstd_final1)
            inverse_root(4, 3, EPS2, rstd, 1, rstd_final1)
            settle(V.tensor_tensor(rstd[:], rstd[:], rstd_final1[:], ALU.mult))
            f = to_proj(in2, proj2)
            split(in2, 0, f, 4)
            with dve.Fori(1, 3) as i:
                split(in2, i, f)

            def after(i, j):
                chunks(in2, i, j, j + 1)
                if j == 0:
                    f(i - 1, 1)
                    dve.wait_ge(strips_out, in2.strip(i, 0))
                elif j == 4:
                    f(i, 0)

            after(3, 0)
            for x in range(3):
                p = proj2[:, 8 * x:8 * x + 8, :]
                V.tensor_tensor(spare[:, :, 1:], p[:, :, 0:T - 1], p[:, :, 1:], ALU.subtract)
                settle(V.tensor_scalar(spare[:, :, 0:1], p[:, :, 0:1], -1.0, None, ALU.mult))
                after(3, 2 * x + 1)
                for n in range(NT):
                    p = proj2[:, 8 * x + n, :]
                    last = V.scalar_tensor_tensor(p, spare[:, n, :], pcol("rwkv_mu_2", 8 * x + n), p, ALU.mult, ALU.add)
                settle(last)
                after(3, 2 * x + 2)
            after(3, 7)
            for i, h, part in ((4, 0, "qk"), (5, 1, "v")):
                after(i, 0)
                for n in range(8 * h, 8 * h + 8):
                    last = V.tensor_scalar(spare[:, n % 8, :], cv[:, n, :], pcol("gdn_conv_w_2", 48 + n), None, ALU.mult)
                settle(last)
                for d in range(1, 4):
                    chunks(in2, i, d, d + 1)
                    for n in range(8 * h, 8 * h + 8):
                        last = V.scalar_tensor_tensor(spare[:, n % 8, d:], cv[:, n, 0:T - d], pcol("gdn_conv_w_2", 16 * (3 - d) + n),
                                                      spare[:, n % 8, d:], ALU.mult, ALU.add)
                    if d < 3:
                        settle(last)
                last.then_inc(step(f"gd_cv_{part}"), 1)
                if i == 4:
                    after(i, 4)
                    chunks(in2, i, 5, 7)
                else:
                    chunks(in2, i, 4, 7)
                dve.wait_ge(*at_step(f"gd_sig_{part}"))
                c = cv[:, 8 * h:8 * h + 8, :]
                V.tensor_tensor(c, c, spare, ALU.mult).then_inc(step(f"gd_silu_{part}"), 1)
                dve.wait_ge(*at_step(f"gd_silu_{part}"))
                if i == 5:
                    f(5, 0)
                chunks(in2, i, 7, 8)
            f(5, 1)
            for k in range(KT):
                last = V.scalar_tensor_tensor(X[:, k, :], X[:, k, :], pcol("g_final", k), rstd_final1[:], ALU.mult, ALU.mult)
            settle(last)
            dve.wait_ge(*at_step("lora_mm"))
            V.tensor_tensor(gb[:], bank(2)[0:H, T:2 * T], rstd[0:H, :], ALU.mult)
            settle(V.tensor_tensor(neg_f[:], bank(2)[0:H, 0:T], rstd[0:H, :], ALU.mult))
            V.tensor_scalar(neg_f[:], neg_f[:], dtb[:], None, ALU.add).then_inc(step("ab_out"), 1)
            V.tensor_tensor(lp[:, 0:2, :], bank(0).rearrange("p (k n) -> p k n", k=2), rstds(P, 2), ALU.mult)
            V.tensor_tensor(lp[0:32, 2, :], bank(1)[0:32, 0:T], rstd[0:32, :], ALU.mult).then_inc(step("lora_out"), 1)
            dve.wait_ge(*at_step("lora_out"))
            V.tensor_tensor(lpd[:, 0:2, 1:], lp[:, 0:2, 0:T - 1], lp[:, 0:2, 1:], ALU.subtract)
            V.tensor_scalar(lpd[:, 0:2, 0:1], lp[:, 0:2, 0:1], -1.0, None, ALU.mult)
            V.tensor_tensor(lpd[0:32, 2, 1:], lp[0:32, 2, 0:T - 1], lp[0:32, 2, 1:], ALU.subtract)
            settle(V.tensor_scalar(lpd[0:32, 2, 0:1], lp[0:32, 2, 0:1], -1.0, None, ALU.mult))
            for k, m in ((0, P), (1, P), (2, 32)):
                last = V.scalar_tensor_tensor(lp[0:m, k, :], lpd[0:m, k, :], pcol("rwkv_mu_2", 24 + k, m), lp[0:m, k, :],
                                              ALU.mult, ALU.add)
            last.then_inc(step("lora_in"), 1)
            dve.wait_ge(strips_out, in2.sbase + in2.ns * in2.bodies)
            for n in range(NT):
                last = V.tensor_scalar(kk[:, n, :], Kw[:, n, :], pcol("rwkv_k_k_2", n), None, ALU.mult)
            last.then_inc(step("kk"), 1)
            dve.wait_ge(*at_step("ld_out"))
            settle(V.tensor_scalar(ld[:], ld[:], -0.6065306597126334, None, ALU.mult))
            dve.wait_ge(*at_step("reset_built"))
            dve.wait_ge(*at_step("za_mm"))
            settle(V.tensor_tensor_scan(flat(cum[:]), flat(reset[:]), flat(ld[:]), 0.0, ALU.mult, ALU.add))
            V.tensor_tensor(ld[:], cum[:], ld[:], ALU.subtract).then_inc(step("l_prev"), 1)
            dve.wait_ge(*at_step("kk_sum"))
            V.tensor_scalar(at_f[:].rearrange("p (b t) n -> p b (t n)", t=2), psum[:, 4:8, :], 1e-12, None, ALU.add).then_inc(step("kk_mean"), 1)
            dve.wait_ge(*at_step("a_out"))
            dve.wait_ge(*at_step("kk_sum"))
            for n in range(NT):
                last = V.tensor_scalar(bonus[:, n, :], a_lr[:, n, :], -1.0, pcol("rwkv_k_a_2", n), ALU.add, ALU.mult)
            settle(last)
            settle(V.scalar_tensor_tensor(Kw, bonus[:], 1.0, Kw, ALU.add, ALU.mult))
            for n in range(NT):
                last = V.scalar_tensor_tensor(bt_f[:, n, :], Rw[:, n, :], pcol("rwkv_r_k_2", n), Kw[:, n, :], ALU.mult, ALU.mult)
            last.then_inc(step("rk"), 1)
            dve.wait_ge(*at_step("kk_root"))
            settle(V.reciprocal(at_f[:], at_f[:]))
            settle(V.tensor_tensor(kk[:], kk[:], at_f[:], ALU.mult))
            V.tensor_tensor(a_lr[:], kk[:], a_lr[:], ALU.mult)
            dve.wait_ge(*at_step("e_prev"))
            V.scalar_tensor_tensor(at_f[:], kk[:], -1.0, ld[:], ALU.mult, ALU.mult).then_inc(step("at_made"), 1)
            dve.wait_ge(*at_step("rk_sum"))
            V.tensor_tensor(bonus[:].rearrange("p (b t) n -> p b (t n)", t=2), psum[:, 0:4, :],
                            Vw.rearrange("p (b t) n -> p b (t n)", t=2), ALU.mult)
            dve.wait_ge(*at_step("e_plus"))
            V.tensor_tensor(Rw, Rw, ld[:], ALU.mult)
            V.tensor_copy(chunk_decay[:], ld[:].rearrange("p k (c t) -> p k c t", t=CH)[:, :, :, CH - 1])
            dve.wait_ge(*at_step("e_minus"))
            V.tensor_tensor(Kw, Kw, cum[:], ALU.mult)
            V.tensor_tensor(bt_f[:], a_lr[:], cum[:], ALU.mult).then_inc(step("rw_fm"), 1)

            def inverse(call, lv, x, xt, z):
                base = sum(4 * n for n in INV_LEVELS[:call])
                for k, n in enumerate(lv):
                    for b in range(4):
                        dve.wait_ge(S("inv_z"), base + 4 * k + b + 1)
                        V.tensor_tensor(z[:, 4 * b:4 * b + 4, :], bank(b).rearrange("p (u n) -> p u n", u=4), bc(low[n], 4),
                                        ALU.mult).then_inc(S("inv_z_out"), 1)
                    for b in range(4):
                        dve.wait_ge(S("inv_x"), base + 4 * k + b + 1)
                        for o in range(2):
                            m = (xt if o else x)[:, 4 * b:4 * b + 4, :]
                            last = V.tensor_tensor(m, m, bank(4 + 2 * (b % 2) + o).rearrange("p (u n) -> p u n", u=4), ALU.add)
                        last.then_inc(S("inv_x_out"), 1)

            for cp in range(2):
                for m, dst in ((2, kt_tok), (3, v_tok2)):
                    dve.wait_ge(S("rw_tok"), 4 * cp + m + 1)
                    V.tensor_copy(dst[:], psum[:, 2 * m:2 * m + 2, :].rearrange("p b n -> p (b n)")).then_inc(S("rw_tok_out"), 1)
                q = 0
                for b in range(4):
                    u = slice(4 * b, 4 * b + 4)

                    def masked(dst, m):
                        dve.wait_ge(S("rw_gram"), 20 * cp + q + 1)
                        return V.tensor_tensor(dst[:, u, :], bank(q % 8).rearrange("p (u n) -> p u n", u=4), bc(m, 4),
                                               ALU.mult).then_inc(S("rw_gram_out"), 1)
                    masked(x_r, low[0])
                    q += 1
                    masked(nt_r, upper_strict)
                    q += 1
                    dve.wait_ge(S("rw_gram_out"), 20 * cp + q)
                    settle(V.tensor_tensor(xt_r[:, u, :], nt_r[:, u, :], bc(low0_t, 4), ALU.mult))
                    V.tensor_tensor(x_r[:, u, :], x_r[:, u, :], bc(ident, 4), ALU.add)
                    V.tensor_tensor(xt_r[:, u, :], xt_r[:, u, :], bc(ident, 4), ALU.add).then_inc(S("inv_x_out"), 1)
                    for dst, m in ((akt, upper_strict), (rbt, upper_incl), (rkt, upper_incl)):
                        masked(dst, m)
                        q += 1
                inverse(cp, range(1, 6), x_r, xt_r, z_r)
                for c in range(2):
                    g, tp = 2 * cp + c, slice(64 * c, 64 * c + 64)
                    dve.wait_ge(S("rw_u_mm"), g + 1)
                    dve.wait_ge(S("rw_uv_out"), cp + 1)
                    V.tensor_tensor(u_tok[tp, :], psum[tp, 6:8, :].rearrange("p b n -> p (b n)"), uv[tp, :], ALU.add).then_inc(S("rw_u"), 1)
                    dve.wait_ge(S("rw_s_mm"), g + 1)
                    settle(V.tensor_tensor(state[:].rearrange("p k n -> p (k n)"), bank(2 + c), state[:].rearrange("p k n -> p (k n)"), ALU.add))
                    V.tensor_tensor(state[:], state[:], chunk_decay[:, :, g:g + 1].to_broadcast([P, NT, 64]), ALU.mult).then_inc(S("rw_state"), 1)
            v4 = lambda t: t.rearrange("p (b t) n -> p b (t n)", t=2)
            dve.wait_ge(*at_step("gn_mean"))
            V.scalar_tensor_tensor(v4(y_rw[:]), psum[:, 0:4, :], -1.0 / 64, v4(y_rw[:]), ALU.mult, ALU.add).then_inc(step("gn_c"), 1)
            dve.wait_ge(*at_step("gn_var"))
            V.tensor_scalar(v4(gn_r[:]), psum[:, 4:8, :], 1.0 / 64, 64e-5, ALU.mult, ALU.add).then_inc(step("gn_m"), 1)
            dve.wait_ge(*at_step("gn_root"))
            settle(V.reciprocal(gn_r[:], gn_r[:]))
            settle(V.tensor_tensor(y_rw[:], y_rw[:], gn_r[:], ALU.mult))
            for n in range(NT):
                last = V.tensor_scalar(y_rw[:, n, :], y_rw[:, n, :], pcol("rwkv_ln_w_2", n), pcol("rwkv_ln_b_2", n), ALU.mult, ALU.add)
            settle(last)
            settle(V.tensor_tensor(y_rw[:], y_rw[:], bonus[:], ALU.add))
            V.tensor_tensor(yfin[:, 0:8, :], y_rw[:], gate2[:], ALU.mult).then_inc(step("gn_out"), 1)
            dve.wait_ge(*at_step("gn_out"))
            settle(V.tensor_copy(gn[0][:], neg_f[:]))
            softplus(2, gn[0][:], gn[1][:], gn[2][:], gn[3][:], gn[4][:])
            dve.wait_ge(*at_step("gd_expA"))
            settle(V.tensor_scalar(gn[5][:], gn[4][:], alog[:], -1.0, ALU.mult, ALU.mult))
            for c in range(2):
                tk = slice(c * P, (c + 1) * P)
                last = V.tensor_tensor_scan(gn[4][:, tk], ones8[:, tk], gn[5][:, tk], 0.0, ALU.mult, ALU.add)
            settle(last)
            V.tensor_scalar(gn[7][:, 0:P], ones8[:, 0:P], gn[4][:, P - 1:P], None, ALU.mult)
            dve.wait_ge(*at_step("gd_beta"))
            V.tensor_scalar(gn[5][:], gn[4][:], -1.0, None, ALU.mult).then_inc(step("gd_cum"), 1)
            dve.wait_ge(*at_step("gd_cum"))
            for h in range(H):
                V.tensor_scalar(gm[:, h, :], gn[4][:], ident[0:H, h:h + 1], None, ALU.mult)
                last = V.tensor_scalar(ngm[:, h, :], gn[5][:], ident[0:H, h:h + 1], None, ALU.mult)
            last.then_inc(step("gd_rows"), 1)
            dve.wait_ge(*at_step("gd_tok"))
            V.tensor_copy(tokp[:, 0:4, :], bank(0)[:, 0:4 * H].rearrange("p (k h) -> p k h", h=H))
            V.tensor_copy(tokp[:, 6, :], bank(0)[:, 4 * H:5 * H]).then_inc(step("gd_tok_out"), 1)
            dve.wait_ge(*at_step("gd_l2"))
            V.tensor_scalar(v4(l2s[:]), psum[:, 4:8, :], 1e-6, None, ALU.add).then_inc(step("gd_l2_mean"), 1)
            dve.wait_ge(*at_step("gd_l2_root"))
            settle(V.reciprocal(l2s[:], l2s[:]))
            V.scalar_tensor_tensor(cv[:, 0:4, :], cv[:, 0:4, :], float(P) ** -0.5, l2s[:, 0:4, :], ALU.mult, ALU.mult)
            V.tensor_tensor(cv[:, 4:8, :], cv[:, 4:8, :], l2s[:, 4:8, :], ALU.mult).then_inc(step("gd_qk"), 1)
            dve.wait_ge(*at_step("gd_tok_exp"))
            V.tensor_tensor(tokp[:, 4:6, :], tokp[:, 4:6, :], tokp[:, 2:4, :], ALU.mult)
            settle(V.tensor_scalar(tokp[:, 0:2, :], tokp[:, 2:4, :], -1.0, None, ALU.mult))
            dve.wait_ge(*at_step("gd_gram"))
            for c in range(2):
                for b in range(2):
                    dve.wait_ge(S("gd_gam"), 2 * c + b + 1)
                    for h in range(4 * b, 4 * b + 4):
                        last = V.scalar_tensor_tensor(x_g[:, 8 * c + h, :], bank(c)[:, (h // 2) * P:(h // 2 + 1) * P],
                                                      tokp[:, c, h:h + 1], gam[:, 8 * c + h, :], ALU.mult, ALU.mult)
            last.then_inc(step("gd_n"), 1)
            for c in range(2):
                for b in range(2):
                    dve.wait_ge(S("gd_gam"), 4 + 2 * c + b + 1)
                    for h in range(4 * b, 4 * b + 4):
                        V.tensor_tensor(aqk[:, 8 * c + h, :], bank(2 + c)[:, (h // 2) * P:(h // 2 + 1) * P],
                                        gam_t[:, 8 * c + h, :], ALU.mult)
            for b in range(4):
                u = slice(4 * b, 4 * b + 4)
                dve.wait_ge(S("gd_nt_out"), b + 1)
                V.tensor_tensor(x_g[:, u, :], x_g[:, u, :], bc(low[0], 4), ALU.mult)
                settle(V.tensor_tensor(xt_g[:, u, :], nt_g[:, u, :], bc(low0_t, 4), ALU.mult))
                V.tensor_tensor(x_g[:, u, :], x_g[:, u, :], bc(ident, 4), ALU.add)
                V.tensor_tensor(xt_g[:, u, :], xt_g[:, u, :], bc(ident, 4), ALU.add).then_inc(S("inv_x_out"), 1)
            inverse(2, range(1, 7), x_g, xt_g, z_g)
            for c in range(2):
                dve.wait_ge(S("gd_k_t"), c + 1)
                for h in range(H):
                    src = bank(4 + c)[:, (h // 2) * P:(h // 2 + 1) * P]
                    if c:
                        last = V.tensor_scalar(k_bg[:, 8 + h, :], src, tokp[:, 4 + c, h:h + 1], None, ALU.mult)
                    else:
                        V.tensor_scalar(k_g[:, h, :], src, tokp[:, 6, h:h + 1], None, ALU.mult)
            last.then_inc(step("gd_k_bg"), 1)
            dve.wait_ge(*at_step("gd_eg"))
            for h in range(H):
                last = V.tensor_tensor(q_g[:, h, :], cv[:, h // 2, P:T], bank(h // 4)[:, (h % 4) * P:(h % 4 + 1) * P], ALU.mult)
            last.then_inc(step("gd_qg"), 1)
            dve.wait_ge(*at_step("gd_ws"))
            V.tensor_tensor(v_new[:].rearrange("p k n -> p (k n)"), u_g[:, 8:16, :].rearrange("p k n -> p (k n)"),
                            psum[:, 4:6, :].rearrange("p b n -> p (b n)"), ALU.subtract).then_inc(step("gd_vn"), 1)
            dve.wait_ge(y2_hi, 1)
            V.tensor_tensor(Ml[1][:, 0:8, :], yfin[:, 0:8, :], Mh[:, 0:8, :].bitcast(F32), ALU.subtract).then_inc(y2_parts, 2)
            dve.wait_ge(*at_step("gd_z_sig"))
            zz = proj2[:, 40:48, :]
            settle(V.tensor_tensor(z_sig[:], z_sig[:], zz, ALU.mult))
            dve.wait_ge(*at_step("gd_o_sum"))
            V.tensor_scalar(v4(o_r[:]), psum[:, 4:8, :], 1.0 / P, 1e-6, ALU.mult, ALU.add).then_inc(step("gd_o_mean"), 1)
            chunks(wo2, 0, 0, 2)
            dve.wait_ge(*at_step("gd_o_root"))
            settle(V.reciprocal(o_r[:], o_r[:]))
            for q in range(2):
                k = slice(4 * q, 4 * q + 4)
                settle(V.scalar_tensor_tensor(o_g[:, k, :], o_g[:, k, :], pcol("gdn_norm_w_2"), o_r[:, k, :], ALU.mult, ALU.mult))
                V.tensor_tensor(yfin[:, 8 + 4 * q:12 + 4 * q, :], o_g[:, k, :], z_sig[:, k, :], ALU.mult).then_inc(y2_made, 1)
            for q in range(2):
                dve.wait_ge(y2_hi, 2 + q)
                k = slice(8 + 4 * q, 12 + 4 * q)
                V.tensor_tensor(Ml[1][:, k, :], yfin[:, k, :], Mh[:, k, :].bitcast(F32), ALU.subtract).then_inc(y2_parts, 1)
            out_ffn(wo2, up2, dn2, 3, "ffn_norm_w_2", EPS2, 1, 2)
            chunks(dn2, dn2.bodies - 1, 0, 4)
            for q in range(4):
                down_out(dn2, q, 9 + q)
            inverse_root(6, 5, EPS2)
            for k in range(KT):
                last = V.scalar_tensor_tensor(U[0][:, k, :], X[:, k, :], pcol("final_norm_w_2", k), rstd[:], ALU.mult, ALU.mult)
            last.then_inc(h_ready, 1)
            for n in range(1, 8, 2):
                dve.wait_ge(out_turned, n + 1)
                V.tensor_copy(out_tokens[:, n % 2, n // 2 * 512:(n // 2 + 1) * 512], bank(n)).then_inc(out_copied, 1)


INPUTS = ["x", "g_mix", "w_in", "b_forget", "conv_w", "conv_b", "w_rg", "b_rg", "w_ig", "b_ig", "lru_lambda", "w_pool",
          "pool_scale", "w_branch_rnn", "w_branch_attn", "w_branch_pool", "w_out", "g_ffn", "w_ffn_in", "w_ffn_out",
          "g_final", "attn_norm_w_2", "w_in_2", "rwkv_mu_2", "rwkv_w0_2", "rwkv_w_up_2", "rwkv_a0_2", "rwkv_a_up_2",
          "rwkv_g_up_2", "rwkv_k_k_2", "rwkv_k_a_2", "rwkv_r_k_2", "rwkv_ln_w_2", "rwkv_ln_b_2", "gdn_conv_w_2",
          "gdn_A_log_2", "gdn_dt_bias_2", "gdn_norm_w_2", "w_out_2", "ffn_norm_w_2", "ffn_w_gate_2", "ffn_w_up_2",
          "ffn_w_down_2", "final_norm_w_2"]


def kernel(**inputs):
    import numpy as np
    import concourse.bacc as bacc
    from concourse.bass_utils import run_bass_kernel_spmd

    nc = bacc.Bacc("TRN2", target_bir_lowering=False, num_devices=1)
    arrays, args = {}, {}
    for name in INPUTS:
        arrays[f"in_{name}"] = np.ascontiguousarray(inputs[name])
        args[name] = nc.dram_tensor(f"in_{name}", arrays[f"in_{name}"].shape, F32, kind="ExternalInput").ap()
    out = nc.dram_tensor("out_dram", (1, T, D), F32, kind="ExternalOutput").ap()
    build(nc, args, out)
    r = run_bass_kernel_spmd(nc, [arrays], core_ids=[0])
    return r.results[0]["out_dram"]
```
